# Optimizing a Trainium2 kernel written in Bass

```python
import math
import functools
import numpy as np
import jax
import jax.numpy as jnp
from jax import lax

D_MODEL = 1024
BATCH = 1
SEQ = 512
DEPTH = 1
DEC_BATCH = 8
DEC_SEQ = 1
PAST_LEN = 2048
PAGE_SIZE = 128

M_HEADS = 4
M_HEAD_DIM = 128
M_WIDTH = M_HEADS * M_HEAD_DIM
M_CONV = 4
M_CHUNK = 64
A_HEADS = 8
A_KV_HEADS = 2
A_HEAD_DIM = 64
A_WIDTH = A_HEADS * A_HEAD_DIM
A_GROUP = A_HEADS // A_KV_HEADS
A_SCALE = A_HEAD_DIM ** -0.5
CMP_STRIDE = 16
CMP_BLOCK = 2 * CMP_STRIDE
CMP_HIDDEN = A_HEAD_DIM
SEL_BLOCK = 64
N_SEL = 16
WINDOW = 512
Q_BLOCK = 128
R_HEADS = 8
R_HEAD_DIM = 64
R_WIDTH = R_HEADS * R_HEAD_DIM
R_DECAY_RANK = 64
R_A_RANK = 64
R_GATE_RANK = 128
R_COLS = 3 * R_WIDTH + R_DECAY_RANK + R_A_RANK + R_GATE_RANK
LN_X_EPS = 64e-5
D_FF = ((-(-8 * D_MODEL // 3)) + 255) // 256 * 256
IN_SPLITS = (2 * M_WIDTH, M_WIDTH, M_WIDTH, 2 * M_HEADS,
             A_WIDTH, 6 * A_KV_HEADS * A_HEAD_DIM, 3 * A_HEADS,
             R_COLS, 3 * D_MODEL)
IN_COLS = sum(IN_SPLITS)
RMS_EPS = 1e-6
NEG = -1e30
FORCE = 1e9

kernel_name = 'hybrid_mlstm_nsa_rwkv7_step'

def split_last(z, sizes):
    return jnp.split(z, np.cumsum(sizes)[:-1].tolist(), axis=-1)

def rmsnorm(x, g):
    xf = x.astype(jnp.float32)
    y = xf * lax.rsqrt(jnp.mean(xf * xf, axis=-1, keepdims=True) + RMS_EPS)
    return (y * g.astype(jnp.float32)).astype(x.dtype)

def mlstm_chunk(carry, xs):
    C, n, m = carry
    q, k, v, li, lf = xs
    L = q.shape[1]
    b = jnp.cumsum(lf, axis=1)
    dmat = b[:, :, None, :] - b[:, None, :, :] + li[:, None, :, :]
    causal = jnp.tril(jnp.ones((L, L), bool))
    dmat = jnp.where(causal[None, :, :, None], dmat, -jnp.inf)
    inter = b + m[:, None, :]
    m_t = jnp.maximum(inter, jnp.max(dmat, axis=2))
    w_intra = jnp.exp(dmat - m_t[:, :, None, :])
    w_inter = jnp.exp(inter - m_t)
    att = w_intra * jnp.einsum('bthd,bshd->btsh', q, k)
    num = (jnp.einsum('btsh,bshv->bthv', att, v)
           + w_inter[..., None] * jnp.einsum('bthd,bhdv->bthv', q, C))
    den = jnp.sum(att, axis=2) + w_inter * jnp.einsum('bthd,bhd->bth', q, n)
    h = num / jnp.maximum(jnp.abs(den), jnp.exp(-m_t))[..., None]
    m_new = m_t[:, -1]
    carry_scale = jnp.exp(b[:, -1] + m - m_new)
    w_end = jnp.exp(b[:, -1:, :] - b + li - m_new[:, None, :])
    C_new = carry_scale[..., None, None] * C + jnp.einsum('bsh,bshd,bshv->bhdv', w_end, k, v)
    n_new = carry_scale[..., None] * n + jnp.einsum('bsh,bshd->bhd', w_end, k)
    return (C_new, n_new, m_new), h

def mlstm_mix(m_qk, m_v, m_o, m_if, m_state, conv_w, conv_b, if_bias):
    conv_buf, C, n, m = m_state
    B, T, _ = m_qk.shape
    f32 = jnp.float32
    full = jnp.concatenate([conv_buf.astype(m_qk.dtype), m_qk], axis=1)
    qk = jax.nn.silu(conv_b + sum(full[:, j:j + T] * conv_w[j] for j in range(M_CONV)))
    q, k = jnp.split(qk.astype(f32), 2, axis=-1)
    q = q.reshape(B, T, M_HEADS, M_HEAD_DIM)
    k = k.reshape(B, T, M_HEADS, M_HEAD_DIM) * (M_HEAD_DIM ** -0.5)
    v = m_v.astype(f32).reshape(B, T, M_HEADS, M_HEAD_DIM)
    gates = m_if.astype(f32).reshape(B, T, 2, M_HEADS) + if_bias.astype(f32)
    li = gates[:, :, 0]
    lf = jax.nn.log_sigmoid(gates[:, :, 1])
    L = math.gcd(T, M_CHUNK)
    nc = T // L

    def chunks(a):
        return jnp.moveaxis(a.reshape(B, nc, L, *a.shape[2:]), 1, 0)

    carry0 = (C.astype(f32), n.astype(f32), m.astype(f32))
    (C, n, m), h = lax.scan(mlstm_chunk, carry0,
                            (chunks(q), chunks(k), chunks(v), chunks(li), chunks(lf)))
    h = jnp.moveaxis(h, 0, 1).reshape(B, T, M_WIDTH)
    y = jax.nn.sigmoid(m_o.astype(f32)) * h
    return y.astype(m_qk.dtype), (full[:, -(M_CONV - 1):], C, n, m)

def compress(rows, pe, w1, w2):
    B, T, G, d = rows.shape
    nchunk = T // CMP_STRIDE
    c = rows[:, :nchunk * CMP_STRIDE].reshape(B, nchunk, CMP_STRIDE, G, d)
    w1 = w1.reshape(2, CMP_STRIDE, d, CMP_HIDDEN)
    halves = jnp.einsum('bnlgd,jldh->jbngh', c, w1)
    pe_term = jnp.einsum('jld,jldh->h', pe.reshape(2, CMP_STRIDE, d), w1)
    hid = jax.nn.silu(halves[0, :, :-1] + halves[1, :, 1:] + pe_term)
    return jnp.einsum('bngh,hd->bngd', hid, w2)

def cmp_attend(q, kc, vc, q_pos):
    B, Q = q.shape[:2]
    N = kc.shape[1]
    qg = q.reshape(B, Q, A_KV_HEADS, A_GROUP, A_HEAD_DIM)
    s = jnp.einsum('bqgjd,bngd->bgjqn', qg, kc).astype(jnp.float32) * A_SCALE
    blk_end = jnp.arange(N) * CMP_STRIDE + CMP_BLOCK - 1
    mask = blk_end[None, :] <= q_pos[:, None]
    p = jax.nn.softmax(jnp.where(mask, s, NEG), axis=-1)
    p = jnp.where(mask, p, 0.0)
    o = jnp.einsum('bgjqn,bngd->bqgjd', p.astype(vc.dtype), vc)
    return o.reshape(B, Q, A_HEADS, A_HEAD_DIM), jnp.sum(p, axis=2)

def select_blocks(p_grp, q_pos, n_total):
    N = p_grp.shape[-1]
    n_blocks = -(-n_total // SEL_BLOCK)
    i = np.arange(N)[:, None]
    j = np.arange(n_blocks)[None, :]
    covers = (i * CMP_STRIDE < (j + 1) * SEL_BLOCK) & (i * CMP_STRIDE + CMP_BLOCK > j * SEL_BLOCK)
    score = jnp.einsum('bgqn,nj->bgqj', p_grp, jnp.asarray(covers, jnp.float32))
    cur = q_pos[:, None] // SEL_BLOCK
    jj = jnp.arange(n_blocks)[None, :]
    forced = (jj == 0) | (jj == cur) | (jj == cur - 1)
    rank = jnp.where(jj <= cur, jnp.where(forced, FORCE, score), NEG)
    _, idx = lax.top_k(rank, min(N_SEL, n_blocks))
    return idx

def block_tokens(idx):
    tok = idx[..., None] * SEL_BLOCK + jnp.arange(SEL_BLOCK, dtype=idx.dtype)
    return tok.reshape(*idx.shape[:-1], idx.shape[-1] * SEL_BLOCK)

def gathered_attend(q, kg, vg, tok, q_pos):
    B, Q = q.shape[:2]
    qg = q.reshape(B, Q, A_KV_HEADS, A_GROUP, A_HEAD_DIM)
    s = jnp.einsum('bqgjd,bgqsd->bgjqs', qg, kg).astype(jnp.float32) * A_SCALE
    mask = (tok <= q_pos[None, None, :, None])[:, :, None]
    p = jax.nn.softmax(jnp.where(mask, s, NEG), axis=-1)
    o = jnp.einsum('bgjqs,bgqsd->bqgjd', p.astype(vg.dtype), vg)
    return o.reshape(B, Q, A_HEADS, A_HEAD_DIM)

def band_attend(q, k, v, q_pos, k_pos):
    B, Q = q.shape[:2]
    qg = q.reshape(B, Q, A_KV_HEADS, A_GROUP, A_HEAD_DIM)
    s = jnp.einsum('bqgjd,bkgd->bgjqk', qg, k).astype(jnp.float32) * A_SCALE
    rel = q_pos[:, None] - k_pos[None, :]
    mask = (rel >= 0) & (rel < WINDOW) & (k_pos[None, :] >= 0)
    p = jax.nn.softmax(jnp.where(mask, s, NEG), axis=-1)
    o = jnp.einsum('bgjqk,bkgd->bqgjd', p.astype(v.dtype), v)
    return o.reshape(B, Q, A_HEADS, A_HEAD_DIM)

def combine_branches(a_gate, o_cmp, o_sel, o_win):
    B, T = a_gate.shape[:2]
    g = jax.nn.sigmoid(a_gate.astype(jnp.float32)).reshape(B, T, 3, A_HEADS, 1)
    o = g[:, :, 0] * o_cmp + g[:, :, 1] * o_sel + g[:, :, 2] * o_win
    return o.reshape(B, T, A_WIDTH).astype(a_gate.dtype)

def split_nsa(a_q, a_kv):
    B, T, _ = a_q.shape
    q = a_q.reshape(B, T, A_HEADS, A_HEAD_DIM)
    rows = [r.reshape(B, T, A_KV_HEADS, A_HEAD_DIM) for r in jnp.split(a_kv, 6, axis=-1)]
    return q, rows

def nsa_prompt(a_q, a_kv, a_gate, cmp_pe, cmp_w1, cmp_w2):
    B, T, _ = a_q.shape
    q, (kcr, vcr, ksr, vsr, kwr, vwr) = split_nsa(a_q, a_kv)
    q_pos = jnp.arange(T)
    kc = compress(kcr, cmp_pe[0], cmp_w1[0], cmp_w2[0])
    vc = compress(vcr, cmp_pe[1], cmp_w1[1], cmp_w2[1])
    o_cmp, p_grp = cmp_attend(q, kc, vc, q_pos)
    idx = select_blocks(p_grp, q_pos, T)
    nqb = T // Q_BLOCK
    qb = jnp.moveaxis(q.reshape(B, nqb, Q_BLOCK, A_HEADS, A_HEAD_DIM), 1, 0)
    idxb = jnp.moveaxis(idx.reshape(B, A_KV_HEADS, nqb, Q_BLOCK, idx.shape[-1]), 2, 0)
    starts = jnp.arange(nqb) * Q_BLOCK
    ks_t = jnp.swapaxes(ksr, 1, 2)
    vs_t = jnp.swapaxes(vsr, 1, 2)
    bi = jnp.arange(B)[:, None, None]
    gi = jnp.arange(A_KV_HEADS)[None, :, None]

    def sel_block(args):
        qq, ii, st = args
        tok = block_tokens(ii)
        flat = tok.reshape(B, A_KV_HEADS, -1)
        kg = ks_t[bi, gi, flat].reshape(*tok.shape, A_HEAD_DIM)
        vg = vs_t[bi, gi, flat].reshape(*tok.shape, A_HEAD_DIM)
        return gathered_attend(qq, kg, vg, tok, st + jnp.arange(Q_BLOCK))

    o_sel = lax.map(sel_block, (qb, idxb, starts))
    o_sel = jnp.moveaxis(o_sel, 0, 1).reshape(B, T, A_HEADS, A_HEAD_DIM)
    pad = ((0, 0), (WINDOW, 0), (0, 0), (0, 0))
    kw_pad = jnp.pad(kwr, pad)
    vw_pad = jnp.pad(vwr, pad)

    def win_block(args):
        qq, st = args
        kb = lax.dynamic_slice_in_dim(kw_pad, st, WINDOW + Q_BLOCK, axis=1)
        vb = lax.dynamic_slice_in_dim(vw_pad, st, WINDOW + Q_BLOCK, axis=1)
        return band_attend(qq, kb, vb, st + jnp.arange(Q_BLOCK),
                           st - WINDOW + jnp.arange(WINDOW + Q_BLOCK))

    o_win = lax.map(win_block, (qb, starts))
    o_win = jnp.moveaxis(o_win, 0, 1).reshape(B, T, A_HEADS, A_HEAD_DIM)
    out = combine_branches(a_gate, o_cmp, o_sel, o_win)
    keep = min(WINDOW, T)
    return out, (kcr, vcr, ksr, vsr, kwr[:, T - keep:], vwr[:, T - keep:])

def gather_paged(pool, new_rows, page_table, tok):
    B, G = tok.shape[:2]
    n_pages = page_table.shape[1]
    past_len = n_pages * PAGE_SIZE
    b = jnp.arange(B)[:, None, None, None]
    g = jnp.arange(G)[None, :, None, None]
    phys = page_table[b, jnp.minimum(tok // PAGE_SIZE, n_pages - 1)]
    from_pool = pool[phys, tok % PAGE_SIZE, g].astype(new_rows.dtype)
    from_new = new_rows[b, jnp.clip(tok - past_len, 0, new_rows.shape[1] - 1), g]
    return jnp.where((tok < past_len)[..., None], from_pool, from_new)

def nsa_sample(a_q, a_kv, a_gate, pool_kc, pool_vc, pool_ks, pool_vs, win_k, win_v,
               page_table, cmp_pe, cmp_w1, cmp_w2):
    B, Q, _ = a_q.shape
    q, (kcr, vcr, ksr, vsr, kwr, vwr) = split_nsa(a_q, a_kv)
    q_pos = PAST_LEN + jnp.arange(Q)

    def full_rows(pool, new):
        past = pool[page_table].reshape(B, -1, A_KV_HEADS, A_HEAD_DIM)
        return jnp.concatenate([past.astype(new.dtype), new], axis=1)

    kc = compress(full_rows(pool_kc, kcr), cmp_pe[0], cmp_w1[0], cmp_w2[0])
    vc = compress(full_rows(pool_vc, vcr), cmp_pe[1], cmp_w1[1], cmp_w2[1])
    o_cmp, p_grp = cmp_attend(q, kc, vc, q_pos)
    tok = block_tokens(select_blocks(p_grp, q_pos, PAST_LEN + Q))
    kg = gather_paged(pool_ks, ksr, page_table, tok)
    vg = gather_paged(pool_vs, vsr, page_table, tok)
    o_sel = gathered_attend(q, kg, vg, tok, q_pos)
    keep = win_k.shape[1]
    kw = jnp.concatenate([win_k.astype(kwr.dtype), kwr], axis=1)
    vw = jnp.concatenate([win_v.astype(vwr.dtype), vwr], axis=1)
    o_win = band_attend(q, kw, vw, q_pos, PAST_LEN - keep + jnp.arange(keep + Q))
    out = combine_branches(a_gate, o_cmp, o_sel, o_win)
    return out, (kcr, vcr, ksr, vsr, kw[:, -keep:], vw[:, -keep:])

def rwkv_step(S, xs):
    r, w, k, v, a, b = xs
    sa = jnp.einsum('bhij,bhj->bhi', S, a)
    S = S * w[:, :, None, :] + sa[..., None] * b[:, :, None, :] + v[..., None] * k[:, :, None, :]
    return S, jnp.einsum('bhij,bhj->bhi', S, r)

def rwkv_mix(cols, r_state, lp):
    shift_buf, S = r_state
    B, T, _ = cols.shape
    f32 = jnp.float32
    prev = jnp.concatenate([shift_buf.astype(cols.dtype), cols[:, :-1]], axis=1)
    mixed = (cols + (prev - cols) * lp['rwkv_mu']).astype(f32)
    r, k, v, wd, ad, gd = split_last(mixed, (R_WIDTH, R_WIDTH, R_WIDTH, R_DECAY_RANK, R_A_RANK, R_GATE_RANK))
    w = -jax.nn.softplus(-(lp['rwkv_w0'] + jnp.tanh(wd) @ lp['rwkv_w2'])) - 0.5
    decay = jnp.exp(-jnp.exp(w))
    a = jax.nn.sigmoid(lp['rwkv_a0'] + ad @ lp['rwkv_a2'])
    g = jax.nn.sigmoid(gd) @ lp['rwkv_g2']

    def heads(z):
        return z.reshape(B, T, R_HEADS, R_HEAD_DIM)

    def time_major(z):
        return jnp.moveaxis(z, 1, 0)

    kk = heads(k * lp['rwkv_k_k'])
    kk = kk * lax.rsqrt(jnp.maximum(jnp.sum(kk * kk, axis=-1, keepdims=True), 1e-24))
    k = k * (1.0 + (a - 1.0) * lp['rwkv_k_a'])
    r_h, k_h, v_h, a_h = heads(r), heads(k), heads(v), heads(a)
    S, y = lax.scan(rwkv_step, S.astype(f32),
                    (time_major(r_h), time_major(heads(decay)), time_major(k_h), time_major(v_h),
                     time_major(-kk), time_major(kk * a_h)))
    y = jnp.moveaxis(y, 0, 1)
    mean = jnp.mean(y, axis=-1, keepdims=True)
    var = jnp.mean(jnp.square(y - mean), axis=-1, keepdims=True)
    y = ((y - mean) * lax.rsqrt(var + LN_X_EPS)).reshape(B, T, R_WIDTH) * lp['rwkv_ln_g'] + lp['rwkv_ln_b']
    bonus = jnp.sum(r_h * k_h * lp['rwkv_r_k'], axis=-1, keepdims=True) * v_h
    y = (y + bonus.reshape(B, T, R_WIDTH)) * g
    return y.astype(cols.dtype), (cols[:, -1:], S)

def trunk_layer(x, lp, nsa_fn, m_state, r_state):
    B, T, _ = x.shape
    h = rmsnorm(x, lp['norm1_g'])
    m_qk, m_v, m_o, m_if, a_q, a_kv, a_gate, r_cols, merge = split_last(h @ lp['w_in'], IN_SPLITS)
    y_m, m_new = mlstm_mix(m_qk, m_v, m_o, m_if, m_state, lp['mlstm_conv_w'], lp['mlstm_conv_b'], lp['mlstm_if_bias'])
    y_a, nsa_new = nsa_fn(a_q, a_kv, a_gate)
    y_r, r_new = rwkv_mix(r_cols, r_state, lp)
    gates = jax.nn.sigmoid(merge.astype(jnp.float32)).reshape(B, T, 3, D_MODEL)
    merged = (gates[:, :, 0] * (y_m @ lp['w_branch_m'])
              + gates[:, :, 1] * (y_a @ lp['w_branch_a'])
              + gates[:, :, 2] * (y_r @ lp['w_branch_r']))
    x = x + merged.astype(x.dtype) @ lp['w_out']
    h2 = rmsnorm(x, lp['norm2_g'])
    gte, up = jnp.split(h2 @ lp['w_gate_up'], 2, axis=-1)
    x = x + (jax.nn.silu(gte) * up) @ lp['w_down']
    return x, nsa_new, m_new, r_new

def setup_inputs(seed: int = 0) -> dict:
    key = jax.random.key(seed)
    keys = iter(jax.random.split(key, 64))
    f32 = jnp.float32
    n_pages = PAST_LEN // PAGE_SIZE
    n_used = DEC_BATCH * n_pages
    n_pool = n_used + max(1, n_used // 4)
    win_keep = min(WINDOW, PAST_LEN)
    L = DEPTH

    def normal(shape, scale=1.0):
        return scale * jax.random.normal(next(keys), shape, f32)

    def uniform(shape, lo, hi):
        return jax.random.uniform(next(keys), shape, f32, lo, hi)

    pool = (L, n_pool, PAGE_SIZE, A_KV_HEADS, A_HEAD_DIM)
    win = (L, DEC_BATCH, win_keep, A_KV_HEADS, A_HEAD_DIM)
    page_table = jax.random.permutation(next(keys), n_pool)[:n_used].reshape(DEC_BATCH, n_pages).astype(jnp.int32)
    return {
        'x_prompt': normal((BATCH, SEQ, D_MODEL)),
        'x_sample': normal((DEC_BATCH, DEC_SEQ, D_MODEL)),
        'cache_cmp_k': normal(pool),
        'cache_cmp_v': normal(pool),
        'cache_slc_k': normal(pool),
        'cache_slc_v': normal(pool),
        'cache_win_k': normal(win),
        'cache_win_v': normal(win),
        'state_mlstm_conv': normal((L, DEC_BATCH, M_CONV - 1, 2 * M_WIDTH)),
        'state_mlstm_C': normal((L, DEC_BATCH, M_HEADS, M_HEAD_DIM, M_HEAD_DIM), 0.1),
        'state_mlstm_n': normal((L, DEC_BATCH, M_HEADS, M_HEAD_DIM), 0.1),
        'state_mlstm_m': normal((L, DEC_BATCH, M_HEADS)),
        'state_rwkv_shift': normal((L, DEC_BATCH, 1, R_COLS)),
        'state_rwkv': normal((L, DEC_BATCH, R_HEADS, R_HEAD_DIM, R_HEAD_DIM), 0.1),
        'page_table': page_table,
        'norm1_g': 1.0 + normal((L, D_MODEL), 0.02),
        'w_in': normal((L, D_MODEL, IN_COLS), D_MODEL ** -0.5),
        'mlstm_if_bias': jnp.stack([normal((L, M_HEADS), 0.1), uniform((L, M_HEADS), 3.0, 6.0)], axis=1),
        'mlstm_conv_w': normal((L, M_CONV, 2 * M_WIDTH), 0.5),
        'mlstm_conv_b': normal((L, 2 * M_WIDTH), 0.02),
        'nsa_cmp_pe': normal((L, 2, CMP_BLOCK, A_HEAD_DIM), 0.1),
        'nsa_cmp_w1': normal((L, 2, CMP_BLOCK * A_HEAD_DIM, CMP_HIDDEN), (CMP_BLOCK * A_HEAD_DIM) ** -0.5),
        'nsa_cmp_w2': normal((L, 2, CMP_HIDDEN, A_HEAD_DIM), CMP_HIDDEN ** -0.5),
        'rwkv_mu': uniform((L, R_COLS), 0.0, 1.0),
        'rwkv_w0': uniform((L, R_WIDTH), -6.0, -1.0),
        'rwkv_w2': normal((L, R_DECAY_RANK, R_WIDTH), 0.1),
        'rwkv_a0': normal((L, R_WIDTH), 0.1),
        'rwkv_a2': normal((L, R_A_RANK, R_WIDTH), R_A_RANK ** -0.5),
        'rwkv_g2': normal((L, R_GATE_RANK, R_WIDTH), R_GATE_RANK ** -0.5),
        'rwkv_k_k': 0.85 + normal((L, R_WIDTH), 0.02),
        'rwkv_k_a': 1.0 + normal((L, R_WIDTH), 0.02),
        'rwkv_r_k': normal((L, R_HEADS, R_HEAD_DIM), 0.1),
        'rwkv_ln_g': 1.0 + normal((L, R_WIDTH), 0.02),
        'rwkv_ln_b': normal((L, R_WIDTH), 0.02),
        'w_branch_m': normal((L, M_WIDTH, D_MODEL), M_WIDTH ** -0.5),
        'w_branch_a': normal((L, A_WIDTH, D_MODEL), A_WIDTH ** -0.5),
        'w_branch_r': normal((L, R_WIDTH, D_MODEL), R_WIDTH ** -0.5),
        'w_out': normal((L, D_MODEL, D_MODEL), D_MODEL ** -0.5),
        'norm2_g': 1.0 + normal((L, D_MODEL), 0.02),
        'w_gate_up': normal((L, D_MODEL, 2 * D_FF), D_MODEL ** -0.5),
        'w_down': normal((L, D_FF, D_MODEL), D_FF ** -0.5),
        'final_norm_g': 1.0 + normal((D_MODEL,), 0.02),
    }

def reference(x_prompt, x_sample, cache_cmp_k, cache_cmp_v, cache_slc_k, cache_slc_v,
              cache_win_k, cache_win_v, state_mlstm_conv, state_mlstm_C, state_mlstm_n,
              state_mlstm_m, state_rwkv_shift, state_rwkv, page_table, norm1_g, w_in,
              mlstm_if_bias, mlstm_conv_w, mlstm_conv_b, nsa_cmp_pe, nsa_cmp_w1, nsa_cmp_w2,
              rwkv_mu, rwkv_w0, rwkv_w2, rwkv_a0, rwkv_a2, rwkv_g2, rwkv_k_k, rwkv_k_a,
              rwkv_r_k, rwkv_ln_g, rwkv_ln_b, w_branch_m, w_branch_a, w_branch_r, w_out,
              norm2_g, w_gate_up, w_down, final_norm_g):
    f32 = jnp.float32
    bp = x_prompt.shape[0]
    xp, xs = x_prompt, x_sample
    states_p, states_s = [], []
    for l in range(DEPTH):
        lp = {'norm1_g': norm1_g[l], 'w_in': w_in[l], 'mlstm_if_bias': mlstm_if_bias[l],
              'mlstm_conv_w': mlstm_conv_w[l], 'mlstm_conv_b': mlstm_conv_b[l],
              'rwkv_mu': rwkv_mu[l], 'rwkv_w0': rwkv_w0[l], 'rwkv_w2': rwkv_w2[l],
              'rwkv_a0': rwkv_a0[l], 'rwkv_a2': rwkv_a2[l], 'rwkv_g2': rwkv_g2[l],
              'rwkv_k_k': rwkv_k_k[l], 'rwkv_k_a': rwkv_k_a[l], 'rwkv_r_k': rwkv_r_k[l],
              'rwkv_ln_g': rwkv_ln_g[l], 'rwkv_ln_b': rwkv_ln_b[l],
              'w_branch_m': w_branch_m[l], 'w_branch_a': w_branch_a[l], 'w_branch_r': w_branch_r[l],
              'w_out': w_out[l], 'norm2_g': norm2_g[l], 'w_gate_up': w_gate_up[l], 'w_down': w_down[l]}
        nsa_p = functools.partial(nsa_prompt, cmp_pe=nsa_cmp_pe[l], cmp_w1=nsa_cmp_w1[l], cmp_w2=nsa_cmp_w2[l])
        m_zero = (jnp.zeros((bp, M_CONV - 1, 2 * M_WIDTH), xp.dtype),
                  jnp.zeros((bp, M_HEADS, M_HEAD_DIM, M_HEAD_DIM), f32),
                  jnp.zeros((bp, M_HEADS, M_HEAD_DIM), f32),
                  jnp.zeros((bp, M_HEADS), f32))
        r_zero = (jnp.zeros((bp, 1, R_COLS), xp.dtype),
                  jnp.zeros((bp, R_HEADS, R_HEAD_DIM, R_HEAD_DIM), f32))
        xp, nsa_new, m_new, r_new = trunk_layer(xp, lp, nsa_p, m_zero, r_zero)
        states_p.append(nsa_new + m_new + r_new)
        nsa_s = functools.partial(nsa_sample, pool_kc=cache_cmp_k[l], pool_vc=cache_cmp_v[l],
                                  pool_ks=cache_slc_k[l], pool_vs=cache_slc_v[l],
                                  win_k=cache_win_k[l], win_v=cache_win_v[l], page_table=page_table,
                                  cmp_pe=nsa_cmp_pe[l], cmp_w1=nsa_cmp_w1[l], cmp_w2=nsa_cmp_w2[l])
        xs, nsa_new, m_new, r_new = trunk_layer(
            xs, lp, nsa_s,
            (state_mlstm_conv[l], state_mlstm_C[l], state_mlstm_n[l], state_mlstm_m[l]),
            (state_rwkv_shift[l], state_rwkv[l]))
        states_s.append(nsa_new + m_new + r_new)
    y_prompt = rmsnorm(xp, final_norm_g)
    y_sample = rmsnorm(xs, final_norm_g)
    (p_cmp_k, p_cmp_v, p_slc_k, p_slc_v, p_win_k, p_win_v, p_m_conv, p_m_C, p_m_n, p_m_m,
     p_r_shift, p_r_S) = [jnp.stack(a) for a in zip(*states_p)]
    (s_cmp_k, s_cmp_v, s_slc_k, s_slc_v, s_win_k, s_win_v, s_m_conv, s_m_C, s_m_n, s_m_m,
     s_r_shift, s_r_S) = [jnp.stack(a) for a in zip(*states_s)]
    return (y_prompt, y_sample,
            p_cmp_k, p_cmp_v, p_slc_k, p_slc_v, p_win_k, p_win_v,
            p_m_conv, p_m_C, p_m_n, p_m_m, p_r_shift, p_r_S,
            s_cmp_k, s_cmp_v, s_slc_k, s_slc_v, s_win_k, s_win_v,
            s_m_conv, s_m_C, s_m_n, s_m_m, s_r_shift, s_r_S)


_drawn_inputs = setup_inputs


def setup_inputs(seed=0):
    import zlib

    import numpy as np

    out = dict(_drawn_inputs(seed))
    spreads = {}
    factors = {'cache_cmp_k': 3.946,
     'cache_cmp_v': 3.439,
     'cache_slc_k': 4.145,
     'cache_slc_v': 3.266,
     'nsa_cmp_pe': 3.547,
     'rwkv_ln_g': 8.0,
     'rwkv_ln_b': 8.0,
     'norm2_g': 3.837,
     'final_norm_g': 2.734}
    for name, (base, spread) in spreads.items():
        noise = np.random.default_rng([zlib.crc32(name.encode()), seed]).standard_normal(out[name].shape)
        drawn = base * np.exp(spread * noise) if base else spread * noise
        out[name] = jnp.asarray(drawn.astype(out[name].dtype))
    for name, factor in factors.items():
        out[name] = (out[name] * factor).astype(out[name].dtype)
    return out
```

```python
from contextlib import ExitStack

import concourse.bass as bass
from concourse import mybir
import numpy as np

F32 = mybir.dt.float32
I32 = mybir.dt.int32
ALU = mybir.AluOpType
ACT = mybir.ActivationFunctionType
AX = mybir.AxisListType

D, T, NS = 1024, 512, 8
TOK = T + NS
HALF = TOK // 2
KT = D // 128
MH, MD = 4, 128
NPAGE, PAGE = 16, 128
NBLK = 33
FF = 2816
FT = FF // 128
RMS_EPS, LN_EPS = 1e-6, 64e-5
NEG = -1e30
RING = 4
CH = 64
NC_ = T // CH
SCALE = 64 ** -0.5
KSCALE = MD ** -0.5

N_RWKV, N_MQK, N_MV, N_MO, N_Q, N_KV = 14, 8, 4, 4, 4, 6


def constants():
    p = np.arange(128)
    c = {}
    c["ident"] = np.eye(128)
    c["ones"] = np.ones((128, 128))
    c["bones"] = (p[:, None] // 64 == p[None, :] // 64) * 1.0
    c["id2"] = (p[:, None] % 64 == np.arange(64)[None, :]) * 1.0
    s, t = (p % 64)[:, None], np.arange(64)[None, :]
    c["strict"] = (s < t) * 1.0
    c["upto"] = (s <= t) * 1.0
    c["below"] = (s > t) * 1.0
    c["off1"] = ((s // 2 == t // 2) & (s < t)) * 1.0
    for n in (1, 2, 4, 8, 16, 32):
        c[f"offT{n}"] = ((s // (2 * n) == t // (2 * n)) & (s // n > t // n)) * 1.0
    c["reset"] = np.broadcast_to((np.arange(T) % CH != 0) * 1.0, (128, T))
    c["causal"] = np.where(np.arange(128)[None, :] <= p[:, None], 0.0, NEG)
    c["tri"] = (p[:, None] <= np.arange(128)[None, :]) * 1.0
    q = np.arange(4)[None, :, None] * 128 + p[:, None, None]
    end = np.arange(32)[None, None, :] * 16 + 31
    ok = (end <= q) & (np.arange(32)[None, None, :] < 31)
    c["cmpadd"] = np.where(ok, 0.0, NEG).reshape(128, 128)
    c["cmp01"] = (ok * 1.0).reshape(128, 128)
    n, j = p[:, None], np.arange(NBLK)[None, :]
    c["covers"] = ((n < 4 * j + 4) & (n >= 4 * j - 1) & (n < 127)) * 1.0
    e = np.zeros((128, 4, 128))
    for h in range(4):
        e[h, h] = 1.0
    c["headsel"] = e.reshape(128, 512)
    c["first"] = np.zeros((128, 1))
    c["first"][0] = NEG
    at, cols, out = 0, {}, []
    for k, v in c.items():
        cols[k] = (at, at + v.shape[1])
        at += v.shape[1]
        out.append(v)
    return np.ascontiguousarray(np.concatenate(out, 1).astype(np.float32)), cols


def block_selector():
    e = np.zeros((128, NPAGE, 2, 64))
    for b in range(32):
        e[b, b // 2, b % 2] = 1.0
    return e.reshape(128, 2048)[0:32].astype(np.float32)


PRM = {}
_at = 0
for _n, _w in (("g1", 8), ("g2", 8), ("gf", 8), ("mu", 14), ("w0", 4), ("a0", 4), ("kk", 4), ("ka", 4), ("rk", 4),
               ("lng", 4), ("lnb", 4), ("cw", 32), ("cb", 8)):
    PRM[_n] = (_at, _at + _w)
    _at += _w
NPRM = _at


class Counts:

    def __init__(self, nc, ctx, known):
        self.nc, self.ctx, self.known, self.found, self.sems, self.count = nc, ctx, known, {}, {}, {}

    def sem(self, key):
        if key not in self.sems:
            self.sems[key] = self.ctx.enter_context(self.nc.semaphore(key))
        return self.sems[key]

    def _add(self, key, name, n):
        self.count[key] = self.count.get(key, 0) + n
        if name:
            self.found[name] = (key, self.count[key])
        return self.sem(key), n

    def step(self, engine, *name):
        return self._add(engine + "_steps", name, 1)

    def tile_done(self, g):
        return self._add("tile_done", ("tile", g), 1)

    def moved(self, name, *index, lane=""):
        return self._add(f"moved_{name}{lane}", (name, *index), 16)

    def so_far(self, engine):
        return self.sem(engine + "_steps"), self.count[engine + "_steps"]

    def at(self, *name):
        key, value = self.known[name] if self.known else ("pe_steps", 1)
        return self.sem(key), value


def v3(ap, a):
    return ap.rearrange("p (a n) -> p a n", a=a)


def build(nc, io, known, phases):
    ctx = ExitStack()
    with ctx:
        counts = Counts(nc, ctx, known)
        sem, step, tile_done, moved, so_far, at = (counts.sem, counts.step, counts.tile_done, counts.moved,
                                                   counts.so_far, counts.at)
        _, CC = constants()
        NCN = max(b for _, b in CC.values())

        def sb(name, n, dt=F32):
            return ctx.enter_context(nc.sbuf_tensor(name, [128, n], dt))

        PS = ctx.enter_context(nc.psum_tensor("PS", [128, 8, 512], F32))
        cn = sb("cn", NCN)
        prm = sb("prm", NPRM)
        xn = sb("xn", KT * TOK)
        yr = sb("yr", 4 * TOK)
        ring = sb("ring", RING * 1024)
        rs = sb("rs", TOK)
        arena = sb("arena", 37900)

        def C(name, a=None):
            v = cn[:, CC[name][0]:CC[name][1]]
            return v if a is None else v3(v, a)

        def col(name, i=0):
            a = PRM[name][0] + i
            return prm[:, a:a + 1]

        def region(at, n):
            return arena[:, at:at + n]

        def tiles(ap, n):
            return v3(ap, n)

        def halves(ap):
            return v3(ap, 2)

        def pair(i):
            return PS[:, 2 * i:2 * i + 2, 0:HALF]

        XN = tiles(xn[:, :], KT)
        YR = tiles(yr[:, :], 4)
        id128 = C("ident")

        PIECES = []
        start = {}

        def plan(name, sizes):
            start[name] = len(PIECES)
            PIECES.extend(sizes)

        plan("rwkv", [8] * 14)
        plan("small", [8])
        plan("mlstm", [8] * 16)
        plan("attn", [8] * 10)
        plan("merge", [8, 4] * 24)
        plan("out", [8] * 8)
        plan("up", [8] * 44)
        plan("down", [8, 8, 6] * 8)

        def weight(g, k):
            s = g % RING
            return ring[:, s * 1024 + k * 128:s * 1024 + (k + 1) * 128]

        def product(pe, g, bank, src, first=True, last=True, kts=8, k0=0):
            pe.wait_ge(*at("weights", g))
            for k in range(kts):
                for half in range(2):
                    ins = nc.tensor.matmul(PS[:, 2 * bank + half, 0:HALF], weight(g, k),
                                           src[:, k0 + k, half * HALF:(half + 1) * HALF],
                                           start=first and k == 0, stop=last and k == kts - 1)
            ins.then_inc(*tile_done(g))

        def meet(eng, name, phase):
            if name + "_steps" in counts.count:
                eng.wait_ge(*so_far(name))
            eng.sem_inc(sem("phase_left"), 1)
            eng.wait_ge(sem("phase_left"), 4 * (phase + 1))

        def bones(pe, src, names, which="bones"):
            for t in range(4):
                for half in range(2):
                    ins = nc.tensor.matmul(PS[:, 2 * t + half, 0:HALF], C(which), src[:, t, half * HALF:(half + 1) * HALF],
                                           start=True, stop=True)
            ins.then_inc(*step("pe", *names))

        ALL8 = PS[:, :, 0:HALF]

        def all8(ap):
            return ap.rearrange("p (t n) -> p t n", t=8)

        X0 = tiles(region(0, KT * TOK), KT)
        SQ = tiles(region(KT * TOK, KT * TOK), KT)

        def norm_pe(pe, tag, sq):
            pe.wait_ge(*at(tag, "squares"))
            for k in range(KT):
                for half in range(2):
                    ins = nc.tensor.matmul(PS[:, 6 + half, 0:HALF], C("ones"), sq[:, k, half * HALF:(half + 1) * HALF],
                                           start=k == 0, stop=k == KT - 1)
            ins.then_inc(*step("pe", tag, "sum"))

        def norm_act(act, tag):
            act.wait_ge(*at(tag, "mean"))
            nc.scalar.activation(rs[:, :], rs[:, :], ACT.Sqrt).then_inc(*step("act", tag, "root"))
            act.wait_ge(*so_far("act"))

        def norm_dve(v, tag, src, sq, dst, gain):
            nc.vector.tensor_tensor(sq, src, src, ALU.mult).then_inc(*step("dve", tag, "squares"))
            v.wait_ge(*so_far("dve"))
            v.wait_ge(*at(tag, "sum"))
            nc.vector.tensor_scalar(halves(rs[:, :]), pair(3), 1.0 / D, RMS_EPS, ALU.mult, ALU.add).then_inc(*step("dve", tag, "mean"))
            v.wait_ge(*so_far("dve"))
            v.wait_ge(*at(tag, "root"))
            nc.vector.reciprocal(rs[:, :], rs[:, :]).then_inc(*step("dve"))
            v.wait_ge(*so_far("dve"))
            for k in range(KT):
                nc.vector.scalar_tensor_tensor(dst[:, k, :], src[:, k, :], col(gain, k), rs[:, :], ALU.mult, ALU.mult).then_inc(*step("dve", tag, "out"))
            v.wait_ge(*so_far("dve"))

        class Norm1:
            def pe(pe):
                pe.wait_ge(*at("cn"))
                norm_pe(pe, "norm1", SQ)

            def act(act):
                norm_act(act, "norm1")

            def dve(v):
                v.wait_ge(*at("x"))
                v.wait_ge(*at("cn"))
                v.wait_ge(*at("prm"))
                norm_dve(v, "norm1", X0, SQ, XN, "g1")

            def pool(p):
                p.dma_start(cn[:, :], io["cn"]).then_inc(*moved("cn"))
                p.dma_start(prm[:, :], io["prm"]).then_inc(*moved("prm"))
                p.dma_start(region(0, KT * TOK), io["x"]).then_inc(*moved("x"))

        a = 0

        def take(n):
            nonlocal a
            a += n
            return region(a - n, n)

        mixed = take(14 * TOK)
        raw = take(14 * (TOK + 1))
        LWr, AAr, KKr, TMPr = take(4 * TOK), take(4 * TOK), take(4 * TOK), take(4 * TOK)
        Gr, BNr = take(4 * TOK), take(4 * TOK)
        KHr, CUMr = take(4 * T), take(4 * T)
        rows = take(3 * 4 * T)
        small_r = take(600)
        MX = tiles(mixed, 14)
        RC = tiles(raw, 14)
        shift = small_r[:, 0:112].rearrange("p (t b) -> p t b", t=14)
        WS = small_r[:, 112:144].rearrange("p (t b) -> p t b", t=4)
        GL = small_r[:, 144:176].rearrange("p (t c) -> p t c", t=4)
        R_, K_, V_ = MX[:, 0:4, :], MX[:, 4:8, :], MX[:, 8:12, :]
        LW, AA, KK, TMP, G, BN = (tiles(r, 4) for r in (LWr, AAr, KKr, TMPr, Gr, BNr))
        lora = region(0, 1536)
        w2a2 = rows[:, 0:512]
        g2w = rows[:, 512:1024]
        AR = raw[:, 0:4096].rearrange("p (t c k n) -> p t c k n", t=4, c=NC_, k=2)
        BH = tiles(raw[:, 4096:6144], 4)
        KH, CUM = tiles(KHr, 4), tiles(CUMr, 4)
        CUMc = CUMr.rearrange("p (t c n) -> p t c n", t=4, c=NC_)
        ROW = {n: rows[:, i * 2048:(i + 1) * 2048].rearrange("p (c t n) -> p c t n", c=NC_, t=4) for i, n in enumerate("vbk")}
        big = region(14 * TOK + 14 * (TOK + 1), 8192)
        MB = big[:, 0:4096].rearrange("p (c t k n) -> p c t k n", c=NC_, t=4, k=2)
        MK = big[:, 4096:8192].rearrange("p (c t k n) -> p c t k n", c=NC_, t=4, k=2)
        MTt, Tt, TTt = (mixed[:, i * 2048:(i + 1) * 2048].rearrange("p (g n) -> p g n", g=32) for i in range(3))
        Wt = CUMr.rearrange("p (g n) -> p g n", g=32)
        OFF = MB[:, :, :, 0, :].rearrange("p c t n -> p (c t) n")
        Ssr, SAr, SBr = rows[:, 0:2048], rows[:, 2048:4096], rows[:, 4096:6144]
        XU = small_r

        def sview(ap):
            return ap.rearrange("p (b t n) -> p b t n", b=NS, t=4)

        def per_bt(ap):
            return ap.rearrange("p t b -> p b t").unsqueeze(3).broadcast_to([128, NS, 4, 64])

        ST = [sb(f"rwkv_state{i}", 256) for i in range(2)]
        XS, US = sb("rwkv_x", 256), sb("rwkv_u", 256)

        def q4(ap):
            return v3(ap, 4)

        BANKS4 = [PS[:, 0:4, :], PS[:, 4:8, :]]

        def b4(ap):
            return v3(ap, 4)

        def sc(x, t):
            return x[:, :, T:TOK]

        class Rwkv:
            def pe(pe):
                pe.wait_ge(*at("norm1", "out"))
                for t in range(14):
                    if t >= 3:
                        pe.wait_ge(*at("raw", t - 3))
                    product(pe, start["rwkv"] + t, t % 3, XN)
                pe.wait_ge(*at("lora"))
                pe.wait_ge(*at("tanh"))
                pe.wait_ge(*at("siggd"))
                for j in range(12):
                    kind, t = j // 4, j % 4
                    if j == 0:
                        pe.wait_ge(*at("raw", 13))
                    if j >= 4:
                        pe.wait_ge(*at("lora_out", j - 4))
                    rows_ = (slice(0, 64), slice(64, 128), slice(0, 128))[kind]
                    w = (w2a2, w2a2, g2w)[kind]
                    src = MX[:, 12 + kind // 2, :]
                    for half in range(2):
                        ins = nc.tensor.matmul(PS[:, 2 * t + half, 0:HALF], w[rows_, t * 128:(t + 1) * 128],
                                               src[rows_, half * HALF:(half + 1) * HALF], start=True, stop=True)
                    ins.then_inc(*step("pe", "lora_ps", j))
                pe.wait_ge(*at("lora_out", 11))
                pe.wait_ge(*at("kk_squares"))
                bones(pe, TMP, ("kk_sums",))
                pe.wait_ge(*at("bonus_terms"))
                bones(pe, TMP, ("bonus_sums",))
                pe.wait_ge(*at("s_sa_terms"))
                for i in range(4):
                    ins = nc.tensor.matmul(PS[:, i, :], C("bones"), SAr[:, i * 512:(i + 1) * 512], start=True, stop=True)
                ins.then_inc(*step("pe", "s_sa"))
                pe.wait_ge(*at("s_v_terms"))
                for i in range(4):
                    ins = nc.tensor.matmul(PS[:, 4 + i, :], C("bones"), SBr[:, i * 512:(i + 1) * 512], start=True, stop=True)
                ins.then_inc(*step("pe", "s_v"))
                pe.wait_ge(*at("s_state"))
                for b in range(NS):
                    for t in range(4):
                        for h in range(2):
                            q = slice(64 * h, 64 * h + 64)
                            ins = nc.tensor.matmul(PS[q, 0, t * 8 + b:t * 8 + b + 1], sview(Ssr)[q, b, t, :],
                                                   R_[q, t, T + b:T + b + 1], start=True, stop=True)
                ins.then_inc(*step("pe", "s_y"))
                pe.wait_ge(*at("hats"))
                for i, src in enumerate((V_, BH, KH)):
                    for c in range(NC_):
                        n = i * NC_ + c
                        bank = 1 + n // 2 % 4
                        if n % 2 == 0 and n >= 8:
                            pe.wait_ge(*at("row", n // 2 - 4))
                        for t in range(4):
                            for h in range(2):
                                q = slice(64 * h, 64 * h + 64)
                                ins = nc.tensor.matmul(PS[q, bank, (n % 2) * 256 + t * 64:(n % 2) * 256 + t * 64 + 64],
                                                       src[q, t, c * CH:(c + 1) * CH], C("id2")[q, :], start=True, stop=True)
                        if n % 2:
                            ins.then_inc(*step("pe", "row_ps", n // 2))
                pe.wait_ge(*at("row", 10))
                pe.wait_ge(*at("row", 11))
                for c in range(NC_):
                    o = 4 * (c % 2)
                    if c >= 2:
                        pe.wait_ge(*at("chunk_m", c - 2))
                    for t in range(4):
                        for h in range(2):
                            q = slice(64 * h, 64 * h + 64)
                            ar = AR[q, t, c, :, :].rearrange("p k n -> p (k n)")
                            cc = slice(c * CH, (c + 1) * CH)
                            nc.tensor.matmul(PS[q, o, t * 128:(t + 1) * 128], BH[q, t, cc], ar, start=True, stop=True)
                            nc.tensor.matmul(PS[q, o + 1, t * 128:(t + 1) * 128], KH[q, t, cc], ar, start=True, stop=True)
                            ins = nc.tensor.matmul(PS[q, o + 2, t * 64:(t + 1) * 64], AR[q, t, c, 0, :], BH[q, t, cc], start=True, stop=True)
                    ins.then_inc(*step("pe", "chunk_ps", c))
                for l in range(5):
                    pe.wait_ge(*at("off", l))
                    for g in range(32):
                        for h in range(2):
                            q = slice(64 * h, 64 * h + 64)
                            ins = nc.tensor.matmul(PS[q, g // 8, g % 8 * 64:g % 8 * 64 + 64], OFF[q, g, :], Tt[q, g, :], start=True, stop=True)
                    ins.then_inc(*step("pe", "w_ps", l))
                    pe.wait_ge(*at("w", l))
                    for g in range(32):
                        for h in range(2):
                            q = slice(64 * h, 64 * h + 64)
                            nc.tensor.matmul(PS[q, 4 + g // 8, g % 8 * 64:g % 8 * 64 + 64], TTt[q, g, :], Wt[q, g, :], start=True, stop=True)
                            ins = nc.tensor.matmul(PS[q, g // 8, g % 8 * 64:g % 8 * 64 + 64], Wt[q, g, :], TTt[q, g, :], start=True, stop=True)
                    ins.then_inc(*step("pe", "t_ps", l))
                pe.wait_ge(*at("t", 4))
                for c in range(NC_):
                    pe.wait_ge(*at("st", c))
                    S = q4(ST[c % 2][:, :])
                    for t in range(4):
                        for h in range(2):
                            q = slice(64 * h, 64 * h + 64)
                            n = slice(t * 64, t * 64 + 64)
                            nc.tensor.matmul(PS[q, 0, n], AR[q, t, c, 0, :], S[q, t, :], start=True, stop=False)
                            ins = nc.tensor.matmul(PS[q, 0, n], MK[q, c, t, 0, :], ROW["v"][q, c, t, :], start=False, stop=True)
                    ins.then_inc(*step("pe", "x_ps", c))
                    pe.wait_ge(*at("x_sb", c))
                    for t in range(4):
                        for h in range(2):
                            q = slice(64 * h, 64 * h + 64)
                            n = slice(t * 64, t * 64 + 64)
                            ins = nc.tensor.matmul(PS[q, 1, n], Tt[q, c * 4 + t, :], q4(XS[:, :])[q, t, :], start=True, stop=True)
                    ins.then_inc(*step("pe", "u_ps", c))
                    pe.wait_ge(*at("u_sb", c))
                    U = q4(US[:, :])
                    for t in range(4):
                        for h in range(2):
                            q = slice(64 * h, 64 * h + 64)
                            n = slice(t * 64, t * 64 + 64)
                            nc.tensor.matmul(PS[q, 3, n], ROW["b"][q, c, t, :], U[q, t, :], start=True, stop=False)
                            ins = nc.tensor.matmul(PS[q, 3, n], ROW["k"][q, c, t, :], ROW["v"][q, c, t, :], start=False, stop=True)
                    ins.then_inc(*step("pe", "s_ps", c))
                    if c >= 1:
                        pe.wait_ge(*at("y_sb", c - 1))
                    for t in range(4):
                        for h in range(2):
                            q = slice(64 * h, 64 * h + 64)
                            n = slice(t * 64, t * 64 + 64)
                            nc.tensor.matmul(PS[q, 2, n], S[q, t, :], AR[q, t, c, 1, :], start=True, stop=False)
                            nc.tensor.matmul(PS[q, 2, n], U[q, t, :], MB[q, c, t, 1, :], start=False, stop=False)
                            ins = nc.tensor.matmul(PS[q, 2, n], ROW["v"][q, c, t, :], MK[q, c, t, 1, :], start=False, stop=True)
                    ins.then_inc(*step("pe", "y_ps", c))
                pe.wait_ge(*at("y_sb", NC_ - 1))
                pe.wait_ge(*at("st", NC_))
                bones(pe, YR, ("y_sums",))
                pe.wait_ge(*at("y_squares"))
                bones(pe, TMP, ("y_square_sums",))
                pe.wait_ge(*so_far("pe"))

            def act(act):
                for t in range(14):
                    act.wait_ge(*at("tile", start["rwkv"] + t))
                    nc.scalar.copy(halves(RC[:, t, 1:TOK + 1]), pair(t % 3)).then_inc(*step("act", "raw", t))
                act.wait_ge(*at("mixed", 13))
                nc.scalar.activation(MX[0:64, 12, :], MX[0:64, 12, :], ACT.Tanh).then_inc(*step("act", "tanh"))
                act.wait_ge(*so_far("act"))
                nc.scalar.activation(MX[:, 13, :], MX[:, 13, :], ACT.Sigmoid).then_inc(*step("act", "siggd"))
                act.wait_ge(*so_far("act"))
                for j in range(8):
                    act.wait_ge(*at("lora_ps", j))
                    kind, t = j // 4, j % 4
                    nc.scalar.activation(halves((LW, AA)[kind][:, t, :]), pair(t), ACT.Sigmoid,
                                                  bias=col(("w0", "a0")[kind], t)).then_inc(*step("act", "lora_out", j))
                for t in range(4):
                    act.wait_ge(*at("lora_ps", 8 + t))
                    nc.scalar.copy(halves(G[:, t, :]), pair(t)).then_inc(*step("act", "lora_out", 8 + t))
                act.wait_ge(*at("kk_max"))
                nc.scalar.activation(TMPr, TMPr, ACT.Sqrt).then_inc(*step("act", "kk_root"))
                act.wait_ge(*so_far("act"))
                act.wait_ge(*at("lw"))
                nc.scalar.activation(WS, LW[:, :, T:TOK], ACT.Exp).then_inc(*step("act", "ws"))
                act.wait_ge(*so_far("act"))
                act.wait_ge(*at("cum_prev"))
                nc.scalar.activation(TMP[:, :, 0:T], TMP[:, :, 0:T], ACT.Exp).then_inc(*step("act", "e_prev"))
                act.wait_ge(*so_far("act"))
                act.wait_ge(*at("a_hat"))
                nc.scalar.activation(TMP[:, :, 0:T], CUM, ACT.Exp).then_inc(*step("act", "e_cum"))
                act.wait_ge(*so_far("act"))
                act.wait_ge(*at("r_hat"))
                nc.scalar.activation(TMP[:, :, 0:T], CUM, ACT.Exp, scale=-1.0).then_inc(*step("act", "e_inv"))
                act.wait_ge(*so_far("act"))
                act.wait_ge(*at("s_state_out"))
                for i in range(12):
                    if i % 2:
                        act.wait_ge(*at("row_ps", i))
                        r = ROW["vbk"[i // 4]][:, 2 * (i % 4):2 * (i % 4) + 2, :, :].rearrange("p c t n -> p (c t n)")
                        nc.scalar.copy(r, PS[:, 1 + i % 4, :]).then_inc(*step("act", "row", i))
                for l in range(5):
                    act.wait_ge(*at("w_ps", l))
                    nc.scalar.copy(Wt[:, :, :].rearrange("p g n -> p (g n)").rearrange("p (a n) -> p a n", a=4), PS[:, 0:4, :]).then_inc(*step("act", "w", l))
                    act.wait_ge(*so_far("act"))
                for c in range(NC_):
                    act.wait_ge(*at("u_ps", c))
                    if c >= 1:
                        act.wait_ge(*at("y_ps", c - 1))
                    nc.scalar.copy(US[:, :], PS[:, 1, 0:256]).then_inc(*step("act", "u_sb", c))
                    act.wait_ge(*at("y_ps", c))
                    nc.scalar.copy(YR[:, :, c * CH:(c + 1) * CH], q4(PS[:, 2, 0:256])).then_inc(*step("act", "y_sb", c))
                act.wait_ge(*at("y_var"))
                nc.scalar.activation(TMPr, TMPr, ACT.Sqrt).then_inc(*step("act", "y_root"))
                act.wait_ge(*so_far("act"))

            def dve(v):
                v.wait_ge(*at("shift"))
                v.wait_ge(*at("zero_col"))
                for t in range(14):
                    v.wait_ge(*at("raw", t))
                    nc.vector.tensor_tensor(MX[:, t, 0:T], RC[:, t, 0:T], RC[:, t, 1:T + 1], ALU.subtract).then_inc(*step("dve"))
                    nc.vector.tensor_tensor(MX[:, t, T:TOK], shift[:, t, :], RC[:, t, T + 1:TOK + 1], ALU.subtract).then_inc(*step("dve"))
                    v.wait_ge(*so_far("dve"))
                    nc.vector.scalar_tensor_tensor(MX[:, t, :], MX[:, t, :], col("mu", t), RC[:, t, 1:TOK + 1], ALU.mult, ALU.add).then_inc(*step("dve", "mixed", t))
                v.wait_ge(*so_far("dve"))
                for t in range(4):
                    nc.vector.tensor_scalar(KK[:, t, :], K_[:, t, :], col("kk", t), None, ALU.mult).then_inc(*step("dve"))
                v.wait_ge(*so_far("dve"))
                nc.vector.tensor_tensor(TMPr, KKr, KKr, ALU.mult).then_inc(*step("dve", "kk_squares"))
                v.wait_ge(*so_far("dve"))
                v.wait_ge(*at("kk_sums"))
                nc.vector.tensor_scalar(all8(TMPr), ALL8, 1e-24, None, ALU.max).then_inc(*step("dve", "kk_max"))
                v.wait_ge(*so_far("dve"))
                v.wait_ge(*at("kk_root"))
                nc.vector.reciprocal(TMPr, TMPr).then_inc(*step("dve"))
                v.wait_ge(*so_far("dve"))
                nc.vector.tensor_tensor(KKr, KKr, TMPr, ALU.mult).then_inc(*step("dve"))
                v.wait_ge(*so_far("dve"))
                for t in range(4):
                    v.wait_ge(*at("lora_out", 4 + t))
                    nc.vector.tensor_scalar(TMP[:, t, :], AA[:, t, :], 1.0, col("ka", t), ALU.subtract, ALU.mult).then_inc(*step("dve"))
                v.wait_ge(*so_far("dve"))
                nc.vector.scalar_tensor_tensor(K_, TMP, 1.0, K_, ALU.add, ALU.mult).then_inc(*step("dve"))
                v.wait_ge(*so_far("dve"))
                for t in range(4):
                    nc.vector.scalar_tensor_tensor(TMP[:, t, :], R_[:, t, :], col("rk", t), K_[:, t, :], ALU.mult, ALU.mult).then_inc(*step("dve", "bonus_terms"))
                v.wait_ge(*at("bonus_sums"))
                nc.vector.tensor_tensor(all8(BNr), ALL8, all8(mixed[:, 8 * TOK:12 * TOK]), ALU.mult).then_inc(*step("dve", "bonus"))
                v.wait_ge(*so_far("dve"))
                nc.vector.tensor_tensor(AAr, AAr, KKr, ALU.mult).then_inc(*step("dve"))
                v.wait_ge(*so_far("dve"))
                nc.vector.tensor_scalar(LWr, LWr, -float(np.exp(-0.5)), None, ALU.mult).then_inc(*step("dve", "lw"))
                v.wait_ge(*so_far("dve"))
                v.wait_ge(*at("s_rwkv"))
                nc.vector.tensor_tensor(sview(SAr), sview(Ssr), per_bt(KK[:, :, T:TOK]), ALU.mult).then_inc(*step("dve", "s_sa_terms"))
                v.wait_ge(*so_far("dve"))
                nc.vector.tensor_tensor(sview(SBr), C("id2").unsqueeze(1).unsqueeze(1).broadcast_to([128, NS, 4, 64]),
                                               per_bt(V_[:, :, T:TOK]), ALU.mult).then_inc(*step("dve", "s_v_terms"))
                v.wait_ge(*so_far("dve"))
                v.wait_ge(*at("ws"))
                nc.vector.tensor_tensor(sview(Ssr), sview(Ssr), per_bt(WS), ALU.mult).then_inc(*step("dve"))
                v.wait_ge(*so_far("dve"))
                v.wait_ge(*at("s_sa"))
                nc.vector.tensor_tensor(sview(SAr), BANKS4[0].rearrange("p a n -> p (a n)").rearrange("p (b t n) -> p b t n", b=NS, t=4),
                                               per_bt(AA[:, :, T:TOK]), ALU.mult).then_inc(*step("dve"))
                v.wait_ge(*so_far("dve"))
                nc.vector.tensor_tensor(Ssr, Ssr, SAr, ALU.subtract).then_inc(*step("dve"))
                v.wait_ge(*so_far("dve"))
                v.wait_ge(*at("s_v"))
                nc.vector.tensor_tensor(sview(SBr), BANKS4[1].rearrange("p a n -> p (a n)").rearrange("p (b t n) -> p b t n", b=NS, t=4),
                                               per_bt(K_[:, :, T:TOK]), ALU.mult).then_inc(*step("dve"))
                v.wait_ge(*so_far("dve"))
                nc.vector.tensor_tensor(Ssr, Ssr, SBr, ALU.add).then_inc(*step("dve", "s_state"))
                v.wait_ge(*so_far("dve"))
                for t in range(4):
                    nc.vector.tensor_tensor_scan(CUM[:, t, :], C("reset"), LW[:, t, 0:T], 0.0, ALU.mult, ALU.add).then_inc(*step("dve"))
                v.wait_ge(*so_far("dve"))
                nc.vector.tensor_tensor(TMP[:, :, 0:T], CUM, LW[:, :, 0:T], ALU.subtract).then_inc(*step("dve", "cum_prev"))
                v.wait_ge(*so_far("dve"))
                v.wait_ge(*at("e_prev"))
                v.wait_ge(*at("shift_out"))
                for t in range(4):
                    nc.vector.scalar_tensor_tensor(AR[:, t, :, 0, :], KK[:, t, 0:T].rearrange("p (c n) -> p c n", c=NC_), -1.0,
                                                          TMP[:, t, 0:T].rearrange("p (c n) -> p c n", c=NC_), ALU.mult, ALU.mult).then_inc(*step("dve", "a_hat"))
                v.wait_ge(*so_far("dve"))
                v.wait_ge(*at("e_cum"))
                for t in range(4):
                    nc.vector.tensor_tensor(AR[:, t, :, 1, :], R_[:, t, 0:T].rearrange("p (c n) -> p c n", c=NC_),
                                                   TMP[:, t, 0:T].rearrange("p (c n) -> p c n", c=NC_), ALU.mult).then_inc(*step("dve"))
                nc.vector.tensor_copy(GL, TMP[:, :, CH - 1:T:CH]).then_inc(*step("dve", "r_hat"))
                v.wait_ge(*so_far("dve"))
                v.wait_ge(*at("e_inv"))
                nc.vector.tensor_tensor(BH, AA[:, :, 0:T], TMP[:, :, 0:T], ALU.mult).then_inc(*step("dve"))
                nc.vector.tensor_tensor(KH, K_[:, :, 0:T], TMP[:, :, 0:T], ALU.mult).then_inc(*step("dve", "hats"))
                v.wait_ge(*at("s_y"))
                nc.vector.tensor_copy(YR[:, :, T:TOK], PS[:, 0, 0:32].rearrange("p (t b) -> p t b", t=4)).then_inc(*step("dve"))
                v.wait_ge(*at("s_state_out"))
                for i in range(0, 12, 2):
                    v.wait_ge(*at("row_ps", i))
                    r = ROW["vbk"[i // 4]][:, 2 * (i % 4):2 * (i % 4) + 2, :, :].rearrange("p c t n -> p (c t n)")
                    nc.vector.tensor_copy(r, PS[:, 1 + i % 4, :]).then_inc(*step("dve", "row", i))
                v.wait_ge(*at("row", 11))
                v.wait_ge(*so_far("dve"))
                strict = C("strict").unsqueeze(1).broadcast_to([128, 4, 64])
                upto = C("upto").unsqueeze(1).broadcast_to([128, 4, 64])
                below = C("below").unsqueeze(1).broadcast_to([128, 4, 64])
                for c in range(NC_):
                    v.wait_ge(*at("chunk_ps", c))
                    o = 4 * (c % 2)
                    for m, (dst, bank) in enumerate(((MB, o), (MK, o + 1))):
                        ps = PS[:, bank, :].rearrange("p (t k n) -> p t k n", t=4, k=2)
                        nc.vector.tensor_tensor(dst[:, c, :, 0, :], ps[:, :, 0, :], strict, ALU.mult).then_inc(*step("dve"))
                        nc.vector.tensor_tensor(dst[:, c, :, 1, :], ps[:, :, 1, :], upto, ALU.mult).then_inc(*step("dve"))
                    nc.vector.tensor_tensor(MTt[:, 4 * c:4 * c + 4, :], q4(PS[:, o + 2, 0:256]), below, ALU.mult).then_inc(*step("dve", "chunk_m", c))
                v.wait_ge(*so_far("dve"))

                def wide(name):
                    return C(name).unsqueeze(1).broadcast_to([128, 32, 64])

                nc.vector.tensor_tensor(Tt, OFF, wide("off1"), ALU.mult).then_inc(*step("dve"))
                nc.vector.tensor_tensor(TTt, MTt, wide("offT1"), ALU.mult).then_inc(*step("dve"))
                v.wait_ge(*so_far("dve"))
                nc.vector.tensor_tensor(Tt, Tt, wide("id2"), ALU.add).then_inc(*step("dve"))
                nc.vector.tensor_tensor(TTt, TTt, wide("id2"), ALU.add).then_inc(*step("dve"))
                for l in range(5):
                    nc.vector.tensor_tensor(OFF, MTt, wide(f"offT{2 << l}"), ALU.mult).then_inc(*step("dve", "off", l))
                    v.wait_ge(*so_far("dve"))
                    v.wait_ge(*at("t_ps", l))
                    ps = [PS[:, 4 * i:4 * i + 4, :].rearrange("p a n -> p (a n)").rearrange("p (g n) -> p g n", g=32) for i in range(2)]
                    nc.vector.tensor_tensor(Tt, ps[1], Tt, ALU.add).then_inc(*step("dve"))
                    nc.vector.tensor_tensor(TTt, ps[0], TTt, ALU.add).then_inc(*step("dve", "t", l))
                    v.wait_ge(*so_far("dve"))
                nc.vector.memset(ST[0][:, :], 0.0).then_inc(*step("dve", "st", 0))
                v.wait_ge(*so_far("dve"))
                for c in range(NC_):
                    v.wait_ge(*at("x_ps", c))
                    nc.vector.tensor_copy(XS[:, :], PS[:, 0, 0:256]).then_inc(*step("dve", "x_sb", c))
                    v.wait_ge(*at("s_ps", c))
                    if c >= 1:
                        v.wait_ge(*at("y_ps", c - 1))
                    nxt = ST[(c + 1) % 2]
                    nc.vector.tensor_tensor(nxt[:, :], PS[:, 3, 0:256], ST[c % 2][:, :], ALU.add).then_inc(*step("dve"))
                    v.wait_ge(*so_far("dve"))
                    nc.vector.tensor_tensor(q4(nxt[:, :]), q4(nxt[:, :]), GL[:, :, c:c + 1].broadcast_to([128, 4, 64]), ALU.mult).then_inc(*step("dve", "st", c + 1))
                    v.wait_ge(*so_far("dve"))
                v.wait_ge(*at("y_sums"))
                nc.vector.scalar_tensor_tensor(all8(yr[:, :]), ALL8, -1.0 / 64, all8(yr[:, :]), ALU.mult, ALU.add).then_inc(*step("dve"))
                v.wait_ge(*so_far("dve"))
                nc.vector.tensor_tensor(TMPr, yr[:, :], yr[:, :], ALU.mult).then_inc(*step("dve", "y_squares"))
                v.wait_ge(*so_far("dve"))
                v.wait_ge(*at("y_square_sums"))
                nc.vector.tensor_scalar(all8(TMPr), ALL8, 1.0 / 64, LN_EPS, ALU.mult, ALU.add).then_inc(*step("dve", "y_var"))
                v.wait_ge(*so_far("dve"))
                v.wait_ge(*at("y_root"))
                nc.vector.reciprocal(TMPr, TMPr).then_inc(*step("dve"))
                v.wait_ge(*so_far("dve"))
                nc.vector.tensor_tensor(yr[:, :], yr[:, :], TMPr, ALU.mult).then_inc(*step("dve"))
                v.wait_ge(*so_far("dve"))
                for t in range(4):
                    nc.vector.tensor_scalar(YR[:, t, :], YR[:, t, :], col("lng", t), col("lnb", t), ALU.mult, ALU.add).then_inc(*step("dve"))
                v.wait_ge(*so_far("dve"))
                nc.vector.tensor_tensor(yr[:, :], yr[:, :], BNr, ALU.add).then_inc(*step("dve"))
                v.wait_ge(*so_far("dve"))
                nc.vector.tensor_tensor(yr[:, :], yr[:, :], Gr, ALU.mult).then_inc(*step("dve", "yr"))
                v.wait_ge(*so_far("dve"))

            def pool(p):
                nc.gpsimd.memset(RC[:, :, 0:1], 0.0).then_inc(*step("pool", "zero_col"))
                p.dma_start(small_r[:, 0:112], io["rwkv_shift"]).then_inc(*moved("shift"))
                p.dma_start(rows[:, 0:1024], io["lora"]).then_inc(*moved("lora"))
                p.wait_ge(*at("raw", 13))
                p.dma_start(io["o_shift"].rearrange("p (t b) -> p t b", t=14), RC[:, :, T:TOK + 1]).then_inc(*moved("shift_out"))
                p.wait_ge(*at("lora_ps", 11))
                p.dma_start(Ssr, io["rwkv_state"]).then_inc(*moved("s_rwkv"))
                p.wait_ge(*at("s_state"))
                p.dma_start(io["o_sS"], Ssr).then_inc(*moved("s_state_out"))
                p.wait_ge(*at("st", NC_))
                p.dma_start(io["o_pS"], ST[NC_ % 2][:, :]).then_inc(*moved("p_state_out"))
                for n in ("shift_out", "s_state_out", "p_state_out"):
                    p.wait_ge(*at(n))

        TOP = 37900
        ym, ya, g24 = region(TOP - 2080, 2080), region(TOP - 4160, 2080), region(TOP - 4680, TOK)

        YM, YA = tiles(ym, 4), tiles(ya, 4)
        a = 0
        qkraw = take(8 * (T + 3))
        QKR = tiles(qkraw, 8)
        SFULL = take(8 * NS * 4).rearrange("p (t b j) -> p t b j", t=8, b=NS)
        convst = take(192).rearrange("p (t b j) -> p t b j", t=8, b=NS)
        convout = take(8 * 3 * (1 + NS)).rearrange("p (t b j) -> p t b j", t=8, b=1 + NS)
        qkr = take(8 * TOK)
        QK = tiles(qkr, 8)
        MVr, MOr = take(4 * TOK), take(4 * TOK)
        MV, MO = tiles(MVr, 4), tiles(MOr, 4)
        qkt = take(8 * TOK)
        QKT = tiles(qkt, 8)
        VROW = take(2048).rearrange("p (s h v) -> p s h v", s=4, h=MH)
        KROW = take(2048).rearrange("p (s h v) -> p s h v", s=4, h=MH)
        ATT = take(2 * 512)
        NMB, EMB = take(512), take(512)
        gates = take(24 * 1 + TOK)[:, 0:TOK]
        LI, LF, GA, GB = take(TOK), take(TOK), take(TOK), take(TOK)
        CUMF, UU, MM, MS = take(T), take(T), take(T), take(T)
        ifb = take(2)
        UT = take(16).rearrange("p (s h) -> p s h", s=4)
        WEND = take(16).rearrange("p (s h) -> p s h", s=4)
        pC, pn = take(512), take(4)
        m0, mp, cs, wi = take(NS), take(NS), take(NS), take(NS)
        DGs = take(96)
        BC = take(96)
        SN, KW, QN = take(32), take(32), take(64)
        rD = take(512)
        HS = take(32)
        SC = qkraw[:, 0:4096]
        VD = qkt[:, 0:4096]
        SC4 = v3(SC, 32)
        VD4 = v3(VD, 32)


        class Mlstm:
            def pe(pe):
                for n in range(17):
                    g = start["small"] + n
                    if n >= 3:
                        pe.wait_ge(*at("m_evac", n - 3))
                    product(pe, g, n % 3, XN)
                for n in range(14, 17):
                    pe.wait_ge(*at("m_evac", n))
                pe.wait_ge(*at("m_rows"))
                for st in range(4):
                    ins = nc.tensor.transpose(PS[:, 6, st * 4:st * 4 + 4], UU[0:4, st * 128:(st + 1) * 128], id128[0:4, 0:4])
                ins.then_inc(*step("pe", "ut_ps"))
                for i in range(8):
                    src, h0 = (MV, 0) if i < 4 else (QK, 4)
                    st = i % 4
                    if i >= 4:
                        pe.wait_ge(*at("qk", 7))
                        pe.wait_ge(*at("m_row", i - 4))
                    for h in range(MH):
                        ins = nc.tensor.transpose(PS[:, i % 4, h * 128:(h + 1) * 128], src[:, h0 + h, st * 128:(st + 1) * 128], id128)
                    ins.then_inc(*step("pe", "m_row_ps", i))
                n = 0
                for h in range(MH):
                    if h == 0:
                        pe.wait_ge(*at("m_row", 6))
                        pe.wait_ge(*at("m_row", 7))
                        pe.wait_ge(*at("ut"))
                    else:
                        pe.wait_ge(*at("m_bc", h - 1))
                    nc.tensor.matmul(PS[:, 6, :], C("headsel")[0:4, h * 128:(h + 1) * 128], MM[0:4, :], start=True, stop=True)
                    ins = nc.tensor.matmul(PS[:, 7, :], C("headsel")[0:4, h * 128:(h + 1) * 128], MS[0:4, :], start=True, stop=True)
                    ins.then_inc(*step("pe", "m_bc_ps", h))
                    for st in range(4):
                        w = T - st * 128
                        if n >= 2:
                            pe.wait_ge(*at("att_done", n - 2))
                        ins = nc.tensor.matmul(PS[:, n % 2, 0:w], QK[:, 4 + h, st * 128:(st + 1) * 128], QK[:, h, st * 128:T],
                                               start=True, stop=True)
                        ins.then_inc(*step("pe", "att_ps", n))
                        if st == 0 and h >= 1:
                            pe.wait_ge(*at("h_out", h - 1))
                        pe.wait_ge(*at("att_done", n))
                        nc.tensor.matmul(PS[:, 2, st * 128:T], VROW[:, st, h, :], ATT[:, n % 2 * 512:n % 2 * 512 + w], start=st == 0, stop=st == 3)
                        ins = nc.tensor.matmul(PS[:, 3, st * 128:T], C("ones"), ATT[:, n % 2 * 512:n % 2 * 512 + w], start=st == 0, stop=st == 3)
                        ins.then_inc(*step("pe", "num_ps", n))
                        n += 1
                    pe.wait_ge(*at("krow_w", h))
                    for st in range(4):
                        ins = nc.tensor.matmul(PS[:, 4, h * 128:(h + 1) * 128], KROW[:, st, h, :], VROW[:, st, h, :], start=st == 0, stop=st == 3)
                    for st in range(4):
                        ins = nc.tensor.matmul(PS[:, 5, h:h + 1], KROW[:, st, h, :], C("ones")[:, 0:1], start=st == 0, stop=st == 3)
                ins.then_inc(*step("pe", "pC_ps"))
                pe.wait_ge(*at("dg"))
                ins = nc.tensor.matmul(PS[:, 6, 0:96], C("ones")[0:4, :], DGs[0:4, :], start=True, stop=True)
                ins.then_inc(*step("pe", "bc_ps"))
                pe.wait_ge(*at("vd"))
                for i in range(8):
                    if i >= 4:
                        pe.wait_ge(*at("vb", i - 4))
                    ins = nc.tensor.matmul(PS[:, i % 4, :], C("ones"), VD[:, i * 512:(i + 1) * 512], start=True, stop=True)
                    ins.then_inc(*step("pe", "vb_ps", i))
                pe.wait_ge(*at("sC"))
                ins = nc.tensor.matmul(PS[:, 7, 0:32], C("ones"), QN[:, 0:32], start=True, stop=True)
                for h in range(MH):
                    for b in range(NS):
                        i = h * 8 + b
                        ins = nc.tensor.matmul(PS[:, 6, 128 + i:129 + i], SC4[:, i, :], QK[:, h, T + b:T + b + 1], start=True, stop=True)
                ins.then_inc(*step("pe", "s_num_ps"))
                pe.wait_ge(*so_far("pe"))

            def act(act):
                g0 = start["small"]
                act.wait_ge(*at("ifb"))
                act.wait_ge(*at("tile", g0))
                nc.scalar.activation(halves(g24[0:24, :]), PS[0:24, 0:2, 0:HALF], ACT.Sigmoid).then_inc(*step("act", "g24"))
                nc.scalar.activation(halves(LI[0:4, :]), PS[32:36, 0:2, 0:HALF], ACT.Identity, bias=ifb[0:4, 0:1]).then_inc(*step("act"))
                nc.scalar.activation(halves(LF[0:4, :]), PS[64:68, 0:2, 0:HALF], ACT.Identity, bias=ifb[0:4, 1:2]).then_inc(*step("act", "m_evac", 0))
                act.wait_ge(*at("zero_cols"))
                act.wait_ge(*at("m_conv_in"))
                for n in range(1, 9):
                    act.wait_ge(*at("tile", g0 + n))
                    nc.scalar.copy(QKR[:, n - 1, 3:3 + HALF], PS[:, 2 * (n % 3), 0:HALF]).then_inc(*step("act"))
                    nc.scalar.copy(QKR[:, n - 1, 3 + HALF:3 + T], PS[:, 2 * (n % 3) + 1, 0:T - HALF]).then_inc(*step("act"))
                    nc.scalar.copy(SFULL[:, n - 1, :, 3], PS[:, 2 * (n % 3) + 1, T - HALF:HALF]).then_inc(*step("act", "m_evac", n))
                for n in range(9, 17):
                    act.wait_ge(*at("tile", g0 + n))
                    if n < 13:
                        nc.scalar.copy(halves(MV[:, n - 9, :]), pair(n % 3)).then_inc(*step("act", "m_evac", n))
                    else:
                        nc.scalar.activation(halves(MO[:, n - 13, :]), pair(n % 3), ACT.Sigmoid).then_inc(*step("act", "m_evac", n))
                for t in range(8):
                    act.wait_ge(*at("convolved", t))
                    nc.scalar.activation(QKT[:, t, :], QK[:, t, :], ACT.Sigmoid).then_inc(*step("act", "qk_sig", t))
                act.wait_ge(*at("gabs"))
                nc.scalar.activation(GB[0:4, :], GA[0:4, :], ACT.Exp, scale=-1.0).then_inc(*step("act"))
                act.wait_ge(*so_far("act"))
                nc.scalar.activation(GB[0:4, :], GB[0:4, :], ACT.Ln, bias=1.0).then_inc(*step("act", "softplus"))
                act.wait_ge(*so_far("act"))
                for i in range(8):
                    act.wait_ge(*at("m_row_ps", i))
                    dst = (VROW, KROW)[i // 4][:, i % 4, :, :].rearrange("p h v -> p (h v)")
                    nc.scalar.copy(dst, PS[:, i % 4, :]).then_inc(*step("act", "m_row", i))
                n = 0
                for h in range(MH):
                    act.wait_ge(*at("m_bc_ps", h))
                    if h:
                        act.wait_ge(*at("h_out", h - 1))
                    nc.scalar.copy(NMB, PS[:, 6, :]).then_inc(*step("act"))
                    nc.scalar.activation(EMB, PS[:, 7, :], ACT.Exp, scale=-1.0).then_inc(*step("act", "m_bc", h))
                    act.wait_ge(*so_far("act"))
                    act.wait_ge(*at("ut"))
                    nc.scalar.activation(WEND[:, :, h], UT[:, :, h], ACT.Exp, bias=NMB[:, T - 1:T]).then_inc(*step("act", "wend", h))
                    for st in range(4):
                        act.wait_ge(*at("att_arg", n))
                        o = n % 2 * 512
                        nc.scalar.activation(ATT[:, o:o + T - st * 128], ATT[:, o:o + T - st * 128], ACT.Exp).then_inc(*step("act", "att_exp", n))
                        n += 1
                act.wait_ge(*at("s_args"))
                nc.scalar.activation(cs[0:4, :], cs[0:4, :], ACT.Exp).then_inc(*step("act"))
                nc.scalar.activation(wi[0:4, :], wi[0:4, :], ACT.Exp).then_inc(*step("act", "s_exps"))
                act.wait_ge(*at("bc"))
                nc.scalar.activation(BC[:, 64:96], BC[:, 64:96], ACT.Exp, scale=-1.0).then_inc(*step("act", "s_em"))
                act.wait_ge(*so_far("act"))

            def dve(v):
                v.wait_ge(*at("m_evac", 0))
                nc.vector.scalar_tensor_tensor(GA[0:4, :], LF[0:4, :], -1.0, LF[0:4, :], ALU.mult, ALU.max).then_inc(*step("dve", "gabs"))
                v.wait_ge(*so_far("dve"))
                for t in range(8):
                    v.wait_ge(*at("m_evac", 1 + t))
                    cw = [col("cw", t * 4 + j) for j in range(4)]
                    nc.vector.tensor_scalar(QK[:, t, 0:T], QKR[:, t, 0:T], cw[0], col("cb", t), ALU.mult, ALU.add).then_inc(*step("dve"))
                    nc.vector.tensor_scalar(QK[:, t, T:TOK], SFULL[:, t, :, 0], cw[0], col("cb", t), ALU.mult, ALU.add).then_inc(*step("dve"))
                    v.wait_ge(*so_far("dve"))
                    for j in range(1, 4):
                        nc.vector.scalar_tensor_tensor(QK[:, t, 0:T], QKR[:, t, j:j + T], cw[j], QK[:, t, 0:T], ALU.mult, ALU.add).then_inc(*step("dve"))
                        nc.vector.scalar_tensor_tensor(QK[:, t, T:TOK], SFULL[:, t, :, j], cw[j], QK[:, t, T:TOK], ALU.mult, ALU.add).then_inc(*step("dve", "convolved", t))
                        v.wait_ge(*so_far("dve"))
                    if t:
                        v.wait_ge(*at("qk_sig", t - 1))
                        nc.vector.scalar_tensor_tensor(QK[:, t - 1, :], QK[:, t - 1, :], 1.0 if t - 1 < 4 else KSCALE,
                                                              QKT[:, t - 1, :], ALU.mult, ALU.mult).then_inc(*step("dve", "qk", t - 1))
                v.wait_ge(*at("qk_sig", 7))
                nc.vector.scalar_tensor_tensor(QK[:, 7, :], QK[:, 7, :], KSCALE, QKT[:, 7, :], ALU.mult, ALU.mult).then_inc(*step("dve", "qk", 7))
                nc.vector.tensor_copy(convout[:, :, 0, :], QKR[:, :, T:T + 3]).then_inc(*step("dve"))
                nc.vector.tensor_copy(convout[:, :, 1:, :], SFULL[:, :, :, 1:4]).then_inc(*step("dve", "convout"))
                r = slice(0, 4)
                v.wait_ge(*at("softplus"))
                v.wait_ge(*so_far("dve"))
                nc.vector.scalar_tensor_tensor(LF[r, :], LF[r, :], 0.0, GB[r, :], ALU.min, ALU.subtract).then_inc(*step("dve"))
                v.wait_ge(*so_far("dve"))
                nc.vector.tensor_tensor_scan(CUMF[r, :], C("ones")[r, 0:1].broadcast_to([4, T]), LF[r, 0:T], 0.0, ALU.mult, ALU.add).then_inc(*step("dve"))
                v.wait_ge(*so_far("dve"))
                nc.vector.tensor_tensor(UU[r, :], LI[r, 0:T], CUMF[r, :], ALU.subtract).then_inc(*step("dve"))
                v.wait_ge(*so_far("dve"))
                nc.vector.tensor_tensor_scan(MM[r, :], UU[r, :], UU[r, :], 0.0, ALU.max, ALU.max).then_inc(*step("dve"))
                v.wait_ge(*so_far("dve"))
                nc.vector.tensor_tensor(MS[r, :], MM[r, :], CUMF[r, :], ALU.add).then_inc(*step("dve", "m_stab"))
                v.wait_ge(*so_far("dve"))
                nc.vector.tensor_scalar(MM[r, :], MM[r, :], -1.0, None, ALU.mult).then_inc(*step("dve", "m_rows"))
                v.wait_ge(*so_far("dve"))
                v.wait_ge(*at("ut_ps"))
                nc.vector.tensor_copy(UT, PS[:, 6, 0:16].rearrange("p (s h) -> p s h", s=4)).then_inc(*step("dve", "ut"))
                v.wait_ge(*so_far("dve"))
                n = 0
                for h in range(MH):
                    v.wait_ge(*at("m_bc", h))
                    for st in range(4):
                        o, w = n % 2 * 512, T - st * 128
                        if n >= 2:
                            v.wait_ge(*at("num_ps", n - 2))
                        nc.vector.tensor_scalar(ATT[:, o:o + w], NMB[:, st * 128:T], UT[:, st, h:h + 1], 0.0, ALU.add, ALU.min).then_inc(*step("dve", "att_arg", n))
                        v.wait_ge(*so_far("dve"))
                        v.wait_ge(*at("att_exp", n))
                        v.wait_ge(*at("att_ps", n))
                        nc.vector.tensor_tensor(ATT[:, o:o + w], ATT[:, o:o + w], PS[:, n % 2, 0:w], ALU.mult).then_inc(*step("dve"))
                        v.wait_ge(*so_far("dve"))
                        nc.vector.tensor_tensor(ATT[:, o:o + 128], ATT[:, o:o + 128], C("tri"), ALU.mult).then_inc(*step("dve", "att_done", n))
                        v.wait_ge(*so_far("dve"))
                        n += 1
                    v.wait_ge(*at("wend", h))
                    for st in range(4):
                        nc.vector.tensor_scalar(KROW[:, st, h, :], KROW[:, st, h, :], WEND[:, st, h:h + 1], None, ALU.mult).then_inc(*step("dve", "krow_w", h))
                    v.wait_ge(*at("num_ps", n - 1))
                    nc.vector.scalar_tensor_tensor(rD, PS[:, 3, :], -1.0, EMB, ALU.mult, ALU.max).then_inc(*step("dve"))
                    v.wait_ge(*so_far("dve"))
                    nc.vector.tensor_tensor(rD, rD, PS[:, 3, :], ALU.max).then_inc(*step("dve"))
                    v.wait_ge(*so_far("dve"))
                    nc.vector.reciprocal(rD, rD).then_inc(*step("dve"))
                    v.wait_ge(*so_far("dve"))
                    nc.vector.tensor_tensor(rD, rD, PS[:, 2, :], ALU.mult).then_inc(*step("dve", "h_out", h))
                    v.wait_ge(*so_far("dve"))
                    nc.vector.tensor_tensor(YM[:, h, 0:T], rD, MO[:, h, 0:T], ALU.mult).then_inc(*step("dve"))
                    v.wait_ge(*so_far("dve"))
                v.wait_ge(*at("pC_ps"))
                nc.vector.tensor_copy(pC, PS[:, 4, :]).then_inc(*step("dve"))
                nc.vector.tensor_copy(pn, PS[:, 5, 0:4]).then_inc(*step("dve", "pC"))
                v.wait_ge(*at("m0"))
                nc.vector.tensor_tensor(cs[r, :], LF[r, T:TOK], m0[r, :], ALU.add).then_inc(*step("dve"))
                v.wait_ge(*so_far("dve"))
                nc.vector.tensor_tensor(mp[r, :], cs[r, :], LI[r, T:TOK], ALU.max).then_inc(*step("dve", "s_m"))
                v.wait_ge(*so_far("dve"))
                nc.vector.tensor_tensor(cs[r, :], cs[r, :], mp[r, :], ALU.subtract).then_inc(*step("dve"))
                nc.vector.tensor_tensor(wi[r, :], LI[r, T:TOK], mp[r, :], ALU.subtract).then_inc(*step("dve", "s_args"))
                v.wait_ge(*at("s_exps"))
                for i, x in enumerate((cs, wi, mp)):
                    nc.vector.tensor_tensor(DGs[r, i * 32:(i + 1) * 32].rearrange("p (h b) -> p h b", h=4),
                                                   x[r, :].unsqueeze(1).broadcast_to([4, 4, NS]),
                                                   id128[r, 0:4].unsqueeze(2).broadcast_to([4, 4, NS]), ALU.mult).then_inc(*step("dve", "dg"))
                nc.vector.tensor_tensor(VD.rearrange("p (h b v) -> p h b v", h=4, b=NS),
                                               id128.unsqueeze(1).unsqueeze(1).broadcast_to([128, 4, NS, 128]),
                                               MV[:, :, T:TOK].unsqueeze(3).broadcast_to([128, 4, NS, 128]), ALU.mult).then_inc(*step("dve", "vd"))
                v.wait_ge(*at("bc_ps"))
                nc.vector.tensor_copy(BC, PS[:, 6, 0:96]).then_inc(*step("dve", "bc"))
                v.wait_ge(*so_far("dve"))
                v.wait_ge(*at("mn"))
                nc.vector.tensor_tensor(SN, SN, BC[:, 0:32], ALU.mult).then_inc(*step("dve"))
                nc.vector.tensor_tensor(v3(KW, 4), v3(BC[:, 32:64], 4), QK[:, 4:8, T:TOK], ALU.mult).then_inc(*step("dve"))
                v.wait_ge(*so_far("dve"))
                nc.vector.tensor_tensor(SN, SN, KW, ALU.add).then_inc(*step("dve", "sn"))
                v.wait_ge(*so_far("dve"))
                nc.vector.tensor_tensor(v3(QN[:, 0:32], 4), v3(SN, 4), QK[:, 0:4, T:TOK], ALU.mult).then_inc(*step("dve"))
                v.wait_ge(*so_far("dve"))
                v.wait_ge(*at("mC"))
                nc.vector.tensor_tensor(SC4, SC4, BC[:, 0:32].unsqueeze(2).broadcast_to([128, 32, 128]), ALU.mult).then_inc(*step("dve"))
                v.wait_ge(*so_far("dve"))
                for i in range(8):
                    v.wait_ge(*at("vb_ps", i))
                    nc.vector.tensor_tensor(VD4[:, 4 * i:4 * i + 4, :], PS[:, i % 4, :].rearrange("p (g n) -> p g n", g=4),
                                                   KW[:, 4 * i:4 * i + 4].unsqueeze(2).broadcast_to([128, 4, 128]), ALU.mult).then_inc(*step("dve", "vb", i))
                v.wait_ge(*so_far("dve"))
                nc.vector.tensor_tensor(SC, SC, VD, ALU.add).then_inc(*step("dve", "sC"))
                v.wait_ge(*so_far("dve"))
                v.wait_ge(*at("s_em"))
                v.wait_ge(*at("s_num_ps"))
                nc.vector.scalar_tensor_tensor(HS, PS[:, 7, 0:32], -1.0, BC[:, 64:96], ALU.mult, ALU.max).then_inc(*step("dve"))
                v.wait_ge(*so_far("dve"))
                nc.vector.tensor_tensor(HS, HS, PS[:, 7, 0:32], ALU.max).then_inc(*step("dve"))
                v.wait_ge(*so_far("dve"))
                nc.vector.reciprocal(HS, HS).then_inc(*step("dve"))
                v.wait_ge(*so_far("dve"))
                nc.vector.tensor_tensor(HS, HS, PS[:, 6, 128:160], ALU.mult).then_inc(*step("dve"))
                v.wait_ge(*so_far("dve"))
                nc.vector.tensor_tensor(YM[:, :, T:TOK], v3(HS, 4), MO[:, :, T:TOK], ALU.mult).then_inc(*step("dve", "ym"))
                v.wait_ge(*so_far("dve"))

            def pool(p):
                nc.gpsimd.memset(QKR[:, :, 0:3], 0.0).then_inc(*step("pool", "zero_cols"))
                p.dma_start(ifb[0:4, :], io["ifb"]).then_inc(*moved("ifb"))
                p.dma_start(convst.rearrange("p t b j -> p (t b j)")[:, 0:192], io["conv"]).then_inc(*moved("conv_in"))
                p.dma_start(m0[0:4, :], io["mm"]).then_inc(*moved("m0"))
                p.dma_start(SN, io["mn"]).then_inc(*moved("mn"))
                p.wait_ge(*at("conv_in"))
                nc.gpsimd.tensor_copy(SFULL[:, :, :, 0:3], convst).then_inc(*step("pool", "m_conv_in"))
                p.wait_ge(*at("m_stab"))
                p.dma_start(io["o_pm"], MS[0:4, T - 1:T]).then_inc(*moved("pm_out"))
                p.wait_ge(*at("convout"))
                p.dma_start(io["o_conv"], convout.rearrange("p t b j -> p (t b j)")).then_inc(*moved("conv_out"))
                p.dma_start(SC, io["mC"]).then_inc(*moved("mC"))
                n = 0
                p.wait_ge(*at("pC"))
                p.dma_start(io["o_pC"], pC).then_inc(*moved("pC_out"))
                p.dma_start(io["o_pn"], pn).then_inc(*moved("pn_out"))
                p.wait_ge(*at("s_m"))
                p.dma_start(io["o_sm"], mp[0:4, :]).then_inc(*moved("sm_out"))
                p.wait_ge(*at("sn"))
                p.dma_start(io["o_sn"], SN).then_inc(*moved("sn_out"))
                p.wait_ge(*at("sC"))
                p.dma_start(io["o_sC"], SC).then_inc(*moved("sC_out"))
                for x in ("pm_out", "conv_out", "pC_out", "pn_out", "sm_out", "sn_out", "sC_out"):
                    p.wait_ge(*at(x))

        a = 0
        Qr, KVr = take(4 * TOK), take(6 * TOK)
        Q, KV = tiles(Qr, 4), tiles(KVr, 6)
        w1d = take(4096).rearrange("p (kv j l h) -> p kv j l h", kv=2, j=2, l=16)
        w1 = take(2048).rearrange("p (kv j l h) -> p kv j l h", kv=2, j=2, l=8)
        pec = take(32)
        w2 = take(128)
        PEB = take(2)
        KEEP = a
        VR2 = take(1024).rearrange("p (b s f) -> p b s f", b=2, s=4)
        GR = take(96).rearrange("p (s n) -> p s n", s=4)
        HX, HSG = take(64), take(64)
        KC = take(32)
        VC = take(128)
        SCm, MXc, SMc = take(256), take(8), take(8)
        PTC = take(1024)
        Pb = [take(2048).rearrange("p (j n) -> p j n", j=4) for _ in range(2)]
        NBi = [take(4) for _ in range(2)]
        SUMi = [take(4) for _ in range(2)]
        RGi = take(4)
        PTb = [take(512) for _ in range(2)]
        UNITS = [(qt, g, br) for qt in range(4) for g in range(2) for br in range(2)]
        KB = [(i, kb) for i, (qt, g, br) in enumerate(UNITS) for kb in range(qt + 1)]
        KB_AT = {x: n for n, x in enumerate(KB)}

        def hid_evac(eng_act, tag, src, kv, n, X, S):
            nc.scalar.activation(X, src, ACT.Identity, bias=PEB[:, kv:kv + 1]).then_inc(*step("act"))
            nc.scalar.activation(S, src, ACT.Sigmoid, bias=PEB[:, kv:kv + 1]).then_inc(*step("act", tag, "hid_parts", n))

        class Attn:
            def pe(pe):
                for n in range(10):
                    if n >= 3:
                        pe.wait_ge(*at("a_evac", n - 3))
                    product(pe, start["attn"] + n, n % 3, XN)
                pe.wait_ge(*at("w1"))
                pe.wait_ge(*at("pe"))
                for kv in range(2):
                    for g in range(2):
                        for j in range(2):
                            for l in range(8):
                                i = kv * 16 + j * 8 + l
                                ins = nc.tensor.matmul(PS[64 * g:64 * g + 64, 6, kv:kv + 1], w1[:, kv, j, l, :], pec[:, i:i + 1],
                                                       start=j + l == 0, stop=j * 8 + l == 15)
                ins.then_inc(*step("pe", "peb_ps"))
                for n in range(7, 10):
                    pe.wait_ge(*at("a_evac", n))
                for i, br in enumerate((3, 5)):
                    for st in range(4):
                        ins = nc.tensor.transpose(PS[:, i, st * 128:(st + 1) * 128], KV[:, br, st * 128:(st + 1) * 128], id128)
                ins.then_inc(*step("pe", "vr_ps"))
                for st in range(4):
                    ins = nc.tensor.transpose(PS[:, 2, st * 24:st * 24 + 24], g24[0:24, st * 128:(st + 1) * 128], id128[0:24, 0:24])
                ins.then_inc(*step("pe", "gr_ps"))
                pe.wait_ge(*at("w1d"))
                for kv in range(2):
                    for g in range(2):
                        q = slice(64 * g, 64 * g + 64)
                        for j in range(2):
                            for l in range(16):
                                ins = nc.tensor.matmul(PS[q, 3 + kv, 0:31], w1d[q, kv, j, l, :],
                                                       KV[q, kv, 16 * j + l:16 * j + l + 481:16], start=j + l == 0, stop=j * 16 + l == 31)
                ins.then_inc(*step("pe", "hid_ps"))
                pe.wait_ge(*at("hid"))
                pe.wait_ge(*at("w2"))
                for g in range(2):
                    q = slice(64 * g, 64 * g + 64)
                    nc.tensor.matmul(PS[q, 5, 0:32], w2[q, 0:64], HX[q, 0:32], start=True, stop=True)
                for g in range(2):
                    q = slice(64 * g, 64 * g + 64)
                    ins = nc.tensor.matmul(PS[0:32, 7 - g, 0:64], HX[q, 32:64], w2[q, 64:128], start=True, stop=True)
                ins.then_inc(*step("pe", "kvc_ps"))
                pe.wait_ge(*at("kvc"))
                pe.wait_ge(*at("gr"))

                def cmp_scores(qt):
                    for g in range(2):
                        q = slice(64 * g, 64 * g + 64)
                        for j in range(4):
                            ins = nc.tensor.matmul(PS[:, 4 + g, j * 32:j * 32 + 32], Q[q, j, qt * 128:(qt + 1) * 128],
                                                   KC[q, :], start=True, stop=True)
                    ins.then_inc(*step("pe", "cmp_ps", qt))
                    pe.wait_ge(*at("cmp_p", qt))
                    for h in range(8):
                        ins = nc.tensor.transpose(PS[0:32, 4 + h // 4, h % 4 * 128:h % 4 * 128 + 128], SCm[:, h * 32:h * 32 + 32], id128)
                    ins.then_inc(*step("pe", "cmp_pt_ps", qt))
                    pe.wait_ge(*at("cmp_pt", qt))

                def scores(i):
                    qt, g, br = UNITS[i]
                    W = (qt + 1) * 128
                    q = slice(64 * g, 64 * g + 64)
                    if i >= 1:
                        pe.wait_ge(*at("exp", i - 1))
                    for j in range(4):
                        nc.tensor.matmul(PS[:, j, 0:W], Q[q, j, qt * 128:W], KV[q, (2, 4)[br], 0:W], start=True, stop=False)
                        ins = nc.tensor.matmul(PS[:, j, qt * 128:W], id128, C("causal"), start=False, stop=True)
                    ins.then_inc(*step("pe", "sc_ps", i))

                scores(0)
                for i, (qt, g, br) in enumerate(UNITS):
                    if g == 0 and br == 0:
                        if qt >= 1:
                            pe.wait_ge(*at("pt", KB_AT[(i - 1, qt - 1)]))
                            pe.wait_ge(*at("pt", KB_AT[(i - 1, qt - 1)] - 1))
                        cmp_scores(qt)
                    if i + 1 < len(UNITS):
                        scores(i + 1)
                    unit = i // 2
                    o = 6 + unit % 2
                    if br == 0:
                        if unit >= 2:
                            pe.wait_ge(*at("o_out", unit - 2))
                        nc.tensor.matmul(PS[:, o, :], VC[0:32, :], PTC[0:32, g * 512:(g + 1) * 512], start=True, stop=False)
                    pe.wait_ge(*at("p", i))
                    for kb in range(qt + 1):
                        n = KB_AT[(i, kb)]
                        if n >= 2:
                            pe.wait_ge(*at("pt", n - 2))
                        for j in range(4):
                            ins = nc.tensor.transpose(PS[:, 4 + n % 2, j * 128:(j + 1) * 128], Pb[i % 2][:, j, kb * 128:(kb + 1) * 128], id128)
                        ins.then_inc(*step("pe", "pt_ps", n))
                        pe.wait_ge(*at("pt", n))
                        ins = nc.tensor.matmul(PS[:, o, :], VR2[:, br, kb, :], PTb[n % 2], start=False, stop=br == 1 and kb == qt)
                        ins.then_inc(*step("pe", "pv", n))
                pe.wait_ge(*so_far("pe"))

            def act(act):
                for n in range(10):
                    act.wait_ge(*at("tile", start["attn"] + n))
                    dst = Q[:, n, :] if n < 4 else KV[:, n - 4, :]
                    nc.scalar.copy(halves(dst), pair(n % 3)).then_inc(*step("act", "a_evac", n))
                act.wait_ge(*at("peb"))
                act.wait_ge(*at("hid_ps"))
                for kv in range(2):
                    c = slice(kv * 32, kv * 32 + 31)
                    hid_evac(act, "prompt", PS[:, 3 + kv, 0:31], kv, kv, HX[:, c], HSG[:, c])
                for i, (qt, g, br) in enumerate(UNITS):
                    if g == 0 and br == 0:
                        act.wait_ge(*at("cmp_sub", qt))
                        nc.scalar.activation(SCm, SCm, ACT.Exp).then_inc(*step("act", "cmp_exp", qt))
                    act.wait_ge(*at("nb", i))
                    if i >= 2:
                        n = KB_AT[(i - 2, UNITS[i - 2][0])]
                        act.wait_ge(*at("pt_ps", n))
                    W = (qt + 1) * 128
                    for j in range(4):
                        nc.scalar.activation(Pb[i % 2][:, j, 0:W], PS[:, j, 0:W], ACT.Exp, bias=NBi[i % 2][:, j:j + 1], scale=SCALE,
                                                      accum_out=SUMi[i % 2][:, j:j + 1]).then_inc(*step("act", "exp", i))
                    for kb in range(qt + 1):
                        n = KB_AT[(i, kb)]
                        if n % 2:
                            act.wait_ge(*at("pt_ps", n))
                            if n >= 2:
                                act.wait_ge(*at("pv", n - 2))
                            nc.scalar.copy(PTb[n % 2], PS[:, 4 + n % 2, :]).then_inc(*step("act", "pt", n))
                    if br == 1:
                        unit = i // 2
                        act.wait_ge(*at("pv", KB_AT[(i, qt)]))
                        q = slice(64 * g, 64 * g + 64)
                        nc.scalar.copy(YA[q, :, qt * 128:(qt + 1) * 128], PS[q, 6 + unit % 2, :].rearrange("p (j n) -> p j n", j=4)).then_inc(*step("act", "o_out", unit))

            def dve(v):
                nc.vector.memset(HX, 0.0).then_inc(*step("dve", "hx_zero"))
                v.wait_ge(*so_far("dve"))
                v.wait_ge(*at("peb_ps"))
                nc.vector.tensor_copy(PEB, PS[:, 6, 0:2]).then_inc(*step("dve", "peb"))
                v.wait_ge(*at("vr_ps"))
                nc.vector.tensor_copy(VR2[:, :, :, :].rearrange("p b s f -> p b (s f)"), PS[:, 0:2, :]).then_inc(*step("dve"))
                v.wait_ge(*at("gr_ps"))
                nc.vector.tensor_copy(GR[:, :, :].rearrange("p s n -> p (s n)"), PS[:, 2, 0:96]).then_inc(*step("dve", "gr"))
                v.wait_ge(*at("prompt", "hid_parts", 1))
                nc.vector.tensor_tensor(v3(HX, 2)[:, :, 0:31], v3(HX, 2)[:, :, 0:31], v3(HSG, 2)[:, :, 0:31], ALU.mult).then_inc(*step("dve", "hid"))
                v.wait_ge(*so_far("dve"))
                v.wait_ge(*at("kvc_ps"))
                nc.vector.tensor_copy(KC, PS[:, 5, 0:32]).then_inc(*step("dve"))
                nc.vector.tensor_copy(VC[0:32, 0:64], PS[0:32, 7, 0:64]).then_inc(*step("dve"))
                nc.vector.tensor_copy(VC[0:32, 64:128], PS[0:32, 6, 0:64]).then_inc(*step("dve", "kvc"))
                S8 = v3(SCm, 8)

                def cmp(qt):
                    add = v3(C("cmpadd"), 4)[:, qt, :].unsqueeze(1).broadcast_to([128, 8, 32])
                    one = v3(C("cmp01"), 4)[:, qt, :].unsqueeze(1).broadcast_to([128, 8, 32])
                    v.wait_ge(*at("cmp_ps", qt))
                    if qt:
                        v.wait_ge(*at("cmp_pt_ps", qt - 1))
                    for g in range(2):
                        nc.vector.scalar_tensor_tensor(S8[:, 4 * g:4 * g + 4, :], v3(PS[:, 4 + g, 0:128], 4), SCALE, add[:, 0:4, :], ALU.mult, ALU.add).then_inc(*step("dve"))
                    v.wait_ge(*so_far("dve"))
                    nc.vector.tensor_reduce(MXc, S8, AX.X, ALU.max).then_inc(*step("dve"))
                    v.wait_ge(*so_far("dve"))
                    nc.vector.tensor_tensor(S8, S8, MXc.unsqueeze(2).broadcast_to([128, 8, 32]), ALU.subtract).then_inc(*step("dve", "cmp_sub", qt))
                    v.wait_ge(*so_far("dve"))
                    v.wait_ge(*at("cmp_exp", qt))
                    nc.vector.tensor_reduce(SMc, S8, AX.X, ALU.add).then_inc(*step("dve"))
                    v.wait_ge(*so_far("dve"))
                    nc.vector.reciprocal(SMc, SMc).then_inc(*step("dve"))
                    v.wait_ge(*so_far("dve"))
                    nc.vector.tensor_tensor(SMc, SMc, GR[:, qt, 0:8], ALU.mult).then_inc(*step("dve"))
                    v.wait_ge(*so_far("dve"))
                    nc.vector.tensor_tensor(S8, S8, one, ALU.mult).then_inc(*step("dve"))
                    v.wait_ge(*so_far("dve"))
                    nc.vector.tensor_tensor(S8, S8, SMc.unsqueeze(2).broadcast_to([128, 8, 32]), ALU.mult).then_inc(*step("dve", "cmp_p", qt))
                    v.wait_ge(*so_far("dve"))
                    v.wait_ge(*at("cmp_pt_ps", qt))
                    if qt:
                        v.wait_ge(*at("pv", KB_AT[(4 * qt - 1, 0)]))
                    nc.vector.tensor_copy(v3(PTC[0:32, :], 2), PS[0:32, 4:6, :]).then_inc(*step("dve", "cmp_pt", qt))

                def nb(i):
                    W = (UNITS[i][0] + 1) * 128
                    v.wait_ge(*at("sc_ps", i))
                    if i >= 2:
                        v.wait_ge(*at("exp", i - 2))
                    nc.vector.tensor_reduce(NBi[i % 2], PS[:, 0:4, 0:W], AX.X, ALU.max, negate=True).then_inc(*step("dve"))
                    v.wait_ge(*so_far("dve"))
                    nc.vector.tensor_scalar(NBi[i % 2], NBi[i % 2], SCALE, None, ALU.mult).then_inc(*step("dve", "nb", i))
                    v.wait_ge(*so_far("dve"))

                for i, (qt, g, br) in enumerate(UNITS):
                    if g == 0 and br == 0:
                        cmp(qt)
                    if i == 0:
                        nb(0)
                    v.wait_ge(*at("exp", i))
                    nc.vector.reciprocal(RGi, SUMi[i % 2]).then_inc(*step("dve"))
                    v.wait_ge(*so_far("dve"))
                    h = 8 * (br + 1) + 4 * g
                    nc.vector.tensor_tensor(RGi, RGi, GR[:, qt, h:h + 4], ALU.mult).then_inc(*step("dve"))
                    v.wait_ge(*so_far("dve"))
                    W = (qt + 1) * 128
                    for j in range(4):
                        nc.vector.tensor_scalar(Pb[i % 2][:, j, 0:W], Pb[i % 2][:, j, 0:W], RGi[:, j:j + 1], None, ALU.mult).then_inc(*step("dve", "p", i))
                    if i + 1 < len(UNITS):
                        if UNITS[i + 1][1:] == (0, 0):
                            pass
                        nb(i + 1)
                    for kb in range(qt + 1):
                        n = KB_AT[(i, kb)]
                        if n % 2 == 0:
                            v.wait_ge(*at("pt_ps", n))
                            if n >= 2:
                                v.wait_ge(*at("pv", n - 2))
                            nc.vector.tensor_copy(PTb[n % 2], PS[:, 4 + n % 2, :]).then_inc(*step("dve", "pt", n))

            def pool(p):
                p.dma_start(w1d.rearrange("p kv j l h -> p (kv j l h)"), io["w1d"]).then_inc(*moved("w1d"))
                p.dma_start(w1.rearrange("p kv j l h -> p (kv j l h)"), io["w1"]).then_inc(*moved("w1"))
                p.dma_start(pec, io["pe"]).then_inc(*moved("pe"))
                p.dma_start(w2, io["w2"]).then_inc(*moved("w2"))
                p.wait_ge(*at("a_evac", 9))
                p.dma_start(io["o_kv"], KVr).then_inc(*moved("kv_out"))
                p.wait_ge(*at("kv_out"))

        a = KEEP
        NSLOT = 23
        PG = [take(NPAGE * 384).rearrange("p (g k n) -> p g k n", g=NPAGE, k=3) for _ in range(2)]
        WIN = [take(1026).rearrange("p (k n) -> p k n", k=2) for _ in range(2)]
        HID = take(256)
        HSGs = take(256)
        KCs = take(128)
        QD = take(NS * 8).rearrange("p (b h) -> p b h", b=NS)
        SC_ = take(NSLOT * 64).rearrange("p (s n) -> p s n", s=NSLOT)
        VCs = take(NS * 128).rearrange("p (b f) -> p b f", b=NS)
        MXs, SMs = take(192), take(192)
        MXT = take(1)
        DGm = take(192)
        GBs = take(192)
        spent = w1d.rearrange("p kv j l h -> p (kv j l h)")
        ONEW = spent[:, 2048:4096].rearrange("p (k b f) -> p k b f", k=2, b=NS)
        BSEL = spent[:, 0:2048].rearrange("p (g n) -> p g n", g=NPAGE)
        PGRP = take(16)
        RANK, RSEL = take(NBLK), take(NBLK)
        TOP8 = take(8)
        ADDT = take(16)
        ADD = take(256).rearrange("p (g n) -> p g n", g=NPAGE)
        OUTs = take(64)
        G24D = take(192)
        tab = take(128).bitcast(I32)
        VP = [PG[i].rearrange("p g k n -> p (g k n)")[:, 0:2048].rearrange("p (g f) -> p g f", g=NPAGE) for i in range(2)]
        VPw = [PG[i].rearrange("p g k n -> p (g k n)")[:, 2048:2560].rearrange("p (g f) -> p g f", g=4) for i in range(2)]
        assert a <= TOP - 4680, a
        SLOTS = {"sel": (0, 17), "win": (17, 22), "cmp": (22, 23)}

        def bn(ap):
            return ap.rearrange("p (b h) -> p b h", b=NS)

        class Sample:
            def pe(pe):
                pe.wait_ge(*at("g24d"))
                ins = nc.tensor.matmul(PS[:, 7, 0:192], C("ones")[0:24, :], G24D[0:24, :], start=True, stop=True)
                ins.then_inc(*step("pe", "gb_ps"))
                for i, kv in enumerate((3, 5)):
                    for b in range(NS):
                        ins = nc.tensor.transpose(PS[0:1, 3 + 2 * i + b // 4, b % 4 * 128:b % 4 * 128 + 128], KV[:, kv, T + b:T + b + 1], id128)
                ins.then_inc(*step("pe", "new_v_ps"))
                pe.wait_ge(*at("new_v"))
                pe.wait_ge(*at("gb"))
                pe.wait_ge(*at("qd"))
                for b in range(NS):
                    p_ = PG[b % 2]
                    pe.wait_ge(*at("pages", b))
                    if b >= 1:
                        pe.wait_ge(*at("s_hid_parts", b - 1))
                    for kv in range(2):
                        for g in range(2):
                            q = slice(64 * g, 64 * g + 64)
                            for j in range(2):
                                for l in range(8):
                                    c = (l * 2 + g) * 8
                                    ins = nc.tensor.matmul(PS[q, kv, 1 - j:129 - j], w1[:, kv, j, l, :], p_[:, :, kv, c:c + 8],
                                                           start=j + l == 0, stop=j * 8 + l == 15, skip_group_check=True)
                    ins.then_inc(*step("pe", "s_hid_ps", b))
                    if b >= 1:
                        pe.wait_ge(*at("s_scores", b - 1))
                    for pg in range(NPAGE):
                        ins = nc.tensor.matmul(PS[:, 2, pg * 8:pg * 8 + 8], p_[:, pg, 2, :], QD[:, b, :], start=True, stop=True)
                    nc.tensor.matmul(PS[0:1, 2, 128:136], KV[:, 2, T + b:T + b + 1], QD[:, b, :], start=True, stop=True)
                    pe.wait_ge(*at("win", b))
                    for i in range(4):
                        nc.tensor.matmul(PS[:, 2, 136 + i * 8:144 + i * 8], WIN[b % 2][:, 0, i * 128:(i + 1) * 128], QD[:, b, :], start=True, stop=True)
                    ins = nc.tensor.matmul(PS[0:1, 2, 168:176], KV[:, 4, T + b:T + b + 1], QD[:, b, :], start=True, stop=True)
                    ins.then_inc(*step("pe", "s_sc_ps", b))
                    pe.wait_ge(*at("s_hid", b))
                    if b >= 1:
                        pe.wait_ge(*at("s_cmp_scores", b - 1))
                    for g in range(2):
                        q = slice(64 * g, 64 * g + 64)
                        nc.tensor.matmul(PS[q, 3, 0:127], w2[q, 0:64], HID[q, 0:127], start=True, stop=True)
                    for g in range(2):
                        q = slice(64 * g, 64 * g + 64)
                        ins = nc.tensor.matmul(PS[0:127, 4 + g, 0:64], HID[q, 128:255], w2[q, 64:128], start=True, stop=True)
                    ins.then_inc(*step("pe", "s_kvc_ps", b))
                    pe.wait_ge(*at("s_kvc", b))
                    ins = nc.tensor.matmul(PS[0:127, 6, 0:8], KCs[:, 0:127], QD[:, b, :], start=True, stop=True)
                    ins.then_inc(*step("pe", "s_cmp_ps", b))

                def softmax(br):
                    pe.wait_ge(*at("s_max", br))
                    ins = nc.tensor.transpose(PS[0:64, 0, 0:128], MXs[:, 0:64], id128)
                    ins.then_inc(*step("pe", "s_maxt_ps", br))
                    pe.wait_ge(*at("s_maxd", br))
                    ins = nc.tensor.matmul(PS[:, 1, 0:64], C("ones")[0:64, :], DGm[0:64, 0:64], start=True, stop=True)
                    ins.then_inc(*step("pe", "s_maxb_ps", br))
                    pe.wait_ge(*at("s_sum", br))
                    ins = nc.tensor.matmul(PS[:, 2, 0:64], C("ones"), SMs[:, 0:64], start=True, stop=True)
                    ins.then_inc(*step("pe", "s_sum_ps", br))

                pe.wait_ge(*at("s_cmp_scores", NS - 1))
                softmax("cmp")
                pe.wait_ge(*at("pgrp"))
                ins = nc.tensor.matmul(PS[0:16, 3, 0:NBLK], PGRP, C("covers"), start=True, stop=True)
                ins.then_inc(*step("pe", "rank_ps"))
                pe.wait_ge(*at("rsel"))
                ins = nc.tensor.transpose(PS[0:32, 4, 0:16], RSEL[0:16, 0:32], id128[0:16, 0:16])
                ins.then_inc(*step("pe", "addt_ps"))
                pe.wait_ge(*at("addt"))
                pe.wait_ge(*at("blocksel"))
                for pg in range(NPAGE):
                    ins = nc.tensor.matmul(PS[:, 3, pg * 16:pg * 16 + 16], BSEL[0:32, pg, :], ADDT[0:32, :], start=True, stop=True)
                ins.then_inc(*step("pe", "add_ps"))
                softmax("sel")
                softmax("win")
                pe.wait_ge(*at("s_p"))
                pe.wait_ge(*at("new_v"))
                for b in range(NS):
                    o = slice(b * 8, b * 8 + 8)
                    pe.wait_ge(*at("pages_v", b))
                    for pg in range(NPAGE):
                        nc.tensor.matmul(PS[:, 6, o], VP[b % 2][:, pg, :], SC_[:, pg, o], start=pg == 0, stop=False)
                    nc.tensor.matmul(PS[:, 6, o], ONEW[0:1, 0, b, :], SC_[0:1, 16, o], start=False, stop=False)
                    for i in range(4):
                        nc.tensor.matmul(PS[:, 6, o], VPw[b % 2][:, i, :], SC_[:, 17 + i, o], start=False, stop=False)
                    nc.tensor.matmul(PS[:, 6, o], ONEW[0:1, 1, b, :], SC_[0:1, 21, o], start=False, stop=False)
                    ins = nc.tensor.matmul(PS[:, 6, o], VCs[0:127, b, :], SC_[0:127, 22, o], start=False, stop=True)
                    ins.then_inc(*step("pe", "s_pv", b))
                pe.wait_ge(*so_far("pe"))

            def act(act):
                for b in range(NS):
                    act.wait_ge(*at("s_hid_ps", b))
                    if b >= 1:
                        act.wait_ge(*at("s_kvc_ps", b - 1))
                    for kv in range(2):
                        nc.scalar.activation(HID[:, kv * 128:kv * 128 + 127], PS[:, kv, 1:128], ACT.Identity, bias=PEB[:, kv:kv + 1]).then_inc(*step("act"))
                        nc.scalar.activation(HSGs[:, kv * 128:kv * 128 + 127], PS[:, kv, 1:128], ACT.Sigmoid, bias=PEB[:, kv:kv + 1]).then_inc(*step("act", "s_hid_parts", b))
                for br in ("cmp", "sel", "win"):
                    act.wait_ge(*at("s_sub", br))
                    a_, b_ = SLOTS[br]
                    nc.scalar.activation(SC_[:, a_:b_, :], SC_[:, a_:b_, :], ACT.Exp).then_inc(*step("act", "s_exp", br))

            def dve(v):
                nc.vector.memset(SC_, NEG).then_inc(*step("dve", "sc_zero"))
                v.wait_ge(*so_far("dve"))
                nc.vector.tensor_tensor(G24D[0:24, :].rearrange("p (r b h) -> p r b h", r=3, b=NS),
                                               g24[0:24, T:TOK].unsqueeze(1).unsqueeze(3).broadcast_to([24, 3, NS, 8]),
                                               id128[0:24, 0:24].rearrange("p (r h) -> p r h", r=3).unsqueeze(2).broadcast_to([24, 3, NS, 8]),
                                               ALU.mult).then_inc(*step("dve", "g24d"))
                nc.vector.memset(QD, 0.0).then_inc(*step("dve"))
                v.wait_ge(*so_far("dve"))
                for g in range(2):
                    q = slice(64 * g, 64 * g + 64)
                    nc.vector.tensor_copy(QD[q, :, 4 * g:4 * g + 4], Q[q, :, T:TOK].rearrange("p j b -> p b j")).then_inc(*step("dve", "qd"))
                v.wait_ge(*at("gb_ps"))
                nc.vector.tensor_copy(GBs, PS[:, 7, 0:192]).then_inc(*step("dve", "gb"))
                v.wait_ge(*at("new_v_ps"))
                nc.vector.tensor_copy(ONEW[0:1].rearrange("p k b f -> p (k b f)").rearrange("p (a n) -> p a n", a=4), PS[0:1, 3:7, :]).then_inc(*step("dve", "new_v"))
                for b in range(NS):
                    o = slice(b * 8, b * 8 + 8)
                    v.wait_ge(*at("s_sc_ps", b))
                    nc.vector.tensor_scalar(SC_[:, 0:16, o], PS[:, 2, 0:128].rearrange("p (s h) -> p s h", s=16), SCALE, None, ALU.mult).then_inc(*step("dve"))
                    nc.vector.tensor_scalar(SC_[0:1, 16, o], PS[0:1, 2, 128:136], SCALE, None, ALU.mult).then_inc(*step("dve"))
                    nc.vector.tensor_scalar(SC_[:, 17:21, o], PS[:, 2, 136:168].rearrange("p (s h) -> p s h", s=4), SCALE, None, ALU.mult).then_inc(*step("dve"))
                    nc.vector.tensor_scalar(SC_[0:1, 21, o], PS[0:1, 2, 168:176], SCALE, None, ALU.mult).then_inc(*step("dve", "s_scores", b))
                    v.wait_ge(*at("s_hid_parts", b))
                    nc.vector.tensor_tensor(v3(HID, 2)[:, :, 0:127], v3(HID, 2)[:, :, 0:127], v3(HSGs, 2)[:, :, 0:127], ALU.mult).then_inc(*step("dve", "s_hid", b))
                    v.wait_ge(*so_far("dve"))
                    v.wait_ge(*at("s_kvc_ps", b))
                    nc.vector.tensor_copy(KCs[:, 0:127], PS[:, 3, 0:127]).then_inc(*step("dve"))
                    nc.vector.tensor_copy(v3(VCs[0:127, b, :], 2), PS[0:127, 4:6, 0:64]).then_inc(*step("dve", "s_kvc", b))
                    v.wait_ge(*at("s_cmp_ps", b))
                    nc.vector.tensor_scalar(SC_[0:127, 22, o], PS[0:127, 6, 0:8], SCALE, None, ALU.mult).then_inc(*step("dve", "s_cmp_scores", b))
                v.wait_ge(*so_far("dve"))
                nc.vector.tensor_scalar(SC_[:, 17, :], SC_[:, 17, :], C("first"), None, ALU.add).then_inc(*step("dve"))
                v.wait_ge(*so_far("dve"))

                def softmax(br, gate):
                    a_, b_ = SLOTS[br]
                    n = b_ - a_
                    S = SC_[:, a_:b_, :]
                    nc.vector.tensor_reduce(MXs[:, 0:64], S.rearrange("p s n -> p n s"), AX.X, ALU.max).then_inc(*step("dve", "s_max", br))
                    v.wait_ge(*so_far("dve"))
                    v.wait_ge(*at("s_maxt_ps", br))
                    nc.vector.tensor_reduce(MXT[0:64, :], PS[0:64, 0, 0:128], AX.X, ALU.max).then_inc(*step("dve"))
                    v.wait_ge(*so_far("dve"))
                    nc.vector.tensor_scalar(DGm[0:64, 0:64], id128[0:64, 0:64], MXT[0:64, :], None, ALU.mult).then_inc(*step("dve", "s_maxd", br))
                    v.wait_ge(*so_far("dve"))
                    v.wait_ge(*at("s_maxb_ps", br))
                    nc.vector.tensor_tensor(S, S, PS[:, 1, 0:64].unsqueeze(1).broadcast_to([128, n, 64]), ALU.subtract).then_inc(*step("dve", "s_sub", br))
                    v.wait_ge(*so_far("dve"))
                    v.wait_ge(*at("s_exp", br))
                    nc.vector.tensor_reduce(SMs[:, 0:64], S.rearrange("p s n -> p n s"), AX.X, ALU.add).then_inc(*step("dve", "s_sum", br))
                    v.wait_ge(*so_far("dve"))
                    v.wait_ge(*at("s_sum_ps", br))
                    nc.vector.reciprocal(SMs[:, 64:128], PS[:, 2, 0:64]).then_inc(*step("dve"))
                    v.wait_ge(*so_far("dve"))
                    if br == "cmp":
                        nc.vector.tensor_tensor(MXs[:, 64:128], SC_[:, 22, :], SMs[:, 64:128], ALU.mult).then_inc(*step("dve"))
                        v.wait_ge(*so_far("dve"))
                        nc.vector.tensor_reduce(PGRP, MXs[:, 64:128].rearrange("p (g j) -> p g j", j=4), AX.X, ALU.add).then_inc(*step("dve", "pgrp"))
                        v.wait_ge(*so_far("dve"))
                    nc.vector.tensor_tensor(SMs[:, 64:128], SMs[:, 64:128], GBs[:, gate * 64:(gate + 1) * 64], ALU.mult).then_inc(*step("dve"))
                    v.wait_ge(*so_far("dve"))
                    nc.vector.tensor_tensor(S, S, SMs[:, 64:128].unsqueeze(1).broadcast_to([128, n, 64]), ALU.mult).then_inc(*step("dve", "s_p"))
                    v.wait_ge(*so_far("dve"))

                softmax("cmp", 0)
                r = slice(0, 16)
                v.wait_ge(*at("rank_ps"))
                nc.vector.tensor_copy(RANK[r, :], PS[r, 3, 0:NBLK]).then_inc(*step("dve"))
                v.wait_ge(*so_far("dve"))
                nc.vector.memset(RANK[r, 0:1], 1e9).then_inc(*step("dve"))
                v.wait_ge(*so_far("dve"))
                nc.vector.memset(RANK[r, NBLK - 2:NBLK], 1e9).then_inc(*step("dve"))
                v.wait_ge(*so_far("dve"))
                for _ in range(2):
                    nc.vector.max(TOP8[r, :], RANK[r, :]).then_inc(*step("dve"))
                    v.wait_ge(*so_far("dve"))
                    nc.vector.match_replace(RSEL[r, :], TOP8[r, :], RANK[r, :], -3e38).then_inc(*step("dve"))
                    v.wait_ge(*so_far("dve"))
                    nc.vector.tensor_copy(RANK[r, :], RSEL[r, :]).then_inc(*step("dve"))
                    v.wait_ge(*so_far("dve"))
                nc.vector.tensor_scalar(RSEL[r, :], RANK[r, :], -1e37, NEG, ALU.is_gt, ALU.mult).then_inc(*step("dve", "rsel"))
                v.wait_ge(*so_far("dve"))
                v.wait_ge(*at("addt_ps"))
                nc.vector.tensor_copy(ADDT[0:32, :], PS[0:32, 4, 0:16]).then_inc(*step("dve", "addt"))
                v.wait_ge(*so_far("dve"))
                v.wait_ge(*at("add_ps"))
                nc.vector.tensor_copy(ADD, PS[:, 3, 0:256].rearrange("p (g n) -> p g n", g=NPAGE)).then_inc(*step("dve"))
                v.wait_ge(*so_far("dve"))
                S4 = SC_[:, 0:16, :].rearrange("p s (g j) -> p s g j", j=4)
                for j in range(4):
                    nc.vector.tensor_tensor(S4[:, :, :, j], S4[:, :, :, j], ADD, ALU.add).then_inc(*step("dve"))
                v.wait_ge(*so_far("dve"))
                softmax("sel", 1)
                softmax("win", 2)
                v.wait_ge(*at("s_pv", NS - 1))
                O = PS[:, 6, 0:64].rearrange("p (b h) -> p b h", b=NS)
                for g in range(2):
                    q = slice(64 * g, 64 * g + 64)
                    nc.vector.tensor_copy(YA[q, :, T:TOK], O[q, :, 4 * g:4 * g + 4].rearrange("p b j -> p j b")).then_inc(*step("dve", "ya"))

            def pool(p):
                p.dma_start(tab[0:1, :], io["table"]).then_inc(*moved("table"))
                p.dma_start(BSEL[0:32].rearrange("p g n -> p (g n)"), io["blocksel"]).then_inc(*moved("blocksel"))
                p.wait_ge(*at("table"))

                def page(b, pg, limit):
                    return p.value_load(tab[0:1, b * NPAGE + pg:b * NPAGE + pg + 1], min_val=0, max_val=limit - 1)

                n_pool = io["pages"].shape[0]
                for b in range(NS):
                    if b >= 2:
                        p.wait_ge(*at("s_sc_ps", b - 2))
                        p.wait_ge(*at("s_hid_ps", b - 2))
                        p.wait_ge(*at("win_out", b - 2))
                    for pg in range(NPAGE):
                        r = page(b, pg, n_pool)
                        p.dma_start(PG[b % 2][:, pg], io["pages"][bass.ds(r, 1)].rearrange("a p k n -> p (a k) n")).then_inc(*moved("pages", b, lane=b % 2))
                    p.dma_start(WIN[b % 2][:, :, 0:512], io["win"][:, b]).then_inc(*moved("win", b, lane=b % 2))
                    nc.gpsimd.tensor_copy(WIN[b % 2][:, :, 512:513], KV[:, 4:6, T + b:T + b + 1]).then_inc(*step("pool"))
                    p.wait_ge(*so_far("pool"))
                    p.wait_ge(*at("win", b))
                    p.dma_start(io["o_winp"][b].rearrange("k p n -> p k n"), WIN[b % 2][:, :, 1:513]).then_inc(*moved("win_out", b, lane=b % 2))
                for b in range(NS):
                    if b < 2:
                        p.wait_ge(*at("s_sc_ps", NS - 2 + b))
                        p.wait_ge(*at("s_hid_ps", NS - 2 + b))
                    else:
                        p.wait_ge(*at("s_pv", b - 2))
                    for pg in range(NPAGE):
                        r = page(b, pg, n_pool)
                        p.dma_start(VP[b % 2][:, pg], io["pages_v"][bass.ds(r, 1)].rearrange("a p n -> p (a n)")).then_inc(*moved("pages_v", b, lane=b % 2))
                    p.dma_start(VPw[b % 2], io["win_v"][:, b]).then_inc(*moved("pages_v", b, lane=b % 2))
                for b in (NS - 2, NS - 1):
                    p.wait_ge(*at("win_out", b))

        a = 0
        MGr = take(KT * TOK)
        MG = tiles(MGr, KT)
        SG = [take(TOK) for _ in range(2)]
        PR = [take(TOK) for _ in range(2)]
        X2r = take(KT * TOK)
        X2 = tiles(X2r, KT)
        SQ2 = take(KT * TOK)
        assert a < TOP - 4680

        BR = (YM, YA, YR)

        class Merge:
            def pe(pe):
                for i in range(24):
                    g = start["merge"] + 2 * i
                    if i >= 2:
                        pe.wait_ge(*at("gate_sig", i - 2))
                    product(pe, g, i % 2, XN)
                    if i >= 2:
                        pe.wait_ge(*at("gated", i - 2))
                    product(pe, g + 1, 2 + i % 2, BR[i % 3], kts=4)
                for m in range(8):
                    if m == 0:
                        pe.wait_ge(*at("merged"))
                    if m >= 4:
                        pe.wait_ge(*at("x2", m - 4))
                    product(pe, start["out"] + m, m % 4, MG)
                pe.wait_ge(*so_far("pe"))

            def act(act):
                for i in range(24):
                    act.wait_ge(*at("tile", start["merge"] + 2 * i))
                    if i >= 2:
                        act.wait_ge(*at("gated", i - 2))
                    nc.scalar.activation(halves(SG[i % 2]), pair(i % 2), ACT.Sigmoid).then_inc(*step("act", "gate_sig", i))

            def dve(v):
                for i in range(24):
                    m, b = i // 3, i % 3
                    v.wait_ge(*at("gate_sig", i))
                    v.wait_ge(*at("tile", start["merge"] + 2 * i + 1))
                    dst = MG[:, m, :] if b == 0 else PR[i % 2]
                    nc.vector.tensor_tensor(halves(dst), pair(2 + i % 2), halves(SG[i % 2]), ALU.mult).then_inc(*step("dve", "gated", i))
                    v.wait_ge(*so_far("dve"))
                    if b:
                        nc.vector.tensor_tensor(MG[:, m, :], MG[:, m, :], PR[i % 2], ALU.add).then_inc(*step("dve", "merged"))
                        v.wait_ge(*so_far("dve"))
                v.wait_ge(*at("x_again"))
                for m in range(8):
                    v.wait_ge(*at("tile", start["out"] + m))
                    nc.vector.tensor_tensor(halves(X2[:, m, :]), pair(m % 4), halves(X2[:, m, :]), ALU.add).then_inc(*step("dve", "x2", m))

            def pool(p):
                p.dma_start(X2r, io["x"]).then_inc(*moved("x_again"))

        SQ2t = tiles(SQ2, KT)
        a = 2 * KT * TOK + 4 * TOK + KT * TOK
        Hr = take(FT * TOK)
        H = tiles(Hr, FT)
        SGF = [region(0, TOK), region(TOK, TOK)]
        YF = tiles(SQ2, KT)

        class Ffn:
            def pe(pe):
                norm_pe(pe, "norm2", SQ2t)
                pe.wait_ge(*at("norm2", "out"))
                for i in range(FT):
                    g = start["up"] + 2 * i
                    if i >= 2:
                        pe.wait_ge(*at("up_sig", i - 2))
                        pe.wait_ge(*at("h", i - 2))
                    product(pe, g, i % 2, XN)
                    product(pe, g + 1, 2 + i % 2, XN)
                pe.wait_ge(*at("h", FT - 1))
                for m in range(8):
                    g = start["down"] + 3 * m
                    if m >= 4:
                        pe.wait_ge(*at("x3", m - 4))
                    for i, (k0, k1) in enumerate(((0, 8), (8, 16), (16, 22))):
                        product(pe, g + i, m % 4, H, first=i == 0, last=i == 2, kts=k1 - k0, k0=k0)
                pe.wait_ge(*at("x3", 7))
                norm_pe(pe, "normf", SQ2t)
                pe.wait_ge(*so_far("pe"))

            def act(act):
                norm_act(act, "norm2")
                for i in range(FT):
                    act.wait_ge(*at("tile", start["up"] + 2 * i))
                    if i >= 2:
                        act.wait_ge(*at("h", i - 2))
                    nc.scalar.activation(halves(SGF[i % 2]), pair(i % 2), ACT.Sigmoid).then_inc(*step("act", "up_sig", i))
                norm_act(act, "normf")

            def dve(v):
                norm_dve(v, "norm2", X2, SQ2t, XN, "g2")
                for i in range(FT):
                    v.wait_ge(*at("up_sig", i))
                    nc.vector.tensor_tensor(halves(H[:, i, :]), pair(i % 2), halves(SGF[i % 2]), ALU.mult).then_inc(*step("dve"))
                    v.wait_ge(*so_far("dve"))
                    v.wait_ge(*at("tile", start["up"] + 2 * i + 1))
                    nc.vector.tensor_tensor(halves(H[:, i, :]), pair(2 + i % 2), halves(H[:, i, :]), ALU.mult).then_inc(*step("dve", "h", i))
                for m in range(8):
                    v.wait_ge(*at("tile", start["down"] + 3 * m + 2))
                    nc.vector.tensor_tensor(halves(X2[:, m, :]), pair(m % 4), halves(X2[:, m, :]), ALU.add).then_inc(*step("dve", "x3", m))
                v.wait_ge(*so_far("dve"))
                norm_dve(v, "normf", X2, SQ2t, XN, "gf")

            def pool(p):
                p.wait_ge(*at("normf", "out"))
                p.dma_start(io["o_y"], xn[:, :]).then_inc(*moved("y_out"))
                p.wait_ge(*at("y_out"))

        table = {"norm1": Norm1, "rwkv": Rwkv, "mlstm": Mlstm, "attn": Attn, "sample": Sample, "merge": Merge, "ffn": Ffn}
        order = [table[n] for n in phases]

        block = ctx.enter_context(nc.Block())

        def run(eng, name, programs):
            for i, program in enumerate(programs):
                program(eng)
                meet(eng, name, i)

        LAST = {"norm1": 0, "rwkv": 14, "mlstm": 31, "attn": 41, "sample": 41, "merge": 97, "ffn": len(PIECES)}
        n_tiles = LAST[phases[-1]]

        @block.sync
        def _(sp):
            for g in range(n_tiles):
                if g >= RING:
                    sp.wait_ge(sem("tile_done"), g - RING + 1)
                n = PIECES[g] * 128
                sp.dma_start(ring[:, g % RING * 1024:g % RING * 1024 + n], io["w"][g, :, 0:n]).then_inc(
                    *moved("weights", g, lane=g % RING))

        @block.tensor
        def _(eng):
            run(eng, "pe", [phase.pe for phase in order])

        @block.scalar
        def _(eng):
            run(eng, "act", [phase.act for phase in order])

        @block.vector
        def _(eng):
            run(eng, "dve", [phase.dve for phase in order])

        @block.gpsimd
        def _(eng):
            run(eng, "pool", [phase.pool for phase in order])

        return counts.found


OUTS = {"o_y": (128, KT * TOK), "o_kv": (128, 6 * TOK), "o_winp": (NS, 2, 128, 512),
        "o_conv": (128, 8 * 3 * (1 + NS)), "o_pC": (128, MH * 128), "o_pn": (128, MH), "o_pm": (4, 1),
        "o_sC": (128, NS * MH * 128), "o_sn": (128, MH * NS), "o_sm": (4, NS),
        "o_shift": (128, 14 * (1 + NS)), "o_pS": (128, 256), "o_sS": (128, 2048)}


def pack(i):
    f = np.float32
    A = {k: np.asarray(v) for k, v in i.items()}

    def per_feature(v):
        v = v.reshape(-1, v.shape[-1] // 128, 128)
        return v.transpose(2, 1, 0).reshape(128, -1)

    w_in = A["w_in"][0]
    sizes = (1024, 512, 512, 8, 512, 768, 24, 1792, 3072)
    at = np.concatenate([[0], np.cumsum(sizes)])
    m_qk, m_v, m_o, m_if, a_q, a_kv, a_g, r_c, mer = (w_in[:, at[n]:at[n + 1]] for n in range(9))
    small = np.zeros((D, 128), f)
    small[:, 0:24], small[:, 32:36], small[:, 64:68] = a_g, m_if[:, 0:4], m_if[:, 4:8]
    q = a_q.reshape(D, 2, 4, 64).transpose(0, 2, 1, 3).reshape(D, 512)
    tiles = []

    def add(w):
        k, n = w.shape[0] // 128, w.shape[1] // 128
        t = np.zeros((n, 128, 8, 128), f)
        t[:, :, 0:k] = w.reshape(k, 128, n, 128).transpose(2, 1, 0, 3)
        tiles.append(t)

    for w in (r_c, small, m_qk, m_v, m_o, q, a_kv):
        add(w)
    wa = A["w_branch_a"][0].reshape(2, 4, 64, D).transpose(1, 0, 2, 3).reshape(512, D)
    branch = (A["w_branch_m"][0], wa, A["w_branch_r"][0])
    for m in range(8):
        for b in range(3):
            add(mer[:, b * D + m * 128:b * D + m * 128 + 128])
            add(branch[b][:, m * 128:m * 128 + 128])
    add(A["w_out"][0])
    gu = A["w_gate_up"][0]
    for m in range(FT):
        add(gu[:, m * 128:m * 128 + 128])
        add(gu[:, FF + m * 128:FF + m * 128 + 128])
    for m in range(8):
        wd = A["w_down"][0][:, m * 128:m * 128 + 128]
        for a, b in ((0, 8), (8, 16), (16, 22)):
            add(wd[a * 128:b * 128])
    out = {"w": np.concatenate(tiles).reshape(-1, 128, 1024)}
    x = np.concatenate([A["x_prompt"].reshape(T, D), A["x_sample"].reshape(NS, D)])
    out["x"] = per_feature(x)
    out["cn"] = constants()[0]
    out["blocksel"] = block_selector()
    out["prm"] = np.concatenate([per_feature(v) for v in (
        A["norm1_g"], A["norm2_g"], A["final_norm_g"][None], A["rwkv_mu"], A["rwkv_w0"], A["rwkv_a0"], A["rwkv_k_k"],
        A["rwkv_k_a"], A["rwkv_r_k"].reshape(1, 512), A["rwkv_ln_g"], A["rwkv_ln_b"], A["mlstm_conv_w"][0],
        A["mlstm_conv_b"])], 1)
    lora = np.zeros((128, 1024), f)
    lora[0:64, 0:512], lora[64:128, 0:512], lora[:, 512:] = A["rwkv_w2"][0], A["rwkv_a2"][0], A["rwkv_g2"][0]
    out["lora"] = lora
    out["rwkv_shift"] = per_feature(A["state_rwkv_shift"].reshape(NS, 1792))
    s = A["state_rwkv"][0].reshape(NS, 4, 2, 64, 64)
    out["rwkv_state"] = s.transpose(2, 4, 0, 1, 3).reshape(128, 2048)
    cv = A["state_mlstm_conv"][0]
    out["conv"] = cv.reshape(NS, 3, 8, 128).transpose(3, 2, 0, 1).reshape(128, 192)
    out["mC"] = A["state_mlstm_C"][0].transpose(2, 1, 0, 3).reshape(128, NS * MH * 128)
    out["mn"] = A["state_mlstm_n"][0].transpose(2, 1, 0).reshape(128, NS * MH)
    out["mm"] = A["state_mlstm_m"][0].T
    out["ifb"] = A["mlstm_if_bias"][0].T
    def chunked(c):
        c = c[0].reshape(-1, 8, 8, 2, 2, 64)
        return c.transpose(0, 3, 5, 2, 4, 1).reshape(-1, 128, 128)

    keys = A["cache_slc_k"][0].reshape(-1, 128, 128).transpose(0, 2, 1)
    vals = A["cache_slc_v"][0].reshape(-1, 128, 128)
    out["pages"] = np.stack([chunked(A["cache_cmp_k"]), chunked(A["cache_cmp_v"]), keys], 2)
    out["pages_v"] = vals
    out["win"] = np.stack([A["cache_win_k"][0].reshape(NS, 512, 128).transpose(2, 0, 1),
                           A["cache_win_v"][0].reshape(NS, 512, 128).transpose(2, 0, 1)], 2)
    out["win_v"] = A["cache_win_v"][0].reshape(NS, 4, 128, 128).transpose(2, 0, 1, 3)
    out["table"] = A["page_table"].reshape(1, 128)
    w1 = A["nsa_cmp_w1"][0].reshape(2, 2, 8, 2, 64, 64)
    out["w1"] = w1.transpose(3, 4, 0, 1, 2, 5).reshape(128, 2 * 2 * 8 * 64)
    w1 = A["nsa_cmp_w1"][0].reshape(2, 2, 16, 64, 64).transpose(3, 0, 1, 2, 4).reshape(64, 4096)
    out["w1d"] = np.concatenate([w1, w1])
    pe = A["nsa_cmp_pe"][0].reshape(2, 2, 8, 2, 64)
    out["pe"] = pe.transpose(3, 4, 0, 1, 2).reshape(128, 32)
    w2 = A["nsa_cmp_w2"][0].transpose(1, 0, 2).reshape(64, 128)
    out["w2"] = np.concatenate([w2, w2])
    return {k: np.ascontiguousarray(v) for k, v in out.items()}


PHASES = ("norm1", "rwkv", "mlstm", "attn", "sample", "merge", "ffn")


def kernel(**inputs):
    import numpy as _np
    import concourse.bacc as _bacc
    from concourse import mybir as _mybir
    from concourse.bass_utils import run_bass_kernel_spmd as _run

    packed = pack(inputs)
    known = None
    for _ in range(2):
        nc = _bacc.Bacc("TRN2", target_bir_lowering=False, num_devices=1)
        arrays, io = {}, {}
        for name, a in packed.items():
            arrays["in_" + name] = a
            io[name] = nc.dram_tensor("in_" + name, a.shape, _mybir.dt.from_np(a.dtype), kind="ExternalInput").ap()
        for name, shape in OUTS.items():
            io[name] = nc.dram_tensor(name, shape, F32, kind="ExternalOutput").ap()
        known = build(nc, io, known, PHASES)
    o = _run(nc, [arrays], core_ids=[0]).results[0]

    y = o["o_y"].reshape(128, KT, TOK).transpose(2, 1, 0).reshape(TOK, D)
    kv = o["o_kv"].reshape(128, 6, TOK).transpose(1, 2, 0).reshape(6, TOK, 2, 64)
    kvp, kvs = kv[:, :T][:, None, None], kv[:, T:][:, None, :, None]
    winp = o["o_winp"].transpose(1, 0, 3, 2).reshape(2, 1, NS, 512, 2, 64)
    conv = o["o_conv"].reshape(128, 8, 1 + NS, 3).transpose(2, 3, 1, 0).reshape(1 + NS, 3, 1024)
    shift = o["o_shift"].reshape(128, 14, 1 + NS).transpose(2, 1, 0).reshape(1 + NS, 1792)
    pS = o["o_pS"].reshape(2, 64, 4, 64).transpose(2, 0, 3, 1).reshape(1, 1, 8, 64, 64)
    sS = o["o_sS"].reshape(2, 64, NS, 4, 64).transpose(2, 3, 0, 4, 1).reshape(1, NS, 8, 64, 64)
    pC = o["o_pC"].reshape(128, MH, 128).transpose(1, 0, 2)[None, None]
    sC = o["o_sC"].reshape(128, MH, NS, 128).transpose(2, 1, 0, 3)[None]
    sn = o["o_sn"].reshape(128, MH, NS).transpose(2, 1, 0)[None]
    out = (y[None, :T], y[T:, None],
           kvp[0], kvp[1], kvp[2], kvp[3], kvp[4], kvp[5],
           conv[None, 0:1], pC, o["o_pn"].T[None, None], o["o_pm"].reshape(1, 1, 4), shift[0].reshape(1, 1, 1, 1792), pS,
           kvs[0], kvs[1], kvs[2], kvs[3], winp[0], winp[1],
           conv[None, 1:], sC, sn, o["o_sm"].T[None], shift[1:].reshape(1, NS, 1, 1792), sS)
    return tuple(_np.ascontiguousarray(v) for v in out)
```

```python
from contextlib import ExitStack

import concourse.bass as bass
from concourse import mybir
import numpy as np

F32 = mybir.dt.float32
I32 = mybir.dt.int32
ALU = mybir.AluOpType
ACT = mybir.ActivationFunctionType
AX = mybir.AxisListType

D, T, NS = 1024, 512, 8
TOK = T + NS
HALF = TOK // 2
KT = D // 128
MH, MD = 4, 128
NPAGE, PAGE = 16, 128
NBLK = 33
FF = 2816
FT = FF // 128
RMS_EPS, LN_EPS = 1e-6, 64e-5
NEG = -1e30
RING = 4
CH = 64
NC_ = T // CH
SCALE = 64 ** -0.5
KSCALE = MD ** -0.5

N_RWKV, N_MQK, N_MV, N_MO, N_Q, N_KV = 14, 8, 4, 4, 4, 6


def constants():
    p = np.arange(128)
    c = {}
    c["ident"] = np.eye(128)
    c["ones"] = np.ones((128, 128))
    c["bones"] = (p[:, None] // 64 == p[None, :] // 64) * 1.0
    c["id2"] = (p[:, None] % 64 == np.arange(64)[None, :]) * 1.0
    s, t = (p % 64)[:, None], np.arange(64)[None, :]
    c["strict"] = (s < t) * 1.0
    c["upto"] = (s <= t) * 1.0
    c["below"] = (s > t) * 1.0
    c["off1"] = ((s // 2 == t // 2) & (s < t)) * 1.0
    for n in (1, 2, 4, 8, 16, 32):
        c[f"offT{n}"] = ((s // (2 * n) == t // (2 * n)) & (s // n > t // n)) * 1.0
    c["reset"] = np.broadcast_to((np.arange(T) % CH != 0) * 1.0, (128, T))
    c["causal"] = np.where(np.arange(128)[None, :] <= p[:, None], 0.0, NEG)
    c["tri"] = (p[:, None] <= np.arange(128)[None, :]) * 1.0
    q = np.arange(4)[None, :, None] * 128 + p[:, None, None]
    end = np.arange(32)[None, None, :] * 16 + 31
    ok = (end <= q) & (np.arange(32)[None, None, :] < 31)
    c["cmpadd"] = np.where(ok, 0.0, NEG).reshape(128, 128)
    c["cmp01"] = (ok * 1.0).reshape(128, 128)
    n, j = p[:, None], np.arange(NBLK)[None, :]
    c["covers"] = ((n < 4 * j + 4) & (n >= 4 * j - 1) & (n < 127)) * 1.0
    e = np.zeros((128, 4, 128))
    for h in range(4):
        e[h, h] = 1.0
    c["headsel"] = e.reshape(128, 512)
    c["first"] = np.zeros((128, 1))
    c["first"][0] = NEG
    at, cols, out = 0, {}, []
    for k, v in c.items():
        cols[k] = (at, at + v.shape[1])
        at += v.shape[1]
        out.append(v)
    return np.ascontiguousarray(np.concatenate(out, 1).astype(np.float32)), cols


def block_selector():
    e = np.zeros((128, NPAGE, 2, 64))
    for b in range(32):
        e[b, b // 2, b % 2] = 1.0
    return e.reshape(128, 2048)[0:32].astype(np.float32)


PRM = {}
_at = 0
for _n, _w in (("g1", 8), ("g2", 8), ("gf", 8), ("mu", 14), ("w0", 4), ("a0", 4), ("kk", 4), ("ka", 4), ("rk", 4),
               ("lng", 4), ("lnb", 4), ("cw", 32), ("cb", 8)):
    PRM[_n] = (_at, _at + _w)
    _at += _w
NPRM = _at


class Counts:

    def __init__(self, nc, ctx, known):
        self.nc, self.ctx, self.known, self.found, self.sems, self.count = nc, ctx, known, {}, {}, {}

    def sem(self, key):
        if key not in self.sems:
            self.sems[key] = self.ctx.enter_context(self.nc.semaphore(key))
        return self.sems[key]

    def _add(self, key, name, n):
        self.count[key] = self.count.get(key, 0) + n
        if name:
            self.found[name] = (key, self.count[key])
        return self.sem(key), n

    def step(self, engine, *name):
        return self._add(engine + "_steps", name, 1)

    def tile_done(self, g):
        return self._add("tile_done", ("tile", g), 1)

    def moved(self, name, *index, lane=""):
        return self._add(f"moved_{name}{lane}", (name, *index), 16)

    def so_far(self, engine):
        return self.sem(engine + "_steps"), self.count[engine + "_steps"]

    def name_last(self, engine, *name):
        key = engine + "_steps"
        self.found[name] = (key, self.count[key])

    def at(self, *name):
        key, value = self.known[name] if self.known else ("pe_steps", 1)
        return self.sem(key), value


def v3(ap, a):
    return ap.rearrange("p (a n) -> p a n", a=a)


def build(nc, io, known, phases):
    ctx = ExitStack()
    with ctx:
        counts = Counts(nc, ctx, known)
        sem, step, tile_done, moved, so_far, at = (counts.sem, counts.step, counts.tile_done, counts.moved,
                                                   counts.so_far, counts.at)
        _, CC = constants()
        NCN = max(b for _, b in CC.values())

        def sb(name, n, dt=F32):
            return ctx.enter_context(nc.sbuf_tensor(name, [128, n], dt))

        PS = ctx.enter_context(nc.psum_tensor("PS", [128, 8, 512], F32))
        cn = sb("cn", NCN)
        prm = sb("prm", NPRM)
        xn = sb("xn", KT * TOK)
        yr = sb("yr", 4 * TOK)
        ring = sb("ring", RING * 1024)
        rs = sb("rs", TOK)
        arena = sb("arena", 37900)

        def C(name, a=None):
            v = cn[:, CC[name][0]:CC[name][1]]
            return v if a is None else v3(v, a)

        def col(name, i=0):
            a = PRM[name][0] + i
            return prm[:, a:a + 1]

        def region(at, n):
            return arena[:, at:at + n]

        def tiles(ap, n):
            return v3(ap, n)

        def halves(ap):
            return v3(ap, 2)

        def pair(i):
            return PS[:, 2 * i:2 * i + 2, 0:HALF]

        XN = tiles(xn[:, :], KT)
        YR = tiles(yr[:, :], 4)
        id128 = C("ident")

        PIECES = []
        start = {}

        def plan(name, sizes):
            start[name] = len(PIECES)
            PIECES.extend(sizes)

        plan("rwkv", [8] * 14)
        plan("o", [8] * 4)
        plan("qk", [8] * 8)
        plan("small", [8])
        plan("v", [8] * 4)
        plan("attn", [8] * 10)
        plan("early", [8, 4] * 16)
        plan("merge", [8, 4] * 8)
        plan("out", [8] * 8)
        plan("up", [8] * 44)
        plan("down", [8, 8, 6] * 8)

        def weight(g, k):
            s = g % RING
            return ring[:, s * 1024 + k * 128:s * 1024 + (k + 1) * 128]

        def part(pe, g, bank, ks):
            pe.wait_ge(*at("weights", g))
            for k in ks:
                for half in range(2):
                    ins = nc.tensor.matmul(PS[:, 2 * bank + half, 0:HALF], weight(g, k), XN[:, k, half * HALF:(half + 1) * HALF],
                                           start=k == 0, stop=k == KT - 1)
            if KT - 1 in ks:
                ins.then_inc(*tile_done(g))

        def product(pe, g, bank, src, first=True, last=True, kts=8, k0=0):
            pe.wait_ge(*at("weights", g))
            for k in range(kts):
                for half in range(2):
                    ins = nc.tensor.matmul(PS[:, 2 * bank + half, 0:HALF], weight(g, k),
                                           src[:, k0 + k, half * HALF:(half + 1) * HALF],
                                           start=first and k == 0, stop=last and k == kts - 1)
            ins.then_inc(*tile_done(g))

        def meet(eng, name, phase):
            if name + "_steps" in counts.count:
                eng.wait_ge(*so_far(name))
            eng.sem_inc(sem("phase_left"), 1)
            eng.wait_ge(sem("phase_left"), 4 * (phase + 1))

        def bones(pe, src, names, which="bones"):
            for t in range(4):
                for half in range(2):
                    ins = nc.tensor.matmul(PS[:, 2 * t + half, 0:HALF], C(which), src[:, t, half * HALF:(half + 1) * HALF],
                                           start=True, stop=True)
            ins.then_inc(*step("pe", *names))

        ALL8 = PS[:, :, 0:HALF]

        def all8(ap):
            return ap.rearrange("p (t n) -> p t n", t=8)

        X0 = tiles(region(0, KT * TOK), KT)
        SQ = tiles(region(KT * TOK, KT * TOK), KT)

        def norm_pe(pe, tag, sq):
            pe.wait_ge(*at(tag, "squares"))
            for half in range(2):
                ins = nc.tensor.matmul(PS[:, 6 + half, 0:HALF], C("ones"), sq[:, 0, half * HALF:(half + 1) * HALF], start=True, stop=True)
            ins.then_inc(*step("pe", tag, "sum"))

        def squares_act(act, tag, src, sq, tiles_, source=None):
            for k in tiles_:
                if source:
                    act.wait_ge(*at(source, k))
                nc.scalar.activation(sq[:, k, :], src[:, k, :], ACT.Square).then_inc(*step("act", tag, "square", k))

        def root_act(act, tag):
            act.wait_ge(*at(tag, "mean"))
            nc.scalar.activation(rs[:, :], rs[:, :], ACT.Sqrt).then_inc(*step("act", tag, "root"))
            act.wait_ge(*so_far("act"))

        def add_square(v, tag, sq, k):
            v.wait_ge(*at(tag, "square", k))
            if k:
                nc.vector.tensor_tensor(sq[:, 0, :], sq[:, 0, :], sq[:, k, :], ALU.add).then_inc(*step("dve", tag, "squares"))
                v.wait_ge(*so_far("dve"))

        def norm_dve(v, tag, src, dst, gain):
            v.wait_ge(*at(tag, "sum"))
            nc.vector.tensor_scalar(halves(rs[:, :]), pair(3), 1.0 / D, RMS_EPS, ALU.mult, ALU.add).then_inc(*step("dve", tag, "mean"))
            v.wait_ge(*so_far("dve"))
            v.wait_ge(*at(tag, "root"))
            nc.vector.reciprocal(rs[:, :], rs[:, :]).then_inc(*step("dve"))
            v.wait_ge(*so_far("dve"))
            for k in range(KT):
                nc.vector.scalar_tensor_tensor(dst[:, k, :], src[:, k, :], col(gain, k), rs[:, :], ALU.mult, ALU.mult).then_inc(*step("dve", tag, "out", k))
            v.wait_ge(*so_far("dve"))

        def first_product(pe, g, bank, tag):
            for k in range(KT):
                pe.wait_ge(*at(tag, "out", k))
                part(pe, g, bank, range(k, k + 1))

        class Norm1:
            def pe(pe):
                pe.wait_ge(*at("cn"))
                norm_pe(pe, "norm1", SQ)
                first_product(pe, start["rwkv"], 0, "norm1")

            def act(act):
                act.wait_ge(*at("x"))
                squares_act(act, "norm1", X0, SQ, range(KT // 2, KT))
                root_act(act, "norm1")

            def dve(v):
                v.wait_ge(*at("x"))
                v.wait_ge(*at("prm"))
                nc.vector.tensor_tensor(SQ[:, 0:4, :], X0[:, 0:4, :], X0[:, 0:4, :], ALU.mult).then_inc(*step("dve"))
                v.wait_ge(*so_far("dve"))
                v.wait_ge(*at("norm1", "square", KT - 1))
                for n in (4, 2, 1):
                    nc.vector.tensor_tensor(SQ[:, 0:n, :], SQ[:, 0:n, :], SQ[:, n:2 * n, :], ALU.add).then_inc(*step("dve", "norm1", "squares"))
                    v.wait_ge(*so_far("dve"))
                norm_dve(v, "norm1", X0, XN, "g1")

            def pool(p):
                p.dma_start(region(0, KT * TOK), io["x"]).then_inc(*moved("x"))
                p.dma_start(cn[:, :], io["cn"]).then_inc(*moved("cn"))
                p.dma_start(prm[:, :], io["prm"]).then_inc(*moved("prm"))

        a = 0

        def take(n):
            nonlocal a
            a += n
            return region(a - n, n)

        mixed = take(14 * TOK)
        raw = take(14 * (TOK + 1))
        LWr, AAr, KKr, TMPr = take(4 * TOK), take(4 * TOK), take(4 * TOK), take(4 * TOK)
        Gr, BNr = take(4 * TOK), take(4 * TOK)
        AT_KH = a
        KHr, CUMr = take(4 * T), take(4 * T)
        rows = take(3 * 4 * T)
        small_r = take(600)
        MX = tiles(mixed, 14)
        RC = tiles(raw, 14)
        shift = small_r[:, 0:112].rearrange("p (t b) -> p t b", t=14)
        WS = small_r[:, 112:144].rearrange("p (t b) -> p t b", t=4)
        GL = small_r[:, 144:176].rearrange("p (t c) -> p t c", t=4)
        R_, K_, V_ = MX[:, 0:4, :], MX[:, 4:8, :], MX[:, 8:12, :]
        LW, AA, KK, TMP, G, BN = (tiles(r, 4) for r in (LWr, AAr, KKr, TMPr, Gr, BNr))
        w2a2 = rows[:, 0:512]
        g2w = rows[:, 512:1024]
        AR = raw[:, 0:4096].rearrange("p (t c k n) -> p t c k n", t=4, c=NC_, k=2)
        BH = tiles(raw[:, 4096:6144], 4)
        KH, CUM = tiles(KHr, 4), tiles(CUMr, 4)
        CUMc = CUMr.rearrange("p (t c n) -> p t c n", t=4, c=NC_)
        ROW = {n: rows[:, i * 2048:(i + 1) * 2048].rearrange("p (c t n) -> p c t n", c=NC_, t=4) for i, n in enumerate("vbk")}
        big = region(14 * TOK + 14 * (TOK + 1), 8192)
        MB = big[:, 0:4096].rearrange("p (c t k n) -> p c t k n", c=NC_, t=4, k=2)
        MK = big[:, 4096:8192].rearrange("p (c t k n) -> p c t k n", c=NC_, t=4, k=2)
        MTt, TTt, Tt = (mixed[:, i * 2048:(i + 1) * 2048].rearrange("p (g n) -> p g n", g=32) for i in range(3))
        Wt = CUMr.rearrange("p (g n) -> p g n", g=32)
        OFF = MB[:, :, :, 0, :].rearrange("p c t n -> p (c t) n")
        Ssr, SAr, SBr = rows[:, 0:2048], rows[:, 2048:4096], rows[:, 4096:6144]

        def sview(ap):
            return ap.rearrange("p (b t n) -> p b t n", b=NS, t=4)

        def per_bt(ap):
            return ap.rearrange("p t b -> p b t").unsqueeze(3).broadcast_to([128, NS, 4, 64])

        ST = [sb(f"rwkv_state{i}", 256) for i in range(2)]
        XS, US = sb("rwkv_x", 256), sb("rwkv_u", 256)

        def q4(ap):
            return v3(ap, 4)

        BANKS4 = [PS[:, 0:4, :], PS[:, 4:8, :]]

        MOr = raw[:, 4096:4096 + 4 * TOK]
        MO = tiles(MOr, 4)
        QKR = tiles(region(0, 8 * (T + 3)), 8)
        SFULL = region(6144, 8 * NS * 4).rearrange("p (t b j) -> p t b j", t=8, b=NS)
        EARLY_QK = 7

        def qk_evac(t, bank):
            nc.scalar.copy(QKR[:, t, 3:3 + HALF], PS[:, 2 * bank, 0:HALF]).then_inc(*step("act"))
            nc.scalar.copy(QKR[:, t, 3 + HALF:3 + T], PS[:, 2 * bank + 1, 0:T - HALF]).then_inc(*step("act"))
            nc.scalar.copy(SFULL[:, t, :, 3], PS[:, 2 * bank + 1, T - HALF:HALF]).then_inc(*step("act", "qk_evac", t))

        convst = region(6144 + 8 * NS * 4, 192).rearrange("p (t b j) -> p t b j", t=8, b=NS)
        qkr = region(AT_KH, 8 * TOK)
        QK = tiles(qkr, 8)

        def convolve(v, t):
            v.wait_ge(*at("qk_evac", t))
            cw = [col("cw", t * 4 + j) for j in range(4)]
            nc.vector.tensor_scalar(QK[:, t, 0:T], QKR[:, t, 0:T], cw[0], col("cb", t), ALU.mult, ALU.add).then_inc(*step("dve"))
            nc.vector.tensor_scalar(QK[:, t, T:TOK], SFULL[:, t, :, 0], cw[0], col("cb", t), ALU.mult, ALU.add).then_inc(*step("dve"))
            v.wait_ge(*so_far("dve"))
            for j in range(1, 4):
                nc.vector.scalar_tensor_tensor(QK[:, t, 0:T], QKR[:, t, j:j + T], cw[j], QK[:, t, 0:T], ALU.mult, ALU.add).then_inc(*step("dve"))
                nc.vector.scalar_tensor_tensor(QK[:, t, T:TOK], SFULL[:, t, :, j], cw[j], QK[:, t, T:TOK], ALU.mult, ALU.add).then_inc(*step("dve", "convolved", t))
                v.wait_ge(*so_far("dve"))

        def qk_sigmoid(act, t):
            act.wait_ge(*at("convolved", t))
            nc.scalar.activation(QKT[:, t, :], QK[:, t, :], ACT.Sigmoid).then_inc(*step("act", "qk_sig", t))

        def o_evac(act, i, bank):
            act.wait_ge(*at("tile", start["o"] + i))
            nc.scalar.activation(halves(MO[:, i, :]), pair(bank), ACT.Sigmoid).then_inc(*step("act", "o_evac", i))

        class Rwkv:
            def pe(pe):
                for t in range(1, 14):
                    if t >= 3:
                        pe.wait_ge(*at("raw", t - 3))
                    product(pe, start["rwkv"] + t, t % 3, XN)
                for t in (11, 12, 13):
                    pe.wait_ge(*at("raw", t))
                pe.wait_ge(*at("kk_squares"))
                bones(pe, TMP, ("kk_sums",))
                pe.wait_ge(*at("lora"))
                pe.wait_ge(*at("tanh"))
                pe.wait_ge(*at("siggd"))
                for j in range(12):
                    kind, t = j // 4, j % 4
                    if j == 0:
                        pe.wait_ge(*at("kk_max"))
                    if j >= 4:
                        pe.wait_ge(*at("lora_out", j - 4))
                    rows_ = (slice(0, 64), slice(64, 128), slice(0, 128))[kind]
                    w = (w2a2, w2a2, g2w)[kind]
                    src = MX[:, 12 + kind // 2, :]
                    for half in range(2):
                        ins = nc.tensor.matmul(PS[:, 2 * t + half, 0:HALF], w[rows_, t * 128:(t + 1) * 128],
                                               src[rows_, half * HALF:(half + 1) * HALF], start=True, stop=True)
                    ins.then_inc(*step("pe", "lora_ps", j))
                pe.wait_ge(*at("lora_out", 11))
                pe.wait_ge(*at("bonus_terms"))
                bones(pe, TMP, ("bonus_sums",))
                pe.wait_ge(*at("s_sa_terms"))
                for i in range(4):
                    ins = nc.tensor.matmul(PS[:, i, :], C("bones"), SAr[:, i * 512:(i + 1) * 512], start=True, stop=True)
                ins.then_inc(*step("pe", "s_sa"))
                pe.wait_ge(*at("s_v_terms"))
                for i in range(4):
                    ins = nc.tensor.matmul(PS[:, 4 + i, :], C("bones"), SBr[:, i * 512:(i + 1) * 512], start=True, stop=True)
                ins.then_inc(*step("pe", "s_v"))
                pe.wait_ge(*at("s_state"))
                for b in range(NS):
                    for t in range(4):
                        for h in range(2):
                            q = slice(64 * h, 64 * h + 64)
                            ins = nc.tensor.matmul(PS[q, 0, t * 8 + b:t * 8 + b + 1], sview(Ssr)[q, b, t, :],
                                                   R_[q, t, T + b:T + b + 1], start=True, stop=True)
                ins.then_inc(*step("pe", "s_y"))
                for i, src in enumerate((V_, BH, KH)):
                    if i == 1:
                        pe.wait_ge(*at("bk_hat"))
                    for c in range(NC_):
                        n = i * NC_ + c
                        bank = 1 + n // 2 % 4
                        if n % 2 == 0 and n >= 8:
                            pe.wait_ge(*at("row", n // 2 - 4))
                        for t in range(4):
                            for h in range(2):
                                q = slice(64 * h, 64 * h + 64)
                                ins = nc.tensor.matmul(PS[q, bank, (n % 2) * 256 + t * 64:(n % 2) * 256 + t * 64 + 64],
                                                       src[q, t, c * CH:(c + 1) * CH], C("id2")[q, :], start=True, stop=True)
                        if n % 2:
                            ins.then_inc(*step("pe", "row_ps", n // 2))
                pe.wait_ge(*at("hats"))
                pe.wait_ge(*at("row", 10))
                pe.wait_ge(*at("row", 11))
                for c in range(NC_):
                    o = 4 * (c % 2)
                    if c >= 2:
                        pe.wait_ge(*at("chunk_m", c - 2))
                    for t in range(4):
                        for h in range(2):
                            q = slice(64 * h, 64 * h + 64)
                            ar = AR[q, t, c, :, :].rearrange("p k n -> p (k n)")
                            cc = slice(c * CH, (c + 1) * CH)
                            nc.tensor.matmul(PS[q, o, t * 128:(t + 1) * 128], BH[q, t, cc], ar, start=True, stop=True)
                            nc.tensor.matmul(PS[q, o + 1, t * 128:(t + 1) * 128], KH[q, t, cc], ar, start=True, stop=True)
                            ins = nc.tensor.matmul(PS[q, o + 2, t * 64:(t + 1) * 64], AR[q, t, c, 0, :], BH[q, t, cc], start=True, stop=True)
                    ins.then_inc(*step("pe", "chunk_ps", c))
                pe.wait_ge(*at("chunk_m", NC_ - 2))
                for i, bank in enumerate((0, 1, 0)):
                    if i == 2:
                        pe.wait_ge(*at("o_evac", 0))
                    product(pe, start["o"] + i, bank, XN)
                HALF_G = (range(0, 16), range(16, 32))
                for l in range(5):
                    pe.wait_ge(*at("off", l))
                    for x in range(2):
                        if l:
                            pe.wait_ge(*at("tt", l - 1, x))
                        else:
                            pe.wait_ge(*at("chunk_m", NC_ - 1))
                        for g in HALF_G[x]:
                            for h in range(2):
                                q = slice(64 * h, 64 * h + 64)
                                ins = nc.tensor.matmul(PS[q, 4 + g // 8, g % 8 * 64:g % 8 * 64 + 64], OFF[q, g, :], Tt[q, g, :], start=True, stop=True)
                        ins.then_inc(*step("pe", "w_ps", l, x))
                    for x in range(2):
                        pe.wait_ge(*at("w", l, x))
                        if l:
                            pe.wait_ge(*at("t", l - 1, x))
                        else:
                            for i in (1, 2):
                                pe.wait_ge(*at("o_evac", i))
                        for g in HALF_G[x]:
                            for h in range(2):
                                q = slice(64 * h, 64 * h + 64)
                                nc.tensor.matmul(PS[q, 4 + g // 8, g % 8 * 64:g % 8 * 64 + 64], TTt[q, g, :], Wt[q, g, :], start=True, stop=True)
                                ins = nc.tensor.matmul(PS[q, g // 8, g % 8 * 64:g % 8 * 64 + 64], Wt[q, g, :], TTt[q, g, :], start=True, stop=True)
                        ins.then_inc(*step("pe", "t_ps", l, x))
                pe.wait_ge(*at("tt", 4, 0))
                product(pe, start["o"] + 3, 2, XN)
                for x in range(2):
                    pe.wait_ge(*at("t", 4, x))
                for c in range(NC_):
                    pe.wait_ge(*at("st", c))
                    S = q4(ST[c % 2][:, :])
                    for t in range(4):
                        for h in range(2):
                            q = slice(64 * h, 64 * h + 64)
                            n = slice(t * 64, t * 64 + 64)
                            nc.tensor.matmul(PS[q, 0, n], AR[q, t, c, 0, :], S[q, t, :], start=True, stop=False)
                            ins = nc.tensor.matmul(PS[q, 0, n], MK[q, c, t, 0, :], ROW["v"][q, c, t, :], start=False, stop=True)
                    ins.then_inc(*step("pe", "x_ps", c))
                    if c < EARLY_QK:
                        pe.wait_ge(*(at("o_evac", 3) if c < 2 else at("qk_evac", c - 2)))
                        part(pe, start["qk"] + c, 2 + c % 2, range(0, 4))
                    pe.wait_ge(*at("x_sb", c))
                    for t in range(4):
                        for h in range(2):
                            q = slice(64 * h, 64 * h + 64)
                            n = slice(t * 64, t * 64 + 64)
                            ins = nc.tensor.matmul(PS[q, 1, n], Tt[q, c * 4 + t, :], q4(XS[:, :])[q, t, :], start=True, stop=True)
                    ins.then_inc(*step("pe", "u_ps", c))
                    if c < EARLY_QK:
                        part(pe, start["qk"] + c, 2 + c % 2, range(4, 8))
                    pe.wait_ge(*at("u_sb", c))
                    U = q4(US[:, :])
                    for t in range(4):
                        for h in range(2):
                            q = slice(64 * h, 64 * h + 64)
                            n = slice(t * 64, t * 64 + 64)
                            nc.tensor.matmul(PS[q, 3, n], ROW["b"][q, c, t, :], U[q, t, :], start=True, stop=False)
                            ins = nc.tensor.matmul(PS[q, 3, n], ROW["k"][q, c, t, :], ROW["v"][q, c, t, :], start=False, stop=True)
                    ins.then_inc(*step("pe", "s_ps", c))
                    if c >= 1:
                        pe.wait_ge(*at("y_sb", c - 1))
                    for t in range(4):
                        for h in range(2):
                            q = slice(64 * h, 64 * h + 64)
                            n = slice(t * 64, t * 64 + 64)
                            nc.tensor.matmul(PS[q, 2, n], S[q, t, :], AR[q, t, c, 1, :], start=True, stop=False)
                            nc.tensor.matmul(PS[q, 2, n], U[q, t, :], MB[q, c, t, 1, :], start=False, stop=False)
                            ins = nc.tensor.matmul(PS[q, 2, n], ROW["v"][q, c, t, :], MK[q, c, t, 1, :], start=False, stop=True)
                    ins.then_inc(*step("pe", "y_ps", c))
                pe.wait_ge(*at("y_sb", NC_ - 1))
                pe.wait_ge(*at("st", NC_))
                bones(pe, YR, ("y_sums",))
                pe.wait_ge(*at("y_squares"))
                bones(pe, TMP, ("y_square_sums",))
                pe.wait_ge(*at("y_var"))
                for n, g in enumerate(LATE):
                    if n >= 3:
                        pe.wait_ge(*at("m_evac", n - 3))
                    product(pe, g, n % 3, XN)
                pe.wait_ge(*so_far("pe"))

            def act(act):
                for t in range(14):
                    act.wait_ge(*at("tile", start["rwkv"] + t))
                    nc.scalar.copy(halves(RC[:, t, 1:TOK + 1]), pair(t % 3)).then_inc(*step("act", "raw", t))
                act.wait_ge(*at("mixed", 13))
                nc.scalar.activation(MX[0:64, 12, :], MX[0:64, 12, :], ACT.Tanh).then_inc(*step("act", "tanh"))
                act.wait_ge(*so_far("act"))
                nc.scalar.activation(MX[:, 13, :], MX[:, 13, :], ACT.Sigmoid).then_inc(*step("act", "siggd"))
                act.wait_ge(*so_far("act"))
                act.wait_ge(*at("kk_max"))
                nc.scalar.activation(TMPr, TMPr, ACT.Sqrt).then_inc(*step("act", "kk_root"))
                act.wait_ge(*so_far("act"))
                for j in range(8):
                    act.wait_ge(*at("lora_ps", j))
                    kind, t = j // 4, j % 4
                    nc.scalar.activation(halves((LW, AA)[kind][:, t, :]), pair(t), ACT.Sigmoid,
                                                  bias=col(("w0", "a0")[kind], t)).then_inc(*step("act", "lora_out", j))
                for t in range(4):
                    act.wait_ge(*at("lora_ps", 8 + t))
                    nc.scalar.copy(halves(G[:, t, :]), pair(t)).then_inc(*step("act", "lora_out", 8 + t))
                nc.scalar.activation(LWr, LWr, ACT.Copy, scale=-float(np.exp(-0.5))).then_inc(*step("act", "lw"))
                act.wait_ge(*so_far("act"))
                nc.scalar.activation(WS, LW[:, :, T:TOK], ACT.Exp).then_inc(*step("act", "ws"))
                act.wait_ge(*at("cum"))
                act.wait_ge(*at("shift_out"))
                nc.scalar.activation(BH, CUM, ACT.Exp, scale=-1.0).then_inc(*step("act", "e_inv"))
                act.wait_ge(*at("cum_prev"))
                nc.scalar.activation(TMP[:, :, 0:T], TMP[:, :, 0:T], ACT.Exp).then_inc(*step("act", "e_prev"))
                act.wait_ge(*so_far("act"))
                nc.scalar.activation(LW[:, :, 0:T], CUM, ACT.Exp).then_inc(*step("act", "e_cum"))
                act.wait_ge(*so_far("act"))
                act.wait_ge(*at("s_state_out"))
                for i in range(12):
                    if i % 2:
                        act.wait_ge(*at("row_ps", i))
                        r = ROW["vbk"[i // 4]][:, 2 * (i % 4):2 * (i % 4) + 2, :, :].rearrange("p c t n -> p (c t n)")
                        nc.scalar.copy(r, PS[:, 1 + i % 4, :]).then_inc(*step("act", "row", i))
                for i, bank in enumerate((0, 1, 0)):
                    o_evac(act, i, bank)
                for l in range(5):
                    for x in range(2):
                        act.wait_ge(*at("w_ps", l, x))
                        nc.scalar.copy(Wt[:, 16 * x:16 * x + 16, :].rearrange("p g n -> p (g n)").rearrange("p (a n) -> p a n", a=2),
                                       PS[:, 4 + 2 * x:6 + 2 * x, :]).then_inc(*step("act", "w", l, x))
                act.wait_ge(*so_far("act"))
                o_evac(act, 3, 2)
                for c in range(NC_):
                    act.wait_ge(*at("u_ps", c))
                    if c >= 1:
                        act.wait_ge(*at("y_ps", c - 1))
                    nc.scalar.copy(US[:, :], PS[:, 1, 0:256]).then_inc(*step("act", "u_sb", c))
                    act.wait_ge(*at("y_ps", c))
                    nc.scalar.copy(YR[:, :, c * CH:(c + 1) * CH], q4(PS[:, 2, 0:256])).then_inc(*step("act", "y_sb", c))
                    if c < EARLY_QK:
                        act.wait_ge(*at("tile", start["qk"] + c))
                        act.wait_ge(*at("t_ps", 4, 1))
                        qk_evac(c, 2 + c % 2)
                act.wait_ge(*at("y_var"))
                nc.scalar.activation(TMPr, TMPr, ACT.Sqrt).then_inc(*step("act", "y_root"))
                act.wait_ge(*so_far("act"))
                act.wait_ge(*at("ifb"))
                for n, g in enumerate(LATE):
                    act.wait_ge(*at("tile", g))
                    if n < GATES:
                        qk_evac(EARLY_QK + n, n % 3)
                    elif n == GATES:
                        b = 2 * (n % 3)
                        nc.scalar.activation(halves(g24[0:24, :]), PS[0:24, b:b + 2, 0:HALF], ACT.Sigmoid).then_inc(*step("act", "g24"))
                        nc.scalar.activation(halves(LI[0:4, :]), PS[32:36, b:b + 2, 0:HALF], ACT.Identity, bias=ifb[0:4, 0:1]).then_inc(*step("act"))
                        nc.scalar.activation(halves(LF[0:4, :]), PS[64:68, b:b + 2, 0:HALF], ACT.Identity, bias=ifb[0:4, 1:2]).then_inc(*step("act"))
                    else:
                        nc.scalar.copy(halves(MV[:, n - GATES - 1, :]), pair(n % 3)).then_inc(*step("act"))
                    counts.name_last("act", "m_evac", n)
                    if n > GATES:
                        act.wait_ge(*so_far("act"))
                        for t in range(2 * (n - GATES - 1), min(2 * (n - GATES), EARLY_QK)):
                            qk_sigmoid(act, t)

            def dve(v):
                v.wait_ge(*at("shift"))
                v.wait_ge(*at("zero_col"))
                for t in range(14):
                    v.wait_ge(*at("raw", t))
                    nc.vector.tensor_tensor(MX[:, t, 0:T], RC[:, t, 0:T], RC[:, t, 1:T + 1], ALU.subtract).then_inc(*step("dve"))
                    nc.vector.tensor_tensor(MX[:, t, T:TOK], shift[:, t, :], RC[:, t, T + 1:TOK + 1], ALU.subtract).then_inc(*step("dve"))
                    v.wait_ge(*so_far("dve"))
                    nc.vector.scalar_tensor_tensor(MX[:, t, :], MX[:, t, :], col("mu", t), RC[:, t, 1:TOK + 1], ALU.mult, ALU.add).then_inc(*step("dve", "mixed", t))
                v.wait_ge(*so_far("dve"))
                for t in range(4):
                    nc.vector.tensor_scalar(KK[:, t, :], K_[:, t, :], col("kk", t), None, ALU.mult).then_inc(*step("dve"))
                v.wait_ge(*so_far("dve"))
                nc.vector.tensor_tensor(TMPr, KKr, KKr, ALU.mult).then_inc(*step("dve", "kk_squares"))
                v.wait_ge(*so_far("dve"))
                v.wait_ge(*at("kk_sums"))
                nc.vector.tensor_scalar(all8(TMPr), ALL8, 1e-24, None, ALU.max).then_inc(*step("dve", "kk_max"))
                v.wait_ge(*so_far("dve"))
                v.wait_ge(*at("kk_root"))
                nc.vector.reciprocal(TMPr, TMPr).then_inc(*step("dve"))
                v.wait_ge(*so_far("dve"))
                nc.vector.tensor_tensor(KKr, KKr, TMPr, ALU.mult).then_inc(*step("dve"))
                v.wait_ge(*so_far("dve"))
                for t in range(4):
                    v.wait_ge(*at("lora_out", 4 + t))
                    nc.vector.tensor_scalar(TMP[:, t, :], AA[:, t, :], 1.0, col("ka", t), ALU.subtract, ALU.mult).then_inc(*step("dve"))
                v.wait_ge(*so_far("dve"))
                nc.vector.scalar_tensor_tensor(K_, TMP, 1.0, K_, ALU.add, ALU.mult).then_inc(*step("dve"))
                v.wait_ge(*so_far("dve"))
                for t in range(4):
                    nc.vector.scalar_tensor_tensor(TMP[:, t, :], R_[:, t, :], col("rk", t), K_[:, t, :], ALU.mult, ALU.mult).then_inc(*step("dve", "bonus_terms"))
                v.wait_ge(*at("bonus_sums"))
                nc.vector.tensor_tensor(all8(BNr), ALL8, all8(mixed[:, 8 * TOK:12 * TOK]), ALU.mult).then_inc(*step("dve", "bonus"))
                v.wait_ge(*so_far("dve"))
                nc.vector.tensor_tensor(AAr, AAr, KKr, ALU.mult).then_inc(*step("dve"))
                v.wait_ge(*so_far("dve"))
                v.wait_ge(*at("s_rwkv"))
                nc.vector.tensor_tensor(sview(SAr), sview(Ssr), per_bt(KK[:, :, T:TOK]), ALU.mult).then_inc(*step("dve", "s_sa_terms"))
                v.wait_ge(*so_far("dve"))
                nc.vector.tensor_tensor(sview(SBr), C("id2").unsqueeze(1).unsqueeze(1).broadcast_to([128, NS, 4, 64]),
                                               per_bt(V_[:, :, T:TOK]), ALU.mult).then_inc(*step("dve", "s_v_terms"))
                v.wait_ge(*so_far("dve"))
                v.wait_ge(*at("ws"))
                nc.vector.tensor_tensor(sview(Ssr), sview(Ssr), per_bt(WS), ALU.mult).then_inc(*step("dve"))
                v.wait_ge(*so_far("dve"))
                v.wait_ge(*at("s_sa"))
                nc.vector.tensor_tensor(sview(SAr), BANKS4[0].rearrange("p a n -> p (a n)").rearrange("p (b t n) -> p b t n", b=NS, t=4),
                                               per_bt(AA[:, :, T:TOK]), ALU.mult).then_inc(*step("dve"))
                v.wait_ge(*so_far("dve"))
                nc.vector.tensor_tensor(Ssr, Ssr, SAr, ALU.subtract).then_inc(*step("dve"))
                v.wait_ge(*so_far("dve"))
                v.wait_ge(*at("s_v"))
                nc.vector.tensor_tensor(sview(SBr), BANKS4[1].rearrange("p a n -> p (a n)").rearrange("p (b t n) -> p b t n", b=NS, t=4),
                                               per_bt(K_[:, :, T:TOK]), ALU.mult).then_inc(*step("dve"))
                v.wait_ge(*so_far("dve"))
                nc.vector.tensor_tensor(Ssr, Ssr, SBr, ALU.add).then_inc(*step("dve", "s_state"))
                v.wait_ge(*so_far("dve"))
                v.wait_ge(*at("lw"))
                for t in range(4):
                    nc.vector.tensor_tensor_scan(CUM[:, t, :], C("reset"), LW[:, t, 0:T], 0.0, ALU.mult, ALU.add).then_inc(*step("dve", "cum"))
                v.wait_ge(*so_far("dve"))
                nc.vector.tensor_tensor(TMP[:, :, 0:T], CUM, LW[:, :, 0:T], ALU.subtract).then_inc(*step("dve", "cum_prev"))
                v.wait_ge(*so_far("dve"))
                v.wait_ge(*at("e_inv"))
                nc.vector.tensor_tensor(KH, K_[:, :, 0:T], BH, ALU.mult).then_inc(*step("dve"))
                v.wait_ge(*so_far("dve"))
                nc.vector.tensor_tensor(BH, AA[:, :, 0:T], BH, ALU.mult).then_inc(*step("dve", "bk_hat"))
                v.wait_ge(*at("e_prev"))
                v.wait_ge(*at("shift_out"))
                for t in range(4):
                    nc.vector.scalar_tensor_tensor(AR[:, t, :, 0, :], KK[:, t, 0:T].rearrange("p (c n) -> p c n", c=NC_), -1.0,
                                                          TMP[:, t, 0:T].rearrange("p (c n) -> p c n", c=NC_), ALU.mult, ALU.mult).then_inc(*step("dve"))
                v.wait_ge(*at("e_cum"))
                for t in range(4):
                    nc.vector.tensor_tensor(AR[:, t, :, 1, :], R_[:, t, 0:T].rearrange("p (c n) -> p c n", c=NC_),
                                                   LW[:, t, 0:T].rearrange("p (c n) -> p c n", c=NC_), ALU.mult).then_inc(*step("dve"))
                nc.vector.tensor_copy(GL, LW[:, :, CH - 1:T:CH]).then_inc(*step("dve", "hats"))
                v.wait_ge(*at("s_y"))
                nc.vector.tensor_copy(YR[:, :, T:TOK], PS[:, 0, 0:32].rearrange("p (t b) -> p t b", t=4)).then_inc(*step("dve"))
                v.wait_ge(*at("s_state_out"))
                for i in range(0, 12, 2):
                    v.wait_ge(*at("row_ps", i))
                    r = ROW["vbk"[i // 4]][:, 2 * (i % 4):2 * (i % 4) + 2, :, :].rearrange("p c t n -> p (c t n)")
                    nc.vector.tensor_copy(r, PS[:, 1 + i % 4, :]).then_inc(*step("dve", "row", i))
                v.wait_ge(*at("row", 11))
                v.wait_ge(*so_far("dve"))
                strict = C("strict").unsqueeze(1).broadcast_to([128, 4, 64])
                upto = C("upto").unsqueeze(1).broadcast_to([128, 4, 64])
                below = C("below").unsqueeze(1).broadcast_to([128, 4, 64])
                for c in range(NC_):
                    v.wait_ge(*at("chunk_ps", c))
                    o = 4 * (c % 2)
                    for m, (dst, bank) in enumerate(((MB, o), (MK, o + 1))):
                        ps = PS[:, bank, :].rearrange("p (t k n) -> p t k n", t=4, k=2)
                        nc.vector.tensor_tensor(dst[:, c, :, 0, :], ps[:, :, 0, :], strict, ALU.mult).then_inc(*step("dve"))
                        nc.vector.tensor_tensor(dst[:, c, :, 1, :], ps[:, :, 1, :], upto, ALU.mult).then_inc(*step("dve"))
                    nc.vector.tensor_tensor(MTt[:, 4 * c:4 * c + 4, :], q4(PS[:, o + 2, 0:256]), below, ALU.mult).then_inc(*step("dve", "chunk_m", c))
                v.wait_ge(*so_far("dve"))

                def wide(name):
                    return C(name).unsqueeze(1).broadcast_to([128, 32, 64])

                nc.vector.tensor_tensor(Tt, OFF, wide("off1"), ALU.mult).then_inc(*step("dve"))
                nc.vector.tensor_tensor(TTt, MTt, wide("offT1"), ALU.mult).then_inc(*step("dve"))
                v.wait_ge(*so_far("dve"))
                nc.vector.tensor_tensor(Tt, Tt, wide("id2"), ALU.add).then_inc(*step("dve"))
                nc.vector.tensor_tensor(TTt, TTt, wide("id2"), ALU.add).then_inc(*step("dve"))
                nc.vector.tensor_tensor(OFF, MTt, wide("offT2"), ALU.mult).then_inc(*step("dve", "off", 0))
                v.wait_ge(*so_far("dve"))
                for l in range(5):
                    if l < 4:
                        v.wait_ge(*at("w_ps", l, 1))
                        nc.vector.tensor_tensor(OFF, MTt, wide(f"offT{4 << l}"), ALU.mult).then_inc(*step("dve", "off", l + 1))
                    for x in range(2):
                        v.wait_ge(*at("t_ps", l, x))
                        g = slice(16 * x, 16 * x + 16)
                        for name, dst, bank in (("tt", Tt, 4), ("t", TTt, 0)):
                            ps = PS[:, bank + 2 * x:bank + 2 * x + 2, :].rearrange("p a n -> p (a n)").rearrange("p (g n) -> p g n", g=16)
                            nc.vector.tensor_tensor(dst[:, g, :], ps, dst[:, g, :], ALU.add).then_inc(*step("dve", name, l, x))
                    v.wait_ge(*so_far("dve"))
                nc.vector.memset(ST[0][:, :], 0.0).then_inc(*step("dve", "st", 0))
                v.wait_ge(*so_far("dve"))
                for c in range(NC_):
                    v.wait_ge(*at("x_ps", c))
                    nc.vector.tensor_copy(XS[:, :], PS[:, 0, 0:256]).then_inc(*step("dve", "x_sb", c))
                    if 1 <= c <= EARLY_QK:
                        if c == 1:
                            v.wait_ge(*at("zero_cols"))
                            v.wait_ge(*at("m_conv_in"))
                        convolve(v, c - 1)
                    v.wait_ge(*at("s_ps", c))
                    if c >= 1:
                        v.wait_ge(*at("y_ps", c - 1))
                    nxt = ST[(c + 1) % 2]
                    nc.vector.tensor_tensor(nxt[:, :], PS[:, 3, 0:256], ST[c % 2][:, :], ALU.add).then_inc(*step("dve"))
                    v.wait_ge(*so_far("dve"))
                    nc.vector.tensor_tensor(q4(nxt[:, :]), q4(nxt[:, :]), GL[:, :, c:c + 1].broadcast_to([128, 4, 64]), ALU.mult).then_inc(*step("dve", "st", c + 1))
                    v.wait_ge(*so_far("dve"))
                v.wait_ge(*at("y_sums"))
                nc.vector.scalar_tensor_tensor(all8(yr[:, :]), ALL8, -1.0 / 64, all8(yr[:, :]), ALU.mult, ALU.add).then_inc(*step("dve"))
                v.wait_ge(*so_far("dve"))
                nc.vector.tensor_tensor(TMPr, yr[:, :], yr[:, :], ALU.mult).then_inc(*step("dve", "y_squares"))
                v.wait_ge(*so_far("dve"))
                v.wait_ge(*at("y_square_sums"))
                nc.vector.tensor_scalar(all8(TMPr), ALL8, 1.0 / 64, LN_EPS, ALU.mult, ALU.add).then_inc(*step("dve", "y_var"))
                v.wait_ge(*so_far("dve"))
                v.wait_ge(*at("y_root"))
                nc.vector.reciprocal(TMPr, TMPr).then_inc(*step("dve"))
                v.wait_ge(*so_far("dve"))
                nc.vector.tensor_tensor(yr[:, :], yr[:, :], TMPr, ALU.mult).then_inc(*step("dve"))
                v.wait_ge(*so_far("dve"))
                for t in range(4):
                    nc.vector.tensor_scalar(YR[:, t, :], YR[:, t, :], col("lng", t), col("lnb", t), ALU.mult, ALU.add).then_inc(*step("dve"))
                v.wait_ge(*so_far("dve"))
                nc.vector.tensor_tensor(yr[:, :], yr[:, :], BNr, ALU.add).then_inc(*step("dve"))
                v.wait_ge(*so_far("dve"))
                nc.vector.tensor_tensor(yr[:, :], yr[:, :], Gr, ALU.mult).then_inc(*step("dve", "yr"))
                v.wait_ge(*so_far("dve"))

            def pool(p):
                nc.gpsimd.memset(RC[:, :, 0:1], 0.0).then_inc(*step("pool", "zero_col"))
                p.dma_start(small_r[:, 0:112], io["rwkv_shift"]).then_inc(*moved("shift"))
                p.dma_start(rows[:, 0:1024], io["lora"]).then_inc(*moved("lora"))
                p.wait_ge(*at("raw", 13))
                p.dma_start(io["o_shift"].rearrange("p (t b) -> p t b", t=14), RC[:, :, T:TOK + 1]).then_inc(*moved("shift_out"))
                p.wait_ge(*at("lora_ps", 11))
                p.dma_start(Ssr, io["rwkv_state"]).then_inc(*moved("s_rwkv"))
                p.wait_ge(*at("s_state"))
                p.dma_start(io["o_sS"], Ssr).then_inc(*moved("s_state_out"))
                p.wait_ge(*at("t", 4, 1))
                p.wait_ge(*at("t_ps", 4, 1))
                nc.gpsimd.memset(QKR[:, 0:EARLY_QK, 0:3], 0.0).then_inc(*step("pool", "zero_cols"))
                p.dma_start(ifb[0:4, :], io["ifb"]).then_inc(*moved("ifb"))
                p.dma_start(convst.rearrange("p t b j -> p (t b j)")[:, 0:192], io["conv"]).then_inc(*moved("conv_in"))
                p.wait_ge(*at("conv_in"))
                nc.gpsimd.tensor_copy(SFULL[:, :, :, 0:3], convst).then_inc(*step("pool", "m_conv_in"))
                p.wait_ge(*at("st", NC_))
                p.wait_ge(*at("y_ps", NC_ - 1))
                nc.gpsimd.memset(QKR[:, EARLY_QK:8, 0:3], 0.0).then_inc(*step("pool", "zero_last_cols"))
                p.dma_start(io["o_pS"], ST[NC_ % 2][:, :]).then_inc(*moved("p_state_out"))
                for n in ("shift_out", "s_state_out", "p_state_out"):
                    p.wait_ge(*at(n))

        TOP = 37900
        ym, Qr, g24 = region(TOP - 2080, 2080), region(TOP - 4160, 2080), region(TOP - 4680, TOK)
        ya = region(0, 2080)
        Q = tiles(Qr, 4)

        YM, YA = tiles(ym, 4), tiles(ya, 4)
        a = 0
        qkraw = take(8 * (T + 3))
        LI, LF, GA = take(TOK), take(TOK), take(TOK)
        assert a <= 6144
        a = 6144 + 8 * NS * 4
        a += 192
        convout = take(8 * 3 * (1 + NS)).rearrange("p (t b j) -> p t b j", t=8, b=1 + NS)
        ifb = region(7200, 2)
        qkt = take(8 * TOK)
        QKT = tiles(qkt, 8)
        assert a <= 14 * TOK + 4096
        a = 14 * TOK + 4096 + 4 * TOK
        MVr = take(4 * TOK)
        MV = tiles(MVr, 4)
        VROW = take(2048).rearrange("p (s h v) -> p s h v", s=4, h=MH)
        KROW = take(2048).rearrange("p (s h v) -> p s h v", s=4, h=MH)
        ATT = take(2 * 512)
        NMB, EMB = take(512), take(512)
        GB = take(TOK)
        CUMF, UU, MM, MS = take(T), take(T), take(T), take(T)
        UT = take(16).rearrange("p (s h) -> p s h", s=4)
        WEND = take(16).rearrange("p (s h) -> p s h", s=4)
        pC, pn = take(512), take(4)
        m0, mp, cs, wi = take(NS), take(NS), take(NS), take(NS)
        DGs = take(96)
        BC = take(96)
        SN, KW, QN = take(32), take(32), take(64)
        rD = take(512)
        HS = take(32)
        assert a <= AT_KH and AT_KH + 8 * TOK <= TOP - 4680
        SC = qkraw[:, 0:4096]
        VD = qkt[:, 0:4096]
        SC4 = v3(SC, 32)
        VD4 = v3(VD, 32)


        LATE = range(start["qk"] + EARLY_QK, start["v"] + 4)
        GATES = 8 - EARLY_QK

        class Mlstm:
            def pe(pe):
                for i in range(8):
                    src, h0 = (MV, 0) if i < 4 else (QK, 4)
                    st = i % 4
                    if i >= 4:
                        pe.wait_ge(*at("qk", 7))
                        pe.wait_ge(*at("m_row", i - 4))
                    for h in range(MH):
                        ins = nc.tensor.transpose(PS[:, i % 4, h * 128:(h + 1) * 128], src[:, h0 + h, st * 128:(st + 1) * 128], id128)
                    ins.then_inc(*step("pe", "m_row_ps", i))
                pe.wait_ge(*at("m_rows"))
                for st in range(4):
                    ins = nc.tensor.transpose(PS[:, 6, st * 4:st * 4 + 4], UU[0:4, st * 128:(st + 1) * 128], id128[0:4, 0:4])
                ins.then_inc(*step("pe", "ut_ps"))

                def q_k(h, st):
                    n = h * 4 + st
                    if n >= 2:
                        pe.wait_ge(*at("att_done", n - 2))
                    ins = nc.tensor.matmul(PS[:, n % 2, 0:T - st * 128], QK[:, 4 + h, st * 128:(st + 1) * 128], QK[:, h, st * 128:T],
                                           start=True, stop=True)
                    ins.then_inc(*step("pe", "att_ps", n))

                n = 0
                for h in range(MH):
                    if h == 0:
                        pe.wait_ge(*at("m_row", 6))
                        pe.wait_ge(*at("m_row", 7))
                        pe.wait_ge(*at("ut"))
                    else:
                        pe.wait_ge(*at("m_bc", h - 1))
                        pe.wait_ge(*at("q_evac", h - 1))
                    nc.tensor.matmul(PS[:, 6, :], C("headsel")[0:4, h * 128:(h + 1) * 128], MM[0:4, :], start=True, stop=True)
                    ins = nc.tensor.matmul(PS[:, 7, :], C("headsel")[0:4, h * 128:(h + 1) * 128], MS[0:4, :], start=True, stop=True)
                    ins.then_inc(*step("pe", "m_bc_ps", h))
                    q_k(h, 0)
                    for st in range(4):
                        w = T - st * 128
                        if st < 3:
                            q_k(h, st + 1)
                        if st == 0:
                            pe.wait_ge(*at("m_bc", h))
                            if h >= 1:
                                pe.wait_ge(*at("h_out", h - 1))
                        part(pe, start["attn"] + h, 3, range(2 * st, 2 * st + 2))
                        pe.wait_ge(*at("att_done", n))
                        nc.tensor.matmul(PS[:, 2, st * 128:T], VROW[:, st, h, :], ATT[:, n % 2 * 512:n % 2 * 512 + w], start=st == 0, stop=st == 3)
                        ins = nc.tensor.matmul(PS[:, 3, st * 128:T], C("ones"), ATT[:, n % 2 * 512:n % 2 * 512 + w], start=st == 0, stop=st == 3)
                        ins.then_inc(*step("pe", "num_ps", n))
                        n += 1
                    pe.wait_ge(*at("krow_w", h))
                    for st in range(4):
                        ins = nc.tensor.matmul(PS[:, 4, h * 128:(h + 1) * 128], KROW[:, st, h, :], VROW[:, st, h, :], start=st == 0, stop=st == 3)
                    for st in range(4):
                        ins = nc.tensor.matmul(PS[:, 5, h:h + 1], KROW[:, st, h, :], C("ones")[:, 0:1], start=st == 0, stop=st == 3)
                ins.then_inc(*step("pe", "pC_ps"))
                pe.wait_ge(*at("q_evac", MH - 1))
                pe.wait_ge(*at("dg"))
                ins = nc.tensor.matmul(PS[:, 6, 0:96], C("ones")[0:4, :], DGs[0:4, :], start=True, stop=True)
                ins.then_inc(*step("pe", "bc_ps"))
                pe.wait_ge(*at("vd"))
                for i in range(8):
                    if i >= 4:
                        pe.wait_ge(*at("vb", i - 4))
                    ins = nc.tensor.matmul(PS[:, i % 4, :], C("ones"), VD[:, i * 512:(i + 1) * 512], start=True, stop=True)
                    ins.then_inc(*step("pe", "vb_ps", i))
                pe.wait_ge(*at("sC"))
                ins = nc.tensor.matmul(PS[:, 7, 0:32], C("ones"), QN[:, 0:32], start=True, stop=True)
                for h in range(MH):
                    for b in range(NS):
                        i = h * 8 + b
                        ins = nc.tensor.matmul(PS[:, 6, 128 + i:129 + i], SC4[:, i, :], QK[:, h, T + b:T + b + 1], start=True, stop=True)
                ins.then_inc(*step("pe", "s_num_ps"))
                pe.wait_ge(*so_far("pe"))

            def act(act):
                qk_sigmoid(act, 7)
                act.wait_ge(*at("gabs"))
                nc.scalar.activation(GB[0:4, :], GA[0:4, :], ACT.Exp, scale=-1.0).then_inc(*step("act"))
                act.wait_ge(*so_far("act"))
                nc.scalar.activation(GB[0:4, :], GB[0:4, :], ACT.Ln, bias=1.0).then_inc(*step("act", "softplus"))
                act.wait_ge(*so_far("act"))
                for i in range(8):
                    act.wait_ge(*at("m_row_ps", i))
                    dst = (VROW, KROW)[i // 4][:, i % 4, :, :].rearrange("p h v -> p (h v)")
                    nc.scalar.copy(dst, PS[:, i % 4, :]).then_inc(*step("act", "m_row", i))
                n = 0
                for h in range(MH):
                    act.wait_ge(*at("m_bc_ps", h))
                    if h:
                        act.wait_ge(*at("h_out", h - 1))
                    nc.scalar.copy(NMB, PS[:, 6, :]).then_inc(*step("act"))
                    nc.scalar.activation(EMB, PS[:, 7, :], ACT.Exp, scale=-1.0).then_inc(*step("act", "m_bc", h))
                    act.wait_ge(*so_far("act"))
                    act.wait_ge(*at("ut"))
                    nc.scalar.activation(WEND[:, :, h], UT[:, :, h], ACT.Exp, bias=NMB[:, T - 1:T]).then_inc(*step("act", "wend", h))
                    for st in range(4):
                        act.wait_ge(*at("att_arg", n))
                        o = n % 2 * 512
                        nc.scalar.activation(ATT[:, o:o + T - st * 128], ATT[:, o:o + T - st * 128], ACT.Exp).then_inc(*step("act", "att_exp", n))
                        n += 1
                    act.wait_ge(*at("tile", start["attn"] + h))
                    nc.scalar.copy(halves(Q[:, h, :]), pair(3)).then_inc(*step("act", "q_evac", h))
                act.wait_ge(*at("s_args"))
                nc.scalar.activation(cs[0:4, :], cs[0:4, :], ACT.Exp).then_inc(*step("act"))
                nc.scalar.activation(wi[0:4, :], wi[0:4, :], ACT.Exp).then_inc(*step("act", "s_exps"))
                act.wait_ge(*at("bc"))
                nc.scalar.activation(BC[:, 64:96], BC[:, 64:96], ACT.Exp, scale=-1.0).then_inc(*step("act", "s_em"))
                act.wait_ge(*so_far("act"))

            def dve(v):
                v.wait_ge(*at("m_evac", GATES))
                nc.vector.scalar_tensor_tensor(GA[0:4, :], LF[0:4, :], -1.0, LF[0:4, :], ALU.mult, ALU.max).then_inc(*step("dve", "gabs"))
                v.wait_ge(*so_far("dve"))
                v.wait_ge(*at("zero_last_cols"))
                for t in range(EARLY_QK, 8):
                    convolve(v, t)
                for t in range(1, 8):
                    v.wait_ge(*at("qk_sig", t - 1))
                    nc.vector.scalar_tensor_tensor(QK[:, t - 1, :], QK[:, t - 1, :], 1.0 if t - 1 < 4 else KSCALE,
                                                   QKT[:, t - 1, :], ALU.mult, ALU.mult).then_inc(*step("dve", "qk", t - 1))
                v.wait_ge(*at("qk_sig", 7))
                nc.vector.scalar_tensor_tensor(QK[:, 7, :], QK[:, 7, :], KSCALE, QKT[:, 7, :], ALU.mult, ALU.mult).then_inc(*step("dve", "qk", 7))
                nc.vector.tensor_copy(convout[:, :, 0, :], QKR[:, :, T:T + 3]).then_inc(*step("dve"))
                nc.vector.tensor_copy(convout[:, :, 1:, :], SFULL[:, :, :, 1:4]).then_inc(*step("dve", "convout"))
                r = slice(0, 4)
                v.wait_ge(*at("softplus"))
                v.wait_ge(*so_far("dve"))
                nc.vector.scalar_tensor_tensor(LF[r, :], LF[r, :], 0.0, GB[r, :], ALU.min, ALU.subtract).then_inc(*step("dve"))
                v.wait_ge(*so_far("dve"))
                nc.vector.tensor_tensor_scan(CUMF[r, :], C("ones")[r, 0:1].broadcast_to([4, T]), LF[r, 0:T], 0.0, ALU.mult, ALU.add).then_inc(*step("dve"))
                v.wait_ge(*so_far("dve"))
                nc.vector.tensor_tensor(UU[r, :], LI[r, 0:T], CUMF[r, :], ALU.subtract).then_inc(*step("dve"))
                v.wait_ge(*so_far("dve"))
                nc.vector.tensor_tensor_scan(MM[r, :], UU[r, :], UU[r, :], 0.0, ALU.max, ALU.max).then_inc(*step("dve"))
                v.wait_ge(*so_far("dve"))
                nc.vector.tensor_tensor(MS[r, :], MM[r, :], CUMF[r, :], ALU.add).then_inc(*step("dve", "m_stab"))
                v.wait_ge(*so_far("dve"))
                nc.vector.tensor_scalar(MM[r, :], MM[r, :], -1.0, None, ALU.mult).then_inc(*step("dve", "m_rows"))
                v.wait_ge(*so_far("dve"))
                v.wait_ge(*at("ut_ps"))
                nc.vector.tensor_copy(UT, PS[:, 6, 0:16].rearrange("p (s h) -> p s h", s=4)).then_inc(*step("dve", "ut"))
                v.wait_ge(*so_far("dve"))

                def weight_args(h, st):
                    n = h * 4 + st
                    o, w = n % 2 * 512, T - st * 128
                    if n >= 2:
                        v.wait_ge(*at("num_ps", n - 2))
                    nc.vector.tensor_scalar(ATT[:, o:o + w], NMB[:, st * 128:T], UT[:, st, h:h + 1], 0.0, ALU.add, ALU.min).then_inc(*step("dve", "att_arg", n))

                n = 0
                for h in range(MH):
                    v.wait_ge(*at("m_bc", h))
                    weight_args(h, 0)
                    for st in range(4):
                        o, w = n % 2 * 512, T - st * 128
                        if st < 3:
                            weight_args(h, st + 1)
                        v.wait_ge(*so_far("dve"))
                        v.wait_ge(*at("att_exp", n))
                        v.wait_ge(*at("att_ps", n))
                        nc.vector.tensor_tensor(ATT[:, o:o + w], ATT[:, o:o + w], PS[:, n % 2, 0:w], ALU.mult).then_inc(*step("dve"))
                        v.wait_ge(*so_far("dve"))
                        nc.vector.tensor_tensor(ATT[:, o:o + 128], ATT[:, o:o + 128], C("tri"), ALU.mult).then_inc(*step("dve", "att_done", n))
                        v.wait_ge(*so_far("dve"))
                        n += 1
                    v.wait_ge(*at("wend", h))
                    for st in range(4):
                        nc.vector.tensor_scalar(KROW[:, st, h, :], KROW[:, st, h, :], WEND[:, st, h:h + 1], None, ALU.mult).then_inc(*step("dve", "krow_w", h))
                    v.wait_ge(*at("num_ps", n - 1))
                    nc.vector.scalar_tensor_tensor(rD, PS[:, 3, :], -1.0, EMB, ALU.mult, ALU.max).then_inc(*step("dve"))
                    v.wait_ge(*so_far("dve"))
                    nc.vector.tensor_tensor(rD, rD, PS[:, 3, :], ALU.max).then_inc(*step("dve"))
                    v.wait_ge(*so_far("dve"))
                    nc.vector.reciprocal(rD, rD).then_inc(*step("dve"))
                    v.wait_ge(*so_far("dve"))
                    nc.vector.tensor_tensor(rD, rD, PS[:, 2, :], ALU.mult).then_inc(*step("dve", "h_out", h))
                    v.wait_ge(*so_far("dve"))
                    nc.vector.tensor_tensor(YM[:, h, 0:T], rD, MO[:, h, 0:T], ALU.mult).then_inc(*step("dve"))
                    v.wait_ge(*so_far("dve"))
                v.wait_ge(*at("pC_ps"))
                nc.vector.tensor_copy(pC, PS[:, 4, :]).then_inc(*step("dve"))
                nc.vector.tensor_copy(pn, PS[:, 5, 0:4]).then_inc(*step("dve", "pC"))
                v.wait_ge(*at("m0"))
                nc.vector.tensor_tensor(cs[r, :], LF[r, T:TOK], m0[r, :], ALU.add).then_inc(*step("dve"))
                v.wait_ge(*so_far("dve"))
                nc.vector.tensor_tensor(mp[r, :], cs[r, :], LI[r, T:TOK], ALU.max).then_inc(*step("dve", "s_m"))
                v.wait_ge(*so_far("dve"))
                nc.vector.tensor_tensor(cs[r, :], cs[r, :], mp[r, :], ALU.subtract).then_inc(*step("dve"))
                nc.vector.tensor_tensor(wi[r, :], LI[r, T:TOK], mp[r, :], ALU.subtract).then_inc(*step("dve", "s_args"))
                v.wait_ge(*at("s_exps"))
                for i, x in enumerate((cs, wi, mp)):
                    nc.vector.tensor_tensor(DGs[r, i * 32:(i + 1) * 32].rearrange("p (h b) -> p h b", h=4),
                                                   x[r, :].unsqueeze(1).broadcast_to([4, 4, NS]),
                                                   id128[r, 0:4].unsqueeze(2).broadcast_to([4, 4, NS]), ALU.mult).then_inc(*step("dve", "dg"))
                nc.vector.tensor_tensor(VD.rearrange("p (h b v) -> p h b v", h=4, b=NS),
                                               id128.unsqueeze(1).unsqueeze(1).broadcast_to([128, 4, NS, 128]),
                                               MV[:, :, T:TOK].unsqueeze(3).broadcast_to([128, 4, NS, 128]), ALU.mult).then_inc(*step("dve", "vd"))
                v.wait_ge(*at("bc_ps"))
                nc.vector.tensor_copy(BC, PS[:, 6, 0:96]).then_inc(*step("dve", "bc"))
                v.wait_ge(*so_far("dve"))
                v.wait_ge(*at("mn"))
                nc.vector.tensor_tensor(SN, SN, BC[:, 0:32], ALU.mult).then_inc(*step("dve"))
                nc.vector.tensor_tensor(v3(KW, 4), v3(BC[:, 32:64], 4), QK[:, 4:8, T:TOK], ALU.mult).then_inc(*step("dve"))
                v.wait_ge(*so_far("dve"))
                nc.vector.tensor_tensor(SN, SN, KW, ALU.add).then_inc(*step("dve", "sn"))
                v.wait_ge(*so_far("dve"))
                nc.vector.tensor_tensor(v3(QN[:, 0:32], 4), v3(SN, 4), QK[:, 0:4, T:TOK], ALU.mult).then_inc(*step("dve"))
                v.wait_ge(*so_far("dve"))
                v.wait_ge(*at("mC"))
                nc.vector.tensor_tensor(SC4, SC4, BC[:, 0:32].unsqueeze(2).broadcast_to([128, 32, 128]), ALU.mult).then_inc(*step("dve"))
                v.wait_ge(*so_far("dve"))
                for i in range(8):
                    v.wait_ge(*at("vb_ps", i))
                    nc.vector.tensor_tensor(VD4[:, 4 * i:4 * i + 4, :], PS[:, i % 4, :].rearrange("p (g n) -> p g n", g=4),
                                                   KW[:, 4 * i:4 * i + 4].unsqueeze(2).broadcast_to([128, 4, 128]), ALU.mult).then_inc(*step("dve", "vb", i))
                v.wait_ge(*so_far("dve"))
                nc.vector.tensor_tensor(SC, SC, VD, ALU.add).then_inc(*step("dve", "sC"))
                v.wait_ge(*so_far("dve"))
                v.wait_ge(*at("s_em"))
                v.wait_ge(*at("s_num_ps"))
                nc.vector.scalar_tensor_tensor(HS, PS[:, 7, 0:32], -1.0, BC[:, 64:96], ALU.mult, ALU.max).then_inc(*step("dve"))
                v.wait_ge(*so_far("dve"))
                nc.vector.tensor_tensor(HS, HS, PS[:, 7, 0:32], ALU.max).then_inc(*step("dve"))
                v.wait_ge(*so_far("dve"))
                nc.vector.reciprocal(HS, HS).then_inc(*step("dve"))
                v.wait_ge(*so_far("dve"))
                nc.vector.tensor_tensor(HS, HS, PS[:, 6, 128:160], ALU.mult).then_inc(*step("dve"))
                v.wait_ge(*so_far("dve"))
                nc.vector.tensor_tensor(YM[:, :, T:TOK], v3(HS, 4), MO[:, :, T:TOK], ALU.mult).then_inc(*step("dve", "ym"))
                v.wait_ge(*so_far("dve"))

            def pool(p):
                p.dma_start(m0[0:4, :], io["mm"]).then_inc(*moved("m0"))
                p.dma_start(SN, io["mn"]).then_inc(*moved("mn"))
                p.wait_ge(*at("m_stab"))
                p.dma_start(io["o_pm"], MS[0:4, T - 1:T]).then_inc(*moved("pm_out"))
                p.wait_ge(*at("convout"))
                p.dma_start(io["o_conv"], convout.rearrange("p t b j -> p (t b j)")).then_inc(*moved("conv_out"))
                p.dma_start(SC, io["mC"]).then_inc(*moved("mC"))
                p.wait_ge(*at("pC"))
                p.dma_start(io["o_pC"], pC).then_inc(*moved("pC_out"))
                p.dma_start(io["o_pn"], pn).then_inc(*moved("pn_out"))
                p.wait_ge(*at("s_m"))
                p.dma_start(io["o_sm"], mp[0:4, :]).then_inc(*moved("sm_out"))
                p.wait_ge(*at("sn"))
                p.dma_start(io["o_sn"], SN).then_inc(*moved("sn_out"))
                p.wait_ge(*at("sC"))
                p.dma_start(io["o_sC"], SC).then_inc(*moved("sC_out"))
                for x in ("pm_out", "conv_out", "pC_out", "pn_out", "sm_out", "sn_out"):
                    p.wait_ge(*at(x))

        a = 0
        a = 4 * TOK
        KVr = take(6 * TOK)
        KV = tiles(KVr, 6)
        w1d = take(4096).rearrange("p (kv j l h) -> p kv j l h", kv=2, j=2, l=16)
        w1 = take(2048).rearrange("p (kv l j h) -> p kv l j h", kv=2, j=2, l=8)
        pec = take(32)
        w2 = take(128)
        PEB = take(2)
        KEEP = a
        VR2 = take(1024).rearrange("p (b s f) -> p b s f", b=2, s=4)
        GR = take(96).rearrange("p (s n) -> p s n", s=4)
        HX, HSG = take(64), take(64)
        KC = take(32)
        VC = take(128)
        SCm, MXc, SMc = take(256), take(8), take(8)
        PTC = take(1024)
        Pb = [take(2048).rearrange("p (j n) -> p j n", j=4) for _ in range(2)]
        NBi = [take(4) for _ in range(2)]
        SUMi = [take(4) for _ in range(2)]
        RGi = take(4)
        PTb = [take(512) for _ in range(2)]
        attn_end = a
        UNITS = [(qt, g, br) for qt in range(4) for g in range(2) for br in range(2)]
        KB = [(i, kb) for i, (qt, g, br) in enumerate(UNITS) for kb in range(qt + 1)]
        KB_AT = {x: n for n, x in enumerate(KB)}

        def hid_evac(eng_act, tag, src, kv, n, X, S):
            nc.scalar.activation(X, src, ACT.Identity, bias=PEB[:, kv:kv + 1]).then_inc(*step("act"))
            nc.scalar.activation(S, src, ACT.Sigmoid, bias=PEB[:, kv:kv + 1]).then_inc(*step("act", tag, "hid_parts", n))

        EARLY = [(m, b) for m in range(8) for b in (0, 2)]
        MGr = region(TOP - 4680 - KT * TOK, KT * TOK)
        MG = tiles(MGr, KT)
        SGe = region(TOP - 4680 - KT * TOK - TOK, TOK)
        FILL = 3

        def stall_pe(pe, s):
            u, third = s // 3, s % 3
            g = start["early"] + 2 * u
            if third == 0 and u:
                pe.wait_ge(*at("e_gated", u - 1))
            if third == 2:
                pe.wait_ge(*at("e_sig", u))
                product(pe, g + 1, FILL, YM if EARLY[u][1] == 0 else YR, kts=4)
            else:
                part(pe, g, FILL, range(4 * third, 4 * third + 4))

        def stall_act(act, s):
            u, third = s // 3, s % 3
            if third == 1:
                act.wait_ge(*at("tile", start["early"] + 2 * u))
                if u:
                    act.wait_ge(*at("e_merged", u - 1))
                nc.scalar.activation(halves(SGe), pair(FILL), ACT.Sigmoid).then_inc(*step("act", "e_sig", u))

        def stall_dve(v, s):
            u, third = s // 3, s % 3
            if third == 2:
                m, b = EARLY[u]
                v.wait_ge(*at("tile", start["early"] + 2 * u + 1))
                v.wait_ge(*at("e_sig", u))
                if b == 0:
                    nc.vector.tensor_tensor(halves(MG[:, m, :]), pair(FILL), halves(SGe), ALU.mult).then_inc(*step("dve", "e_gated", u))
                    counts.name_last("dve", "e_merged", u)
                else:
                    nc.vector.tensor_tensor(halves(SGe), pair(FILL), halves(SGe), ALU.mult).then_inc(*step("dve", "e_gated", u))
                    v.wait_ge(*so_far("dve"))
                    nc.vector.tensor_tensor(MG[:, m, :], MG[:, m, :], SGe, ALU.add).then_inc(*step("dve", "e_merged", u))

        def stall_cmp(qt, x):
            return KB_AT[(4 * qt, 0)] + 2 * qt + x

        def stall_kb(i, kb):
            return KB_AT[(i, kb)] + 2 * (UNITS[i][0] + 1)

        class Attn:
            def pe(pe):
                for n in range(4, 10):
                    if n >= 7:
                        pe.wait_ge(*at("a_evac", n - 3))
                    product(pe, start["attn"] + n, n % 3, XN)
                pe.wait_ge(*at("w1"))
                pe.wait_ge(*at("pe"))
                for kv in range(2):
                    for g in range(2):
                        for j in range(2):
                            for l in range(8):
                                i = kv * 16 + j * 8 + l
                                ins = nc.tensor.matmul(PS[64 * g:64 * g + 64, 6, kv:kv + 1], w1[:, kv, l, j, :], pec[:, i:i + 1],
                                                       start=j + l == 0, stop=j * 8 + l == 15)
                ins.then_inc(*step("pe", "peb_ps"))
                for n in range(7, 10):
                    pe.wait_ge(*at("a_evac", n))
                for i, br in enumerate((3, 5)):
                    for st in range(4):
                        ins = nc.tensor.transpose(PS[:, i, st * 128:(st + 1) * 128], KV[:, br, st * 128:(st + 1) * 128], id128)
                ins.then_inc(*step("pe", "vr_ps"))
                for st in range(4):
                    ins = nc.tensor.transpose(PS[:, 2, st * 24:st * 24 + 24], g24[0:24, st * 128:(st + 1) * 128], id128[0:24, 0:24])
                ins.then_inc(*step("pe", "gr_ps"))
                pe.wait_ge(*at("w1d"))
                for kv in range(2):
                    for g in range(2):
                        q = slice(64 * g, 64 * g + 64)
                        for j in range(2):
                            for l in range(16):
                                ins = nc.tensor.matmul(PS[q, 3 + kv, 0:31], w1d[q, kv, j, l, :],
                                                       KV[q, kv, 16 * j + l:16 * j + l + 481:16], start=j + l == 0, stop=j * 16 + l == 31)
                ins.then_inc(*step("pe", "hid_ps"))
                pe.wait_ge(*at("hid"))
                pe.wait_ge(*at("w2"))
                for g in range(2):
                    q = slice(64 * g, 64 * g + 64)
                    nc.tensor.matmul(PS[q, 5, 0:32], w2[q, 0:64], HX[q, 0:32], start=True, stop=True)
                for g in range(2):
                    q = slice(64 * g, 64 * g + 64)
                    ins = nc.tensor.matmul(PS[0:32, 7 - g, 0:64], HX[q, 32:64], w2[q, 64:128], start=True, stop=True)
                ins.then_inc(*step("pe", "kvc_ps"))
                pe.wait_ge(*at("kvc"))
                pe.wait_ge(*at("gr"))

                def cmp_scores(qt):
                    for g in range(2):
                        q = slice(64 * g, 64 * g + 64)
                        for j in range(4):
                            ins = nc.tensor.matmul(PS[:, 4 + g, j * 32:j * 32 + 32], Q[q, j, qt * 128:(qt + 1) * 128],
                                                   KC[q, :], start=True, stop=True)
                    ins.then_inc(*step("pe", "cmp_ps", qt))
                    stall_pe(pe, stall_cmp(qt, 0))
                    pe.wait_ge(*at("cmp_p", qt))
                    for h in range(8):
                        ins = nc.tensor.transpose(PS[0:32, 4 + h // 4, h % 4 * 128:h % 4 * 128 + 128], SCm[:, h * 32:h * 32 + 32], id128)
                    ins.then_inc(*step("pe", "cmp_pt_ps", qt))
                    stall_pe(pe, stall_cmp(qt, 1))
                    pe.wait_ge(*at("cmp_pt", qt))

                def scores(i):
                    qt, g, br = UNITS[i]
                    W = (qt + 1) * 128
                    q = slice(64 * g, 64 * g + 64)
                    if i >= 1:
                        pe.wait_ge(*at("exp", i - 1))
                    for j in range(4):
                        ins = nc.tensor.matmul(PS[:, j, 0:W], Q[q, j, qt * 128:W], KV[q, (2, 4)[br], 0:W], start=True, stop=True)
                    ins.then_inc(*step("pe", "sc_ps", i))

                scores(0)
                for i, (qt, g, br) in enumerate(UNITS):
                    if g == 0 and br == 0:
                        if qt >= 1:
                            pe.wait_ge(*at("o_out", i // 2 - 1))
                        cmp_scores(qt)
                    if i + 1 < len(UNITS):
                        scores(i + 1)
                    unit = i // 2
                    o = 5
                    if br == 0:
                        if unit >= 1:
                            pe.wait_ge(*at("o_out", unit - 1))
                        nc.tensor.matmul(PS[:, o, :], VC[0:32, :], PTC[0:32, g * 512:(g + 1) * 512], start=True, stop=False)
                    pe.wait_ge(*at("p", i))
                    for kb in range(qt + 1):
                        n = KB_AT[(i, kb)]
                        for j in range(4):
                            ins = nc.tensor.transpose(PS[:, 4, j * 128:(j + 1) * 128], Pb[i % 2][:, j, kb * 128:(kb + 1) * 128], id128)
                        ins.then_inc(*step("pe", "pt_ps", n))
                        stall_pe(pe, stall_kb(i, kb))
                        pe.wait_ge(*at("pt", n))
                        ins = nc.tensor.matmul(PS[:, o, :], VR2[:, br, kb, :], PTb[n % 2], start=False, stop=br == 1 and kb == qt)
                        ins.then_inc(*step("pe", "pv", n))
                pe.wait_ge(*so_far("pe"))

            def act(act):
                act.wait_ge(*at("sC_out"))
                for n in range(4, 10):
                    act.wait_ge(*at("tile", start["attn"] + n))
                    nc.scalar.copy(halves(KV[:, n - 4, :]), pair(n % 3)).then_inc(*step("act", "a_evac", n))
                act.wait_ge(*at("peb"))
                act.wait_ge(*at("hid_ps"))
                for kv in range(2):
                    c = slice(kv * 32, kv * 32 + 31)
                    hid_evac(act, "prompt", PS[:, 3 + kv, 0:31], kv, kv, HX[:, c], HSG[:, c])
                for i, (qt, g, br) in enumerate(UNITS):
                    if g == 0 and br == 0:
                        act.wait_ge(*at("cmp_sub", qt))
                        nc.scalar.activation(SCm, SCm, ACT.Exp).then_inc(*step("act", "cmp_exp", qt))
                        for x in range(2):
                            stall_act(act, stall_cmp(qt, x))
                    act.wait_ge(*at("nb", i))
                    if i >= 2:
                        n = KB_AT[(i - 2, UNITS[i - 2][0])]
                        act.wait_ge(*at("pt_ps", n))
                    W = (qt + 1) * 128
                    for j in range(4):
                        nc.scalar.activation(Pb[i % 2][:, j, 0:W], PS[:, j, 0:W], ACT.Exp, bias=NBi[i % 2][:, j:j + 1], scale=SCALE,
                                                      accum_out=SUMi[i % 2][:, j:j + 1]).then_inc(*step("act", "exp", i))
                    for kb in range(qt + 1):
                        n = KB_AT[(i, kb)]
                        if n % 2:
                            act.wait_ge(*at("pt_ps", n))
                            if n >= 2:
                                act.wait_ge(*at("pv", n - 2))
                            nc.scalar.copy(PTb[n % 2], PS[:, 4, :]).then_inc(*step("act", "pt", n))
                        stall_act(act, stall_kb(i, kb))
                    if br == 1:
                        unit = i // 2
                        act.wait_ge(*at("pv", KB_AT[(i, qt)]))
                        q = slice(64 * g, 64 * g + 64)
                        nc.scalar.copy(YA[q, :, qt * 128:(qt + 1) * 128], PS[q, 5, :].rearrange("p (j n) -> p j n", j=4)).then_inc(*step("act", "o_out", unit))

            def dve(v):
                nc.vector.memset(HX, 0.0).then_inc(*step("dve", "hx_zero"))
                v.wait_ge(*so_far("dve"))
                v.wait_ge(*at("peb_ps"))
                nc.vector.tensor_copy(PEB, PS[:, 6, 0:2]).then_inc(*step("dve", "peb"))
                v.wait_ge(*at("vr_ps"))
                nc.vector.tensor_copy(VR2[:, :, :, :].rearrange("p b s f -> p b (s f)"), PS[:, 0:2, :]).then_inc(*step("dve"))
                v.wait_ge(*at("gr_ps"))
                nc.vector.tensor_copy(GR[:, :, :].rearrange("p s n -> p (s n)"), PS[:, 2, 0:96]).then_inc(*step("dve", "gr"))
                v.wait_ge(*at("prompt", "hid_parts", 1))
                nc.vector.tensor_tensor(v3(HX, 2)[:, :, 0:31], v3(HX, 2)[:, :, 0:31], v3(HSG, 2)[:, :, 0:31], ALU.mult).then_inc(*step("dve", "hid"))
                v.wait_ge(*so_far("dve"))
                v.wait_ge(*at("kvc_ps"))
                nc.vector.tensor_copy(KC, PS[:, 5, 0:32]).then_inc(*step("dve"))
                nc.vector.tensor_copy(VC[0:32, 0:64], PS[0:32, 7, 0:64]).then_inc(*step("dve"))
                nc.vector.tensor_copy(VC[0:32, 64:128], PS[0:32, 6, 0:64]).then_inc(*step("dve", "kvc"))
                S8 = v3(SCm, 8)

                def cmp(qt):
                    add = v3(C("cmpadd"), 4)[:, qt, :].unsqueeze(1).broadcast_to([128, 8, 32])
                    one = v3(C("cmp01"), 4)[:, qt, :].unsqueeze(1).broadcast_to([128, 8, 32])
                    v.wait_ge(*at("cmp_ps", qt))
                    if qt:
                        v.wait_ge(*at("cmp_pt_ps", qt - 1))
                    for g in range(2):
                        nc.vector.scalar_tensor_tensor(S8[:, 4 * g:4 * g + 4, :], v3(PS[:, 4 + g, 0:128], 4), SCALE, add[:, 0:4, :], ALU.mult, ALU.add).then_inc(*step("dve"))
                    v.wait_ge(*so_far("dve"))
                    nc.vector.tensor_reduce(MXc, S8, AX.X, ALU.max).then_inc(*step("dve"))
                    v.wait_ge(*so_far("dve"))
                    nc.vector.tensor_tensor(S8, S8, MXc.unsqueeze(2).broadcast_to([128, 8, 32]), ALU.subtract).then_inc(*step("dve", "cmp_sub", qt))
                    v.wait_ge(*so_far("dve"))
                    v.wait_ge(*at("cmp_exp", qt))
                    nc.vector.tensor_reduce(SMc, S8, AX.X, ALU.add).then_inc(*step("dve"))
                    v.wait_ge(*so_far("dve"))
                    nc.vector.reciprocal(SMc, SMc).then_inc(*step("dve"))
                    v.wait_ge(*so_far("dve"))
                    nc.vector.tensor_tensor(SMc, SMc, GR[:, qt, 0:8], ALU.mult).then_inc(*step("dve"))
                    v.wait_ge(*so_far("dve"))
                    nc.vector.tensor_tensor(S8, S8, one, ALU.mult).then_inc(*step("dve"))
                    v.wait_ge(*so_far("dve"))
                    nc.vector.tensor_tensor(S8, S8, SMc.unsqueeze(2).broadcast_to([128, 8, 32]), ALU.mult).then_inc(*step("dve", "cmp_p", qt))
                    v.wait_ge(*so_far("dve"))
                    v.wait_ge(*at("cmp_pt_ps", qt))
                    stall_dve(v, stall_cmp(qt, 0))
                    if qt:
                        v.wait_ge(*at("pv", KB_AT[(4 * qt - 1, 0)]))
                    nc.vector.tensor_copy(v3(PTC[0:32, :], 2), PS[0:32, 4:6, :]).then_inc(*step("dve", "cmp_pt", qt))
                    stall_dve(v, stall_cmp(qt, 1))

                def nb(i):
                    W = (UNITS[i][0] + 1) * 128
                    v.wait_ge(*at("sc_ps", i))
                    if i >= 2:
                        v.wait_ge(*at("exp", i - 2))
                    nc.vector.tensor_tensor(PS[:, 0:4, W - 128:W], PS[:, 0:4, W - 128:W], C("causal").unsqueeze(1).broadcast_to([128, 4, 128]),
                                            ALU.add).then_inc(*step("dve"))
                    v.wait_ge(*so_far("dve"))
                    nc.vector.tensor_reduce(NBi[i % 2], PS[:, 0:4, 0:W], AX.X, ALU.max, negate=True).then_inc(*step("dve"))
                    v.wait_ge(*so_far("dve"))
                    nc.vector.tensor_scalar(NBi[i % 2], NBi[i % 2], SCALE, None, ALU.mult).then_inc(*step("dve", "nb", i))
                    v.wait_ge(*so_far("dve"))

                for i, (qt, g, br) in enumerate(UNITS):
                    if g == 0 and br == 0:
                        cmp(qt)
                    if i == 0:
                        nb(0)
                    v.wait_ge(*at("exp", i))
                    nc.vector.reciprocal(RGi, SUMi[i % 2]).then_inc(*step("dve"))
                    v.wait_ge(*so_far("dve"))
                    h = 8 * (br + 1) + 4 * g
                    nc.vector.tensor_tensor(RGi, RGi, GR[:, qt, h:h + 4], ALU.mult).then_inc(*step("dve"))
                    v.wait_ge(*so_far("dve"))
                    W = (qt + 1) * 128
                    for j in range(4):
                        nc.vector.tensor_scalar(Pb[i % 2][:, j, 0:W], Pb[i % 2][:, j, 0:W], RGi[:, j:j + 1], None, ALU.mult).then_inc(*step("dve", "p", i))
                    if i + 1 < len(UNITS):
                        nb(i + 1)
                    for kb in range(qt + 1):
                        n = KB_AT[(i, kb)]
                        if n % 2 == 0:
                            v.wait_ge(*at("pt_ps", n))
                            if n >= 2:
                                v.wait_ge(*at("pv", n - 2))
                            nc.vector.tensor_copy(PTb[n % 2], PS[:, 4, :]).then_inc(*step("dve", "pt", n))
                        stall_dve(v, stall_kb(i, kb))

            def pool(p):
                p.dma_start(w1d.rearrange("p kv j l h -> p (kv j l h)"), io["w1d"]).then_inc(*moved("w1d"))
                p.dma_start(w1.rearrange("p kv l j h -> p (kv l j h)"), io["w1"]).then_inc(*moved("w1"))
                p.dma_start(pec, io["pe"]).then_inc(*moved("pe"))
                p.dma_start(w2, io["w2"]).then_inc(*moved("w2"))
                p.wait_ge(*at("a_evac", 9))
                p.dma_start(io["o_kv"], KVr).then_inc(*moved("kv_out"))
                p.wait_ge(*at("table"))
                key_pages(p, 0, 1)
                for b in range(NS):
                    p.dma_start(io["o_winp"][b], io["win"][:, b, :, 1:512].rearrange("p k n -> k p n")).then_inc(*moved("win_out"))
                p.wait_ge(*at("win_out"))
                p.wait_ge(*at("kv_out"))

        a = KEEP
        NSLOT = 23
        WIN = [Qr[:, i * 512:(i + 1) * 512] for i in range(2)]
        HIDS = take(512)
        HID, HSGs = HIDS[:, 0:256], HIDS[:, 256:512]
        KCs = take(128)
        QD = take(NS * 8).rearrange("p (b h) -> p b h", b=NS)
        SC_ = take(NSLOT * 64).rearrange("p (s n) -> p s n", s=NSLOT)
        VCs = take(NS * 128).rearrange("p (b f) -> p b f", b=NS)
        MXs, SMs = take(192), take(192)
        MXT = take(1)
        DGm = take(192)
        GBs = take(192)
        spent = w1d.rearrange("p kv j l h -> p (kv j l h)")
        ONEW = spent[:, 2048:4096].rearrange("p (k b f) -> p k b f", k=2, b=NS)
        BSEL = spent[:, 0:2048].rearrange("p (g n) -> p g n", g=NPAGE)
        OH = spent[:, 0:1024]
        PGRP = take(16)
        RANK, RSEL = take(NBLK), take(NBLK)
        TOP8 = take(8)
        ADDT = take(16)
        ADD = take(256).rearrange("p (g n) -> p g n", g=NPAGE)
        G24D = take(192)
        VPw = [ap.rearrange("p (g f) -> p g f", g=4) for ap in (
            Qr[:, 1024:1536], Qr[:, 1536:2048], KVr[:, 0:512], KVr[:, 512:1024], SGe[:, 0:512], HIDS, *WIN)]
        base = TOP - 4680 - KT * TOK - TOK - 128 - 2 * NPAGE * 384
        assert a <= base and base + NPAGE * 384 >= attn_end
        PG = [region(base + x * NPAGE * 384, NPAGE * 384).rearrange("p (g k n) -> p g k n", g=NPAGE, k=3) for x in (1, 0)]
        tab = region(TOP - 4680 - KT * TOK - TOK - 128, 128).bitcast(I32)
        NV = 6
        VP = [PG[i // 3].rearrange("p g k n -> p (g k n)")[:, i % 3 * 2048:(i % 3 + 1) * 2048].rearrange("p (g f) -> p g f", g=NPAGE)
              for i in range(NV)]
        assert a <= TOP - 4680, a
        SLOTS = {"sel": (0, 17), "win": (17, 22), "cmp": (22, 23)}

        def page(queue, b, pg):
            n_pool = io["pages"].shape[0]
            return bass.ds(queue.value_load(tab[0:1, b * NPAGE + pg:b * NPAGE + pg + 1], min_val=0, max_val=n_pool - 1), 1)

        def key_pages(queue, b, lane):
            if b >= 2:
                queue.wait_ge(*at("s_sc_ps", b - 2))
                queue.wait_ge(*at("s_hid_ps", b - 2))
            for pg in range(lane, NPAGE, 2):
                queue.dma_start(PG[b % 2][:, pg], io["pages"][page(queue, b, pg)].rearrange("a p k n -> p (a k) n")).then_inc(
                    *moved("pages", b, lane, lane=2 * lane + b % 2))

        def value_pages(queue, b, lane):
            if b < NV:
                queue.wait_ge(*at("s_sc_ps", NS - 2 + b // 3))
            else:
                queue.wait_ge(*at("s_pv", b - NV))
            for pg in (range(0, 6), range(6, 11), range(11, NPAGE))[lane]:
                queue.dma_start(VP[b % NV][:, pg], io["pages_v"][page(queue, b, pg)].rearrange("a p n -> p (a n)")).then_inc(
                    *moved("pages_v", b, lane, lane=NV * lane + b % NV))

        HALVES = [[ap[:, :] for ap in ST], [XS[:, :], US[:, :]]]

        class Sample:
            def pe(pe):
                pe.wait_ge(*at("g24d"))
                ins = nc.tensor.matmul(PS[:, 7, 0:192], C("ones")[0:24, :], G24D[0:24, :], start=True, stop=True)
                ins.then_inc(*step("pe", "gb_ps"))
                for i, kv in enumerate((3, 5)):
                    for b in range(NS):
                        ins = nc.tensor.transpose(PS[0:1, 3 + 2 * i + b // 4, b % 4 * 128:b % 4 * 128 + 128], KV[:, kv, T + b:T + b + 1], id128)
                ins.then_inc(*step("pe", "new_v_ps"))
                pe.wait_ge(*at("new_v"))
                pe.wait_ge(*at("gb"))
                pe.wait_ge(*at("qd"))
                for b in range(NS + 2):
                    if b < NS:
                        p_ = PG[b % 2]
                        for lane in range(2):
                            pe.wait_ge(*at("pages", b, lane))
                        if b >= 1:
                            pe.wait_ge(*at("s_x", b - 1))
                        for kv in range(2):
                            for l in range(8):
                                ins = nc.tensor.matmul(PS[:, kv, 0:256], w1[:, kv, l, :, :].rearrange("p j h -> p (j h)"),
                                                       p_[:, :, kv, l * 16:(l + 1) * 16], start=l == 0, stop=l == 7)
                        ins.then_inc(*step("pe", "s_hid_ps", b))
                    if b >= 2:
                        c = b - 2
                        pe.wait_ge(*at("s_kvc", c))
                        if c >= 1:
                            pe.wait_ge(*at("s_cmp_scores", c - 1))
                        ins = nc.tensor.matmul(PS[0:127, 6, 0:8], KCs[:, 0:127], QD[:, c, :], start=True, stop=True)
                        ins.then_inc(*step("pe", "s_cmp_ps", c))
                    if 1 <= b <= NS:
                        c = b - 1
                        pe.wait_ge(*at("s_x", c))
                        if c >= 1:
                            pe.wait_ge(*at("s_hid_parts", c - 1))
                        for kv in range(2):
                            for g in range(2):
                                for j in range(2):
                                    n = g * 128 + j
                                    ins = nc.tensor.matmul(PS[64 * g:64 * g + 64, 7, kv * 128:kv * 128 + 127], id128[:, 64 * j:64 * j + 64],
                                                           HALVES[c % 2][kv][:, n:n + 127], start=j == 0, stop=j == 1)
                        ins.then_inc(*step("pe", "s_hc_ps", c))
                    if b < NS:
                        if b >= 1:
                            pe.wait_ge(*at("s_scores", b - 1))
                        for pg in range(NPAGE):
                            ins = nc.tensor.matmul(PS[:, 2, pg * 8:pg * 8 + 8], p_[:, pg, 2, :], QD[:, b, :], start=True, stop=True)
                        nc.tensor.matmul(PS[0:1, 2, 128:136], KV[:, 2, T + b:T + b + 1], QD[:, b, :], start=True, stop=True)
                        pe.wait_ge(*at("win", b))
                        for i in range(4):
                            nc.tensor.matmul(PS[:, 2, 136 + i * 8:144 + i * 8], WIN[b % 2][:, i * 128:(i + 1) * 128], QD[:, b, :], start=True, stop=True)
                        ins = nc.tensor.matmul(PS[0:1, 2, 168:176], KV[:, 4, T + b:T + b + 1], QD[:, b, :], start=True, stop=True)
                        ins.then_inc(*step("pe", "s_sc_ps", b))
                    if 1 <= b <= NS:
                        c = b - 1
                        pe.wait_ge(*at("s_hid", c))
                        if c >= 1:
                            pe.wait_ge(*at("s_kvc", c - 1))
                        for g in range(2):
                            q = slice(64 * g, 64 * g + 64)
                            nc.tensor.matmul(PS[q, 3, 0:127], w2[q, 0:64], HID[q, 0:127], start=True, stop=True)
                        for g in range(2):
                            q = slice(64 * g, 64 * g + 64)
                            ins = nc.tensor.matmul(PS[0:127, 4 + g, 0:64], HID[q, 128:255], w2[q, 64:128], start=True, stop=True)
                        ins.then_inc(*step("pe", "s_kvc_ps", c))

                def softmax(br):
                    pe.wait_ge(*at("s_max", br))
                    ins = nc.tensor.transpose(PS[0:64, 0, 0:128], MXs[:, 0:64], id128)
                    ins.then_inc(*step("pe", "s_maxt_ps", br))
                    pe.wait_ge(*at("s_maxd", br))
                    ins = nc.tensor.matmul(PS[:, 1, 0:64], C("ones")[0:64, :], DGm[0:64, 0:64], start=True, stop=True)
                    ins.then_inc(*step("pe", "s_maxb_ps", br))
                    pe.wait_ge(*at("s_sum", br))
                    ins = nc.tensor.matmul(PS[:, 2, 0:64], C("ones"), SMs[:, 0:64], start=True, stop=True)
                    ins.then_inc(*step("pe", "s_sum_ps", br))

                pe.wait_ge(*at("s_cmp_scores", NS - 1))
                softmax("cmp")
                pe.wait_ge(*at("pgrp"))
                ins = nc.tensor.matmul(PS[0:16, 3, 0:NBLK], PGRP, C("covers"), start=True, stop=True)
                ins.then_inc(*step("pe", "rank_ps"))
                pe.wait_ge(*at("rsel"))
                ins = nc.tensor.transpose(PS[0:32, 4, 0:16], RSEL[0:16, 0:32], id128[0:16, 0:16])
                ins.then_inc(*step("pe", "addt_ps"))
                pe.wait_ge(*at("addt"))
                pe.wait_ge(*at("blocksel"))
                for pg in range(NPAGE):
                    ins = nc.tensor.matmul(PS[:, 3, pg * 16:pg * 16 + 16], BSEL[0:32, pg, :], ADDT[0:32, :], start=True, stop=True)
                ins.then_inc(*step("pe", "add_ps"))
                softmax("sel")
                softmax("win")
                product(pe, start["merge"], 0, XN)
                pe.wait_ge(*at("s_p"))
                pe.wait_ge(*at("new_v"))
                for b in range(NS):
                    o = slice(b * 8, b * 8 + 8)
                    out = PS[0:8, 6 + b // 4, b % 4 * 128:b % 4 * 128 + 128]
                    for lane in range(3):
                        pe.wait_ge(*at("pages_v", b, lane))
                    pe.wait_ge(*at("windows_v", b))
                    for pg in range(NPAGE):
                        nc.tensor.matmul(out, SC_[:, pg, o], VP[b % NV][:, pg, :], start=pg == 0, stop=False)
                    nc.tensor.matmul(out, SC_[0:1, 16, o], ONEW[0:1, 0, b, :], start=False, stop=False)
                    for i in range(4):
                        nc.tensor.matmul(out, SC_[:, 17 + i, o], VPw[b][:, i, :], start=False, stop=False)
                    nc.tensor.matmul(out, SC_[0:1, 21, o], ONEW[0:1, 1, b, :], start=False, stop=False)
                    ins = nc.tensor.matmul(out, SC_[0:127, 22, o], VCs[0:127, b, :], start=False, stop=True)
                    ins.then_inc(*step("pe", "s_pv", b))
                pe.wait_ge(*at("s_o"))
                for b in range(NS):
                    ins = nc.tensor.transpose(PS[:, 5, b * 8:b * 8 + 8], OH[0:8, b * 128:b * 128 + 128], id128[0:8, 0:8])
                ins.then_inc(*step("pe", "s_o_ps"))
                pe.wait_ge(*so_far("pe"))

            def act(act):
                for b in range(NS + 1):
                    if b < NS:
                        act.wait_ge(*at("s_hid_ps", b))
                        if b >= 2:
                            act.wait_ge(*at("s_hc_ps", b - 2))
                        for kv in range(2):
                            nc.scalar.copy(HALVES[b % 2][kv].rearrange("p (g s n) -> p g s n", g=2, s=NPAGE),
                                           PS[:, kv, 0:256].rearrange("p (s g n) -> p g s n", g=2, s=NPAGE)).then_inc(*step("act", "s_x", b))
                    if b >= 1:
                        act.wait_ge(*at("s_hc_ps", b - 1))
                        if b >= 2:
                            act.wait_ge(*at("s_kvc_ps", b - 2))
                        for kv in range(2):
                            src = PS[:, 7, kv * 128:kv * 128 + 127]
                            nc.scalar.activation(HID[:, kv * 128:kv * 128 + 127], src, ACT.Identity, bias=PEB[:, kv:kv + 1]).then_inc(*step("act"))
                            nc.scalar.activation(HSGs[:, kv * 128:kv * 128 + 127], src, ACT.Sigmoid, bias=PEB[:, kv:kv + 1]).then_inc(*step("act", "s_hid_parts", b - 1))
                for br in ("cmp", "sel", "win"):
                    act.wait_ge(*at("s_sub", br))
                    a_, b_ = SLOTS[br]
                    nc.scalar.activation(SC_[:, a_:b_, :], SC_[:, a_:b_, :], ACT.Exp).then_inc(*step("act", "s_exp", br))
                    if br == "cmp":
                        for b in range(3):
                            value_pages(act, b, 2)
                for b in range(3, NS):
                    value_pages(act, b, 2)

            def dve(v):
                nc.vector.memset(SC_, NEG).then_inc(*step("dve", "sc_zero"))
                v.wait_ge(*so_far("dve"))
                nc.vector.tensor_tensor(G24D[0:24, :].rearrange("p (r b h) -> p r b h", r=3, b=NS),
                                               g24[0:24, T:TOK].unsqueeze(1).unsqueeze(3).broadcast_to([24, 3, NS, 8]),
                                               id128[0:24, 0:24].rearrange("p (r h) -> p r h", r=3).unsqueeze(2).broadcast_to([24, 3, NS, 8]),
                                               ALU.mult).then_inc(*step("dve", "g24d"))
                nc.vector.memset(QD, 0.0).then_inc(*step("dve"))
                v.wait_ge(*so_far("dve"))
                for g in range(2):
                    q = slice(64 * g, 64 * g + 64)
                    nc.vector.tensor_copy(QD[q, :, 4 * g:4 * g + 4], Q[q, :, T:TOK].rearrange("p j b -> p b j")).then_inc(*step("dve", "qd"))
                v.wait_ge(*at("gb_ps"))
                nc.vector.tensor_copy(GBs, PS[:, 7, 0:192]).then_inc(*step("dve", "gb"))
                v.wait_ge(*at("new_v_ps"))
                nc.vector.tensor_copy(ONEW[0:1].rearrange("p k b f -> p (k b f)").rearrange("p (a n) -> p a n", a=4), PS[0:1, 3:7, :]).then_inc(*step("dve", "new_v"))
                for b in range(NS + 2):
                    if b >= 2:
                        c = b - 2
                        v.wait_ge(*at("s_cmp_ps", c))
                        nc.vector.tensor_scalar(SC_[0:127, 22, c * 8:c * 8 + 8], PS[0:127, 6, 0:8], SCALE, None, ALU.mult).then_inc(*step("dve", "s_cmp_scores", c))
                    if b < NS:
                        o = slice(b * 8, b * 8 + 8)
                        v.wait_ge(*at("s_sc_ps", b))
                        nc.vector.tensor_scalar(SC_[:, 0:16, o], PS[:, 2, 0:128].rearrange("p (s h) -> p s h", s=16), SCALE, None, ALU.mult).then_inc(*step("dve"))
                        nc.vector.tensor_scalar(SC_[0:1, 16, o], PS[0:1, 2, 128:136], SCALE, None, ALU.mult).then_inc(*step("dve"))
                        nc.vector.tensor_scalar(SC_[:, 17:21, o], PS[:, 2, 136:168].rearrange("p (s h) -> p s h", s=4), SCALE, None, ALU.mult).then_inc(*step("dve"))
                        nc.vector.tensor_scalar(SC_[0:1, 21, o], PS[0:1, 2, 168:176], SCALE, None, ALU.mult).then_inc(*step("dve", "s_scores", b))
                    if 1 <= b <= NS:
                        c = b - 1
                        v.wait_ge(*at("s_hid_parts", c))
                        nc.vector.tensor_tensor(v3(HID, 2)[:, :, 0:127], v3(HID, 2)[:, :, 0:127], v3(HSGs, 2)[:, :, 0:127], ALU.mult).then_inc(*step("dve", "s_hid", c))
                        v.wait_ge(*so_far("dve"))
                        v.wait_ge(*at("s_kvc_ps", c))
                        nc.vector.tensor_copy(KCs[:, 0:127], PS[:, 3, 0:127]).then_inc(*step("dve"))
                        nc.vector.tensor_copy(v3(VCs[0:127, c, :], 2), PS[0:127, 4:6, 0:64]).then_inc(*step("dve", "s_kvc", c))
                v.wait_ge(*so_far("dve"))
                nc.vector.tensor_scalar(SC_[:, 17, :], SC_[:, 17, :], C("first"), None, ALU.add).then_inc(*step("dve"))
                v.wait_ge(*so_far("dve"))

                def softmax(br, gate):
                    a_, b_ = SLOTS[br]
                    n = b_ - a_
                    S = SC_[:, a_:b_, :]
                    nc.vector.tensor_reduce(MXs[:, 0:64], S.rearrange("p s n -> p n s"), AX.X, ALU.max).then_inc(*step("dve", "s_max", br))
                    v.wait_ge(*so_far("dve"))
                    v.wait_ge(*at("s_maxt_ps", br))
                    nc.vector.tensor_reduce(MXT[0:64, :], PS[0:64, 0, 0:128], AX.X, ALU.max).then_inc(*step("dve"))
                    v.wait_ge(*so_far("dve"))
                    nc.vector.tensor_scalar(DGm[0:64, 0:64], id128[0:64, 0:64], MXT[0:64, :], None, ALU.mult).then_inc(*step("dve", "s_maxd", br))
                    v.wait_ge(*so_far("dve"))
                    v.wait_ge(*at("s_maxb_ps", br))
                    nc.vector.tensor_tensor(S, S, PS[:, 1, 0:64].unsqueeze(1).broadcast_to([128, n, 64]), ALU.subtract).then_inc(*step("dve", "s_sub", br))
                    v.wait_ge(*so_far("dve"))
                    v.wait_ge(*at("s_exp", br))
                    nc.vector.tensor_reduce(SMs[:, 0:64], S.rearrange("p s n -> p n s"), AX.X, ALU.add).then_inc(*step("dve", "s_sum", br))
                    v.wait_ge(*so_far("dve"))
                    v.wait_ge(*at("s_sum_ps", br))
                    nc.vector.reciprocal(SMs[:, 64:128], PS[:, 2, 0:64]).then_inc(*step("dve"))
                    v.wait_ge(*so_far("dve"))
                    if br == "cmp":
                        nc.vector.tensor_tensor(MXs[:, 64:128], SC_[:, 22, :], SMs[:, 64:128], ALU.mult).then_inc(*step("dve"))
                        v.wait_ge(*so_far("dve"))
                        nc.vector.tensor_reduce(PGRP, MXs[:, 64:128].rearrange("p (g j) -> p g j", j=4), AX.X, ALU.add).then_inc(*step("dve", "pgrp"))
                        v.wait_ge(*so_far("dve"))
                    nc.vector.tensor_tensor(SMs[:, 64:128], SMs[:, 64:128], GBs[:, gate * 64:(gate + 1) * 64], ALU.mult).then_inc(*step("dve"))
                    v.wait_ge(*so_far("dve"))
                    nc.vector.tensor_tensor(S, S, SMs[:, 64:128].unsqueeze(1).broadcast_to([128, n, 64]), ALU.mult).then_inc(*step("dve", "s_p"))
                    v.wait_ge(*so_far("dve"))

                softmax("cmp", 0)
                r = slice(0, 16)
                v.wait_ge(*at("rank_ps"))
                nc.vector.tensor_copy(RANK[r, :], PS[r, 3, 0:NBLK]).then_inc(*step("dve"))
                v.wait_ge(*so_far("dve"))
                nc.vector.memset(RANK[r, 0:1], 1e9).then_inc(*step("dve"))
                v.wait_ge(*so_far("dve"))
                nc.vector.memset(RANK[r, NBLK - 2:NBLK], 1e9).then_inc(*step("dve"))
                v.wait_ge(*so_far("dve"))
                for _ in range(2):
                    nc.vector.max(TOP8[r, :], RANK[r, :]).then_inc(*step("dve"))
                    v.wait_ge(*so_far("dve"))
                    nc.vector.match_replace(RSEL[r, :], TOP8[r, :], RANK[r, :], -3e38).then_inc(*step("dve"))
                    v.wait_ge(*so_far("dve"))
                    nc.vector.tensor_copy(RANK[r, :], RSEL[r, :]).then_inc(*step("dve"))
                    v.wait_ge(*so_far("dve"))
                nc.vector.tensor_scalar(RSEL[r, :], RANK[r, :], -1e37, NEG, ALU.is_gt, ALU.mult).then_inc(*step("dve", "rsel"))
                v.wait_ge(*so_far("dve"))
                v.wait_ge(*at("addt_ps"))
                nc.vector.tensor_copy(ADDT[0:32, :], PS[0:32, 4, 0:16]).then_inc(*step("dve", "addt"))
                v.wait_ge(*so_far("dve"))
                v.wait_ge(*at("add_ps"))
                nc.vector.tensor_copy(ADD, PS[:, 3, 0:256].rearrange("p (g n) -> p g n", g=NPAGE)).then_inc(*step("dve"))
                v.wait_ge(*so_far("dve"))
                S4 = SC_[:, 0:16, :].rearrange("p s (g j) -> p s g j", j=4)
                for j in range(4):
                    nc.vector.tensor_tensor(S4[:, :, :, j], S4[:, :, :, j], ADD, ALU.add).then_inc(*step("dve"))
                v.wait_ge(*so_far("dve"))
                softmax("sel", 1)
                softmax("win", 2)
                v.wait_ge(*at("s_pv", NS - 1))
                nc.vector.tensor_copy(v3(OH[0:8, :], 2), PS[0:8, 6:8, :]).then_inc(*step("dve", "s_o"))
                v.wait_ge(*at("s_o_ps"))
                O = PS[:, 5, 0:64].rearrange("p (b h) -> p b h", b=NS)
                for g in range(2):
                    q = slice(64 * g, 64 * g + 64)
                    nc.vector.tensor_copy(YA[q, :, T:TOK], O[q, :, 4 * g:4 * g + 4].rearrange("p b j -> p j b")).then_inc(*step("dve", "ya"))

            def pool(p):
                p.dma_start(BSEL[0:32].rearrange("p g n -> p (g n)"), io["blocksel"]).then_inc(*moved("blocksel"))
                p.wait_ge(*at("qd"))
                for b in range(NS):
                    if b >= 1:
                        key_pages(p, b, 1)
                    if b >= 2:
                        p.wait_ge(*at("s_sc_ps", b - 2))
                    p.dma_start(WIN[b % 2], io["win"][:, b, 0, :]).then_inc(*moved("win", b, lane=b % 2))
                for b in range(NS):
                    value_pages(p, b, 1)

        a = 0
        a = KT * TOK
        SG = [take(TOK) for _ in range(2)]
        PR = [take(TOK) for _ in range(2)]
        X2r = take(KT * TOK)
        X2 = tiles(X2r, KT)
        SQ2 = take(KT * TOK)
        assert a < TOP - 4680

        class Merge:
            def pe(pe):
                for m in range(8):
                    g = start["merge"] + 2 * m
                    if m >= 2:
                        pe.wait_ge(*at("gate_sig", m - 2))
                    if m:
                        product(pe, g, m % 2, XN)
                    if m >= 2:
                        pe.wait_ge(*at("gated", m - 2))
                    product(pe, g + 1, 2 + m % 2, YA, kts=4)
                for m in range(8):
                    if m == 0:
                        pe.wait_ge(*at("merged"))
                    if m >= 4:
                        pe.wait_ge(*at("x2", m - 4))
                    product(pe, start["out"] + m, m % 4, MG)
                pe.wait_ge(*so_far("pe"))

            def act(act):
                for m in range(8):
                    act.wait_ge(*at("tile", start["merge"] + 2 * m))
                    if m >= 2:
                        act.wait_ge(*at("gated", m - 2))
                    nc.scalar.activation(halves(SG[m % 2]), pair(m % 2), ACT.Sigmoid).then_inc(*step("act", "gate_sig", m))
                squares_act(act, "norm2", X2, SQ2t, range(KT), "x2")

            def dve(v):
                for m in range(8):
                    v.wait_ge(*at("gate_sig", m))
                    v.wait_ge(*at("tile", start["merge"] + 2 * m + 1))
                    nc.vector.tensor_tensor(halves(PR[m % 2]), pair(2 + m % 2), halves(SG[m % 2]), ALU.mult).then_inc(*step("dve", "gated", m))
                    v.wait_ge(*so_far("dve"))
                    nc.vector.tensor_tensor(MG[:, m, :], MG[:, m, :], PR[m % 2], ALU.add).then_inc(*step("dve", "merged"))
                v.wait_ge(*so_far("dve"))
                v.wait_ge(*at("x_again"))
                for m in range(8):
                    v.wait_ge(*at("tile", start["out"] + m))
                    nc.vector.tensor_tensor(halves(X2[:, m, :]), pair(m % 4), halves(X2[:, m, :]), ALU.add).then_inc(*step("dve", "x2", m))
                    if m:
                        add_square(v, "norm2", SQ2t, m - 1)
                add_square(v, "norm2", SQ2t, KT - 1)

            def pool(p):
                p.dma_start(X2r, io["x"]).then_inc(*moved("x_again"))

        SQ2t = tiles(SQ2, KT)
        a = 2 * KT * TOK + 4 * TOK + KT * TOK
        Hr = take(FT * TOK)
        H = tiles(Hr, FT)
        SGF = [region(0, TOK), region(TOK, TOK)]

        class Ffn:
            def pe(pe):
                norm_pe(pe, "norm2", SQ2t)
                first_product(pe, start["up"], 0, "norm2")
                for i in range(FT):
                    g = start["up"] + 2 * i
                    if i >= 2:
                        pe.wait_ge(*at("up_sig", i - 2))
                        pe.wait_ge(*at("h", i - 2))
                    if i:
                        product(pe, g, i % 2, XN)
                    product(pe, g + 1, 2 + i % 2, XN)
                pe.wait_ge(*at("h", FT - 1))
                for m in range(8):
                    g = start["down"] + 3 * m
                    if m >= 4:
                        pe.wait_ge(*at("x3", m - 4))
                    for i, (k0, k1) in enumerate(((0, 8), (8, 16), (16, 22))):
                        product(pe, g + i, m % 4, H, first=i == 0, last=i == 2, kts=k1 - k0, k0=k0)
                pe.wait_ge(*at("x3", 7))
                norm_pe(pe, "normf", SQ2t)
                pe.wait_ge(*so_far("pe"))

            def act(act):
                root_act(act, "norm2")
                for i in range(FT):
                    act.wait_ge(*at("tile", start["up"] + 2 * i))
                    if i >= 2:
                        act.wait_ge(*at("h", i - 2))
                    nc.scalar.activation(halves(SGF[i % 2]), pair(i % 2), ACT.Sigmoid).then_inc(*step("act", "up_sig", i))
                squares_act(act, "normf", X2, SQ2t, range(KT), "x3")
                root_act(act, "normf")

            def dve(v):
                norm_dve(v, "norm2", X2, XN, "g2")
                for i in range(FT):
                    v.wait_ge(*at("up_sig", i))
                    nc.vector.tensor_tensor(halves(H[:, i, :]), pair(i % 2), halves(SGF[i % 2]), ALU.mult).then_inc(*step("dve"))
                    v.wait_ge(*so_far("dve"))
                    v.wait_ge(*at("tile", start["up"] + 2 * i + 1))
                    nc.vector.tensor_tensor(halves(H[:, i, :]), pair(2 + i % 2), halves(H[:, i, :]), ALU.mult).then_inc(*step("dve", "h", i))
                for m in range(8):
                    v.wait_ge(*at("tile", start["down"] + 3 * m + 2))
                    nc.vector.tensor_tensor(halves(X2[:, m, :]), pair(m % 4), halves(X2[:, m, :]), ALU.add).then_inc(*step("dve", "x3", m))
                    if m:
                        add_square(v, "normf", SQ2t, m - 1)
                v.wait_ge(*so_far("dve"))
                add_square(v, "normf", SQ2t, KT - 1)
                norm_dve(v, "normf", X2, XN, "gf")

            def pool(p):
                for k in range(0, KT, 2):
                    p.wait_ge(*at("normf", "out", k + 1))
                    o = slice(k * TOK, (k + 2) * TOK)
                    p.dma_start(io["o_y"][:, o], xn[:, o]).then_inc(*moved("y_out"))
                p.wait_ge(*at("y_out"))

        table = {"norm1": Norm1, "rwkv": Rwkv, "mlstm": Mlstm, "attn": Attn, "sample": Sample, "merge": Merge, "ffn": Ffn}
        order = [table[n] for n in phases]

        block = ctx.enter_context(nc.Block())

        def run(eng, name, programs):
            for i, program in enumerate(programs):
                program(eng)
                meet(eng, name, i)

        @block.sync
        def _(sp):
            def sample_pages():
                sp.wait_ge(sem("phase_left"), 3 * 4)
                sp.dma_start(tab[0:1, :], io["table"]).then_inc(*moved("table"))
                sp.wait_ge(*at("table"))
                for b in range(NS):
                    key_pages(sp, b, 0)
                    if b == 0:
                        for g in range(start["early"], start["merge"]):
                            weights_in(g)
                        sp.wait_ge(sem("phase_left"), 4 * 4)
                for g in range(start["merge"], start["merge"] + RING):
                    weights_in(g)
                for b in range(NS):
                    value_pages(sp, b, 0)
                    if b == 0:
                        sp.wait_ge(*at("qd"))
                        sp.wait_ge(*at("s_kvc_ps", NS - 1))
                    sp.dma_start(VPw[b], io["win_v"][:, b]).then_inc(*moved("windows_v", b, lane=b % NV))

            def weights_in(g):
                if g >= RING:
                    sp.wait_ge(sem("tile_done"), g - RING + 1)
                n = PIECES[g] * 128
                sp.dma_start(ring[:, g % RING * 1024:g % RING * 1024 + n], io["w"][g, :, 0:n]).then_inc(
                    *moved("weights", g, lane=g % RING))

            sp.wait_ge(*at("x"))
            for g in range(start["early"]):
                weights_in(g)
            sample_pages()
            for g in range(start["merge"] + RING, len(PIECES)):
                weights_in(g)

        @block.tensor
        def _(eng):
            run(eng, "pe", [phase.pe for phase in order])

        @block.scalar
        def _(eng):
            run(eng, "act", [phase.act for phase in order])

        @block.vector
        def _(eng):
            run(eng, "dve", [phase.dve for phase in order])

        @block.gpsimd
        def _(eng):
            run(eng, "pool", [phase.pool for phase in order])

        return counts.found


OUTS = {"o_y": (128, KT * TOK), "o_kv": (128, 6 * TOK), "o_winp": (NS, 2, 128, 511),
        "o_conv": (128, 8 * 3 * (1 + NS)), "o_pC": (128, MH * 128), "o_pn": (128, MH), "o_pm": (4, 1),
        "o_sC": (128, NS * MH * 128), "o_sn": (128, MH * NS), "o_sm": (4, NS),
        "o_shift": (128, 14 * (1 + NS)), "o_pS": (128, 256), "o_sS": (128, 2048)}


def pack(i):
    f = np.float32
    A = {k: np.asarray(v) for k, v in i.items()}

    def per_feature(v):
        v = v.reshape(-1, v.shape[-1] // 128, 128)
        return v.transpose(2, 1, 0).reshape(128, -1)

    w_in = A["w_in"][0]
    sizes = (1024, 512, 512, 8, 512, 768, 24, 1792, 3072)
    at = np.concatenate([[0], np.cumsum(sizes)])
    m_qk, m_v, m_o, m_if, a_q, a_kv, a_g, r_c, mer = (w_in[:, at[n]:at[n + 1]] for n in range(9))
    small = np.zeros((D, 128), f)
    small[:, 0:24], small[:, 32:36], small[:, 64:68] = a_g, m_if[:, 0:4], m_if[:, 4:8]
    q = a_q.reshape(D, 2, 4, 64).transpose(0, 2, 1, 3).reshape(D, 512)
    tiles = []

    def add(w):
        k, n = w.shape[0] // 128, w.shape[1] // 128
        t = np.zeros((n, 128, 8, 128), f)
        t[:, :, 0:k] = w.reshape(k, 128, n, 128).transpose(2, 1, 0, 3)
        tiles.append(t)

    for w in (r_c, m_o, m_qk, small, m_v, q, a_kv):
        add(w)
    wa = A["w_branch_a"][0].reshape(2, 4, 64, D).transpose(1, 0, 2, 3).reshape(512, D)
    branch = (A["w_branch_m"][0], wa, A["w_branch_r"][0])
    for m, b in [(m, b) for m in range(8) for b in (0, 2)] + [(m, 1) for m in range(8)]:
            add(mer[:, b * D + m * 128:b * D + m * 128 + 128])
            add(branch[b][:, m * 128:m * 128 + 128])
    add(A["w_out"][0])
    gu = A["w_gate_up"][0]
    for m in range(FT):
        add(gu[:, m * 128:m * 128 + 128])
        add(gu[:, FF + m * 128:FF + m * 128 + 128])
    for m in range(8):
        wd = A["w_down"][0][:, m * 128:m * 128 + 128]
        for a, b in ((0, 8), (8, 16), (16, 22)):
            add(wd[a * 128:b * 128])
    out = {"w": np.concatenate(tiles).reshape(-1, 128, 1024)}
    x = np.concatenate([A["x_prompt"].reshape(T, D), A["x_sample"].reshape(NS, D)])
    out["x"] = per_feature(x)
    out["cn"] = constants()[0]
    out["blocksel"] = block_selector()
    out["prm"] = np.concatenate([per_feature(v) for v in (
        A["norm1_g"], A["norm2_g"], A["final_norm_g"][None], A["rwkv_mu"], A["rwkv_w0"], A["rwkv_a0"], A["rwkv_k_k"],
        A["rwkv_k_a"], A["rwkv_r_k"].reshape(1, 512), A["rwkv_ln_g"], A["rwkv_ln_b"], A["mlstm_conv_w"][0],
        A["mlstm_conv_b"])], 1)
    lora = np.zeros((128, 1024), f)
    lora[0:64, 0:512], lora[64:128, 0:512], lora[:, 512:] = A["rwkv_w2"][0], A["rwkv_a2"][0], A["rwkv_g2"][0]
    out["lora"] = lora
    out["rwkv_shift"] = per_feature(A["state_rwkv_shift"].reshape(NS, 1792))
    s = A["state_rwkv"][0].reshape(NS, 4, 2, 64, 64)
    out["rwkv_state"] = s.transpose(2, 4, 0, 1, 3).reshape(128, 2048)
    cv = A["state_mlstm_conv"][0]
    out["conv"] = cv.reshape(NS, 3, 8, 128).transpose(3, 2, 0, 1).reshape(128, 192)
    out["mC"] = A["state_mlstm_C"][0].transpose(2, 1, 0, 3).reshape(128, NS * MH * 128)
    out["mn"] = A["state_mlstm_n"][0].transpose(2, 1, 0).reshape(128, NS * MH)
    out["mm"] = A["state_mlstm_m"][0].T
    out["ifb"] = A["mlstm_if_bias"][0].T
    def chunked(c):
        c = c[0].reshape(-1, 8, 8, 2, 2, 64)
        return c.transpose(0, 3, 5, 2, 4, 1).reshape(-1, 128, 128)

    keys = A["cache_slc_k"][0].reshape(-1, 128, 128).transpose(0, 2, 1)
    vals = A["cache_slc_v"][0].reshape(-1, 128, 128)
    out["pages"] = np.stack([chunked(A["cache_cmp_k"]), chunked(A["cache_cmp_v"]), keys], 2)
    out["pages_v"] = vals
    out["win"] = np.stack([A["cache_win_k"][0].reshape(NS, 512, 128).transpose(2, 0, 1),
                           A["cache_win_v"][0].reshape(NS, 512, 128).transpose(2, 0, 1)], 2)
    out["win_v"] = A["cache_win_v"][0].reshape(NS, 4, 128, 128).transpose(2, 0, 1, 3)
    out["table"] = A["page_table"].reshape(1, 128)
    w1 = A["nsa_cmp_w1"][0].reshape(2, 2, 8, 2, 64, 64)
    out["w1"] = w1.transpose(3, 4, 0, 2, 1, 5).reshape(128, 2 * 2 * 8 * 64)
    w1 = A["nsa_cmp_w1"][0].reshape(2, 2, 16, 64, 64).transpose(3, 0, 1, 2, 4).reshape(64, 4096)
    out["w1d"] = np.concatenate([w1, w1])
    pe = A["nsa_cmp_pe"][0].reshape(2, 2, 8, 2, 64)
    out["pe"] = pe.transpose(3, 4, 0, 1, 2).reshape(128, 32)
    w2 = A["nsa_cmp_w2"][0].transpose(1, 0, 2).reshape(64, 128)
    out["w2"] = np.concatenate([w2, w2])
    return {k: np.ascontiguousarray(v) for k, v in out.items()}


PHASES = ("norm1", "rwkv", "mlstm", "attn", "sample", "merge", "ffn")


def kernel(**inputs):
    import numpy as _np
    import concourse.bacc as _bacc
    from concourse import mybir as _mybir
    from concourse.bass_utils import run_bass_kernel_spmd as _run

    packed = pack(inputs)
    known = None
    for _ in range(2):
        nc = _bacc.Bacc("TRN2", target_bir_lowering=False, num_devices=1)
        arrays, io = {}, {}
        for name, a in packed.items():
            arrays["in_" + name] = a
            io[name] = nc.dram_tensor("in_" + name, a.shape, _mybir.dt.from_np(a.dtype), kind="ExternalInput").ap()
        for name, shape in OUTS.items():
            io[name] = nc.dram_tensor(name, shape, F32, kind="ExternalOutput").ap()
        known = build(nc, io, known, PHASES)
    o = _run(nc, [arrays], core_ids=[0]).results[0]

    y = o["o_y"].reshape(128, KT, TOK).transpose(2, 1, 0).reshape(TOK, D)
    kv = o["o_kv"].reshape(128, 6, TOK).transpose(1, 2, 0).reshape(6, TOK, 2, 64)
    kvp, kvs = kv[:, :T][:, None, None], kv[:, T:][:, None, :, None]
    winp = np.concatenate([o["o_winp"].transpose(1, 0, 3, 2).reshape(2, 1, NS, 511, 2, 64),
                           kv[4:6, T:].reshape(2, 1, NS, 1, 2, 64)], 3)
    conv = o["o_conv"].reshape(128, 8, 1 + NS, 3).transpose(2, 3, 1, 0).reshape(1 + NS, 3, 1024)
    shift = o["o_shift"].reshape(128, 14, 1 + NS).transpose(2, 1, 0).reshape(1 + NS, 1792)
    pS = o["o_pS"].reshape(2, 64, 4, 64).transpose(2, 0, 3, 1).reshape(1, 1, 8, 64, 64)
    sS = o["o_sS"].reshape(2, 64, NS, 4, 64).transpose(2, 3, 0, 4, 1).reshape(1, NS, 8, 64, 64)
    pC = o["o_pC"].reshape(128, MH, 128).transpose(1, 0, 2)[None, None]
    sC = o["o_sC"].reshape(128, MH, NS, 128).transpose(2, 1, 0, 3)[None]
    sn = o["o_sn"].reshape(128, MH, NS).transpose(2, 1, 0)[None]
    out = (y[None, :T], y[T:, None],
           kvp[0], kvp[1], kvp[2], kvp[3], kvp[4], kvp[5],
           conv[None, 0:1], pC, o["o_pn"].T[None, None], o["o_pm"].reshape(1, 1, 4), shift[0].reshape(1, 1, 1, 1792), pS,
           kvs[0], kvs[1], kvs[2], kvs[3], winp[0], winp[1],
           conv[None, 1:], sC, sn, o["o_sm"].T[None], shift[1:].reshape(1, NS, 1, 1792), sS)
    return tuple(_np.ascontiguousarray(v) for v in out)
```
